# Optimizing a Trainium2 kernel written in Bass

```python
import math
import jax, jax.numpy as jnp
from jax import lax
import numpy as np

D_MODEL = 1024
BATCH = 1
SEQ = 256
DEPTH = 2

CHUNK = 64
Q_BLOCK = 128
HEAD_DIM = 64
A_HEADS = 4
B_HEADS = 8
C_HEADS = 8
IDX_HEADS = 4
IDX_DIM = 64
TOPK_MAX = 256
N_BRANCHES = 3
D_FF = 4 * D_MODEL
PLE_DIM = 256
ROPE_THETA = 10000.0
EPS = 1e-6

A_QK = A_HEADS * 2 * HEAD_DIM
A_V = A_HEADS * 2 * HEAD_DIM
A_WIDTH = A_V
B_WIDTH = B_HEADS * HEAD_DIM
C_WIDTH = C_HEADS * HEAD_DIM
IN_SPLITS = (A_QK, A_QK, A_V, B_WIDTH, B_WIDTH, B_WIDTH, C_WIDTH, C_WIDTH, C_WIDTH,
             IDX_HEADS * IDX_DIM, IDX_DIM, IDX_HEADS, N_BRANCHES * D_MODEL)
W_IN_COLS = (2 * A_QK + A_V + 3 * B_WIDTH + 3 * C_WIDTH + IDX_HEADS * IDX_DIM + IDX_DIM
             + IDX_HEADS + N_BRANCHES * D_MODEL)


def rmsnorm(x, g):
    xf = x.astype(jnp.float32)
    y = xf * lax.rsqrt(jnp.mean(xf * xf, axis=-1, keepdims=True) + EPS)
    return (y * g.astype(jnp.float32)).astype(x.dtype)

def rope_tables(positions, dim):
    inv = ROPE_THETA ** (-jnp.arange(0, dim, 2, dtype=jnp.float32) / dim)
    ang = positions.astype(jnp.float32)[..., None] * inv
    return jnp.cos(ang), jnp.sin(ang)

def apply_rope(x, cos, sin):
    c = cos[:, :, None, :]
    s = sin[:, :, None, :]
    xf = x.astype(jnp.float32)
    x1, x2 = jnp.split(xf, 2, axis=-1)
    return jnp.concatenate([x1 * c - x2 * s, x2 * c + x1 * s], axis=-1).astype(x.dtype)

def sweep_query_blocks(fn, *arrays):
    b, s = arrays[0].shape[:2]
    nb = s // Q_BLOCK
    blocks = tuple(jnp.moveaxis(a.reshape((b, nb, Q_BLOCK) + a.shape[2:]), 1, 0) for a in arrays)
    out = lax.map(lambda args: fn(args[0], *args[1:]), (jnp.arange(nb), *blocks))
    return jnp.moveaxis(out, 0, 1).reshape((b, s) + out.shape[3:])

def block_positions(blk, n_keys):
    q_pos = blk * Q_BLOCK + jnp.arange(Q_BLOCK)
    k_pos = jnp.arange(n_keys)
    chunk_ok = (k_pos[None, :] // CHUNK) <= (q_pos[:, None] // CHUNK)
    return q_pos, k_pos, chunk_ok

def diff_attention(q, k, v, lam, lam_init, subln_g):
    n_keys = k.shape[1]
    scale = HEAD_DIM ** -0.5

    def block(blk, qb):
        _, _, chunk_ok = block_positions(blk, n_keys)
        s = jnp.einsum('bqhcd,bkhcd->bhcqk', qb, k).astype(jnp.float32) * scale
        s = jnp.where(chunk_ok, s, -jnp.inf)
        pr = jax.nn.softmax(s, axis=-1)
        attn = (pr[:, :, 0] - lam * pr[:, :, 1]).astype(v.dtype)
        return jnp.einsum('bhqk,bkhe->bqhe', attn, v)

    o = sweep_query_blocks(block, q)
    return rmsnorm(o, subln_g) * (1.0 - lam_init)

def stick_breaking_attention(q, k, v):
    n_keys = k.shape[1]
    scale = HEAD_DIM ** -0.5

    def block(blk, qb):
        q_pos, k_pos, _ = block_positions(blk, n_keys)
        strict = k_pos[None, :] < q_pos[:, None]
        z = jnp.einsum('bqhd,bkhd->bhqk', qb, k).astype(jnp.float32) * scale
        log_beta = jax.nn.log_sigmoid(z)
        log_one_minus = jnp.where(strict, jax.nn.log_sigmoid(-z), 0.0)
        key_axis = log_one_minus.ndim - 1
        later = lax.cumsum(log_one_minus, axis=key_axis, reverse=True) - log_one_minus
        a = jnp.where(strict, jnp.exp(log_beta + later), 0.0).astype(v.dtype)
        return jnp.einsum('bhqk,bkhd->bqhd', a, v)

    return sweep_query_blocks(block, q)

def dsa_attention(q, k, v, qi, ki, wi):
    n_keys = k.shape[1]
    topk = min(TOPK_MAX, n_keys // 4)
    scale = HEAD_DIM ** -0.5

    def block(blk, qb, qib, wib):
        q_pos, _, chunk_ok = block_positions(blk, n_keys)
        idx_s = jnp.einsum('bqhd,bkd->bqhk', qib, ki).astype(jnp.float32) * (IDX_DIM ** -0.5)
        score = jnp.einsum('bqh,bqhk->bqk', wib.astype(jnp.float32) * (IDX_HEADS ** -0.5),
                           jax.nn.relu(idx_s))
        score = jnp.where(chunk_ok, score, -jnp.inf)
        _, sel = lax.top_k(score, topk)
        ok = (sel // CHUNK) <= (q_pos[None, :, None] // CHUNK)
        kg = jax.vmap(lambda kb, ib: kb[ib])(k, sel)
        vg = jax.vmap(lambda vb, ib: vb[ib])(v, sel)
        s = jnp.einsum('bqhd,bqkhd->bhqk', qb, kg).astype(jnp.float32) * scale
        s = jnp.where(ok[:, None], s, -jnp.inf)
        pr = jax.nn.softmax(s, axis=-1).astype(v.dtype)
        return jnp.einsum('bhqk,bqkhd->bqhd', pr, vg)

    return sweep_query_blocks(block, q, qi, wi)

def first_inputs(seed: int = 0) -> dict:
    key = jax.random.key(seed)
    ks = iter(jax.random.split(key, 32))

    def dense(shape, fan_in):
        return jax.random.normal(next(ks), shape, jnp.float32) * (fan_in ** -0.5)

    def gain(shape):
        return 1.0 + 0.05 * jax.random.normal(next(ks), shape, jnp.float32)

    x = jax.random.normal(next(ks), (BATCH, SEQ, D_MODEL), jnp.float32)
    p = jax.random.normal(next(ks), (DEPTH, BATCH, SEQ, PLE_DIM), jnp.float32)
    offset = jax.random.randint(next(ks), (BATCH, 1), 0, 16, dtype=jnp.int32) * CHUNK
    positions = (offset + jnp.arange(SEQ, dtype=jnp.int32)[None, :]).astype(jnp.int32)
    return {
        "x": x,
        "p": p,
        "positions": positions,
        "attn_norm": gain((DEPTH, D_MODEL)),
        "w_in": dense((DEPTH, D_MODEL, W_IN_COLS), D_MODEL),
        "a_q_norm": gain((DEPTH, HEAD_DIM)),
        "a_k_norm": gain((DEPTH, HEAD_DIM)),
        "a_lambda": 0.1 * jax.random.normal(next(ks), (DEPTH, 4, HEAD_DIM), jnp.float32),
        "a_subln": gain((DEPTH, 2 * HEAD_DIM)),
        "c_q_norm": gain((DEPTH, HEAD_DIM)),
        "c_k_norm": gain((DEPTH, HEAD_DIM)),
        "idx_k_norm": gain((DEPTH, IDX_DIM)),
        "w_br_a": dense((DEPTH, A_WIDTH, D_MODEL), A_WIDTH),
        "w_br_b": dense((DEPTH, B_WIDTH, D_MODEL), B_WIDTH),
        "w_br_c": dense((DEPTH, C_WIDTH, D_MODEL), C_WIDTH),
        "w_out": dense((DEPTH, D_MODEL, D_MODEL), D_MODEL),
        "mlp_norm": gain((DEPTH, D_MODEL)),
        "w_up": dense((DEPTH, D_MODEL, D_FF), D_MODEL),
        "w_down": dense((DEPTH, D_FF, D_MODEL), D_FF),
        "ple_norm": gain((DEPTH, D_MODEL)),
        "w_ple_gate": dense((DEPTH, D_MODEL, D_MODEL), D_MODEL),
        "w_ple_proj": dense((DEPTH, PLE_DIM, D_MODEL), PLE_DIM),
    }

def first_block(x, p, positions, attn_norm, w_in, a_q_norm, a_k_norm, a_lambda, a_subln,
              c_q_norm, c_k_norm, idx_k_norm, w_br_a, w_br_b, w_br_c, w_out,
              mlp_norm, w_up, w_down, ple_norm, w_ple_gate, w_ple_proj):
    b, s = x.shape[:2]
    cos, sin = rope_tables(positions, HEAD_DIM)
    offsets = [int(o) for o in np.cumsum(IN_SPLITS)[:-1]]
    for i in range(DEPTH):
        lam_init = 0.8 - 0.6 * math.exp(-0.3 * i)
        h = rmsnorm(x, attn_norm[i])
        proj = h @ w_in[i]
        (aq, ak, av, bq, bk, bv, cq, ck, cv, iq, ik, iw, gl) = jnp.split(proj, offsets, axis=-1)

        aq = apply_rope(rmsnorm(aq.reshape(b, s, 2 * A_HEADS, HEAD_DIM), a_q_norm[i]), cos, sin)
        ak = apply_rope(rmsnorm(ak.reshape(b, s, 2 * A_HEADS, HEAD_DIM), a_k_norm[i]), cos, sin)
        lp = a_lambda[i].astype(jnp.float32)
        lam = jnp.exp(jnp.sum(lp[0] * lp[1])) - jnp.exp(jnp.sum(lp[2] * lp[3])) + lam_init
        y_a = diff_attention(aq.reshape(b, s, A_HEADS, 2, HEAD_DIM),
                             ak.reshape(b, s, A_HEADS, 2, HEAD_DIM),
                             av.reshape(b, s, A_HEADS, 2 * HEAD_DIM),
                             lam, lam_init, a_subln[i]).reshape(b, s, A_WIDTH)

        y_b = stick_breaking_attention(bq.reshape(b, s, B_HEADS, HEAD_DIM),
                                       bk.reshape(b, s, B_HEADS, HEAD_DIM),
                                       bv.reshape(b, s, B_HEADS, HEAD_DIM)).reshape(b, s, B_WIDTH)

        cq = apply_rope(rmsnorm(cq.reshape(b, s, C_HEADS, HEAD_DIM), c_q_norm[i]), cos, sin)
        ck = apply_rope(rmsnorm(ck.reshape(b, s, C_HEADS, HEAD_DIM), c_k_norm[i]), cos, sin)
        iq = apply_rope(iq.reshape(b, s, IDX_HEADS, IDX_DIM), cos, sin)
        ik = apply_rope(rmsnorm(ik, idx_k_norm[i])[:, :, None, :], cos, sin)[:, :, 0]
        y_c = dsa_attention(cq, ck, cv.reshape(b, s, C_HEADS, HEAD_DIM),
                            iq, ik, iw).reshape(b, s, C_WIDTH)

        gates = jax.nn.sigmoid(gl.reshape(b, s, N_BRANCHES, D_MODEL).astype(jnp.float32)).astype(x.dtype)
        merged = (gates[:, :, 0] * (y_a @ w_br_a[i])
                  + gates[:, :, 1] * (y_b @ w_br_b[i])
                  + gates[:, :, 2] * (y_c @ w_br_c[i]))
        x = x + merged @ w_out[i]

        hm = rmsnorm(x, mlp_norm[i])
        x = x + jnp.square(jax.nn.relu(hm @ w_up[i])) @ w_down[i]

        hp = rmsnorm(x, ple_norm[i])
        x = x + jax.nn.sigmoid(hp @ w_ple_gate[i]) * (p[i] @ w_ple_proj[i])
    return x


RET_HEADS = 4
RET_DK = 128
RET_DV = 256
RET_QK = RET_HEADS * RET_DK
RET_V = RET_HEADS * RET_DV
ROPE_BASE = 10000.0
HG_HEADS = 8
HG_DK = 128
HG_DV = 128
HG_K = HG_HEADS * HG_DK
HG_V = HG_HEADS * HG_DV
HG_BLOCK = 16
SWA_HQ = 16
SWA_HKV = 4
SWA_HD = 64
SWA_Q = SWA_HQ * SWA_HD
SWA_KV = SWA_HKV * SWA_HD
SWA_WINDOW = 128
SWA_WIN_CHUNKS = SWA_WINDOW // CHUNK
D_FF_2 = 2816
N_EXPERTS = 8
TOP_K = 2
D_EXP = 3584
N_DENSE = (DEPTH + 1) // 2
N_MOE = DEPTH // 2
LN_EPS = 1e-5
RMS_EPS = 1e-6
DN_ALPHA = (2.0 * DEPTH) ** 0.25
DN_BETA = (8.0 * DEPTH) ** -0.25
IN_SPLITS_2 = (RET_QK, RET_QK, RET_V, RET_V,
             HG_K, HG_K, HG_V, HG_V,
             SWA_Q, SWA_KV, SWA_KV,
             D_MODEL, D_MODEL, D_MODEL)
N_IN = sum(IN_SPLITS_2)


def layer_norm(x, g, b):
    xf = x.astype(jnp.float32)
    mu = jnp.mean(xf, -1, keepdims=True)
    var = jnp.mean(jnp.square(xf - mu), -1, keepdims=True)
    return ((xf - mu) * lax.rsqrt(var + LN_EPS) * g + b).astype(x.dtype)

def rms_norm(x):
    xf = x.astype(jnp.float32)
    return xf * lax.rsqrt(jnp.mean(xf * xf, -1, keepdims=True) + RMS_EPS)

def rotary(x, pos):
    half = x.shape[-1] // 2
    inv = 1.0 / (ROPE_BASE ** jnp.linspace(0.0, 1.0, half, dtype=jnp.float32))
    ang = pos[:, None] * inv[None, :]
    cos = jnp.cos(ang)[None, :, None, :]
    sin = jnp.sin(ang)[None, :, None, :]
    x1, x2 = x[..., :half], x[..., half:]
    return jnp.concatenate([x1 * cos - x2 * sin, x1 * sin + x2 * cos], axis=-1)

def retention(q, k, v):
    B, S, H, DK = q.shape
    DV = v.shape[-1]
    n = S // CHUNK
    log_gamma = jnp.log(1.0 - 2.0 ** (-5.0 - jnp.arange(H, dtype=jnp.float32)))
    k = k * DK ** -0.5
    qc = q.reshape(B, n, CHUNK, H, DK)
    kc = k.reshape(B, n, CHUNK, H, DK)
    vc = v.reshape(B, n, CHUNK, H, DV)
    idx = jnp.arange(CHUNK, dtype=jnp.float32)
    diff = idx[:, None] - idx[None, :]
    decay = jnp.where(diff[None] >= 0,
                      jnp.exp(jnp.maximum(diff, 0.0)[None] * log_gamma[:, None, None]), 0.0)
    scores = jnp.einsum('bnthd,bnshd->bnhts', qc, kc) * decay
    o_intra = jnp.einsum('bnhts,bnshv->bnthv', scores, vc)
    k_decay = jnp.exp((CHUNK - 1.0 - idx)[:, None] * log_gamma[None, :])
    q_decay = jnp.exp((idx + 1.0)[:, None] * log_gamma[None, :])
    chunk_decay = jnp.exp(CHUNK * log_gamma)[None, :, None, None]

    def step(state, inp):
        q_n, k_n, v_n = inp
        o = jnp.einsum('bthd,th,bhdv->bthv', q_n, q_decay, state)
        state = chunk_decay * state + jnp.einsum('bshd,sh,bshv->bhdv', k_n, k_decay, v_n)
        return state, o

    init = jnp.zeros((B, H, DK, DV), jnp.float32)
    _, o_inter = lax.scan(step, init, (jnp.moveaxis(qc, 1, 0), jnp.moveaxis(kc, 1, 0),
                                       jnp.moveaxis(vc, 1, 0)))
    return (o_intra + jnp.moveaxis(o_inter, 0, 1)).reshape(B, S, H, DV)

def hgrn2_scan(q, log_f, k, v):
    B, S, H, DK = q.shape
    DV = v.shape[-1]
    n = S // HG_BLOCK
    L = HG_BLOCK
    qc = q.reshape(B, n, L, H, DK)
    kc = k.reshape(B, n, L, H, DK)
    vc = v.reshape(B, n, L, H, DV)
    bcum = jnp.cumsum(log_f.reshape(B, n, L, H, DK), axis=2)
    q_t = qc * jnp.exp(bcum)
    k_t = kc * jnp.exp(-bcum)
    causal = jnp.tril(jnp.ones((L, L), dtype=bool))
    a = jnp.where(causal, jnp.einsum('bnthd,bnshd->bnhts', q_t, k_t), 0.0)
    o_intra = jnp.einsum('bnhts,bnshv->bnthv', a, vc)
    b_last = bcum[:, :, -1]
    k_state = kc * jnp.exp(b_last[:, :, None] - bcum)
    blk_decay = jnp.exp(b_last)

    def step(state, inp):
        q_n, ks_n, v_n, d_n = inp
        o = jnp.einsum('bthd,bhdv->bthv', q_n, state)
        state = d_n[..., None] * state + jnp.einsum('bshd,bshv->bhdv', ks_n, v_n)
        return state, o

    init = jnp.zeros((B, H, DK, DV), jnp.float32)
    _, o_inter = lax.scan(step, init, (jnp.moveaxis(q_t, 1, 0), jnp.moveaxis(k_state, 1, 0),
                                       jnp.moveaxis(vc, 1, 0), jnp.moveaxis(blk_decay, 1, 0)))
    return (o_intra + jnp.moveaxis(o_inter, 0, 1)).reshape(B, S, H, DV)

def swa_with_sinks(q, k, v, sinks):
    B, S, HQ, HD = q.shape
    HKV = k.shape[2]
    G = HQ // HKV
    W = SWA_WIN_CHUNKS
    n = S // CHUNK
    qc = q.astype(jnp.float32).reshape(B, n, CHUNK, HKV, G, HD)
    kc = k.astype(jnp.float32).reshape(B, n, CHUNK, HKV, HD)
    vc = v.astype(jnp.float32).reshape(B, n, CHUNK, HKV, HD)
    padw = ((0, 0), (W, 0), (0, 0), (0, 0), (0, 0))
    kp = jnp.pad(kc, padw)
    vp = jnp.pad(vc, padw)
    kb = jnp.concatenate([kp[:, j:j + n] for j in range(W + 1)], axis=2)
    vb = jnp.concatenate([vp[:, j:j + n] for j in range(W + 1)], axis=2)
    chunk_ids = jnp.arange(n)[:, None] - W + jnp.arange(W + 1)[None, :]
    valid = jnp.repeat(chunk_ids >= 0, CHUNK, axis=1)
    s = jnp.einsum('bntkgd,bnskd->bnkgts', qc, kb) * HD ** -0.5
    s = jnp.where(valid[None, :, None, None, None, :], s, -jnp.inf)
    sink = sinks.astype(jnp.float32).reshape(HKV, G)[None, None, :, :, None, None]
    m = jnp.maximum(jnp.max(s, -1, keepdims=True), sink)
    p = jnp.exp(s - m)
    p = p / (jnp.sum(p, -1, keepdims=True) + jnp.exp(sink - m))
    o = jnp.einsum('bnkgts,bnskd->bntkgd', p, vb)
    return o.reshape(B, S, HQ * HD)

def swiglu(h, w_gate, w_up, w_down):
    return (jax.nn.silu(h @ w_gate) * (h @ w_up)) @ w_down

def moe_swiglu(h2, w_router, w_gate, w_up, w_down):
    logits = (h2 @ w_router).astype(jnp.float32)
    top_logits, top_idx = lax.top_k(logits, TOP_K)
    top_w = jax.nn.softmax(top_logits, axis=-1)
    flat_e = top_idx.reshape(-1)
    order = jnp.argsort(flat_e)
    tok = order // TOP_K
    xs = h2[tok]
    sizes = jnp.bincount(flat_e, length=N_EXPERTS).astype(jnp.int32)
    hid = jax.nn.silu(lax.ragged_dot(xs, w_gate, sizes)) * lax.ragged_dot(xs, w_up, sizes)
    y = lax.ragged_dot(hid, w_down, sizes)
    y = y * top_w.reshape(-1)[order][:, None].astype(y.dtype)
    return jnp.zeros_like(h2).at[tok].add(y.astype(h2.dtype))

def second_inputs(seed: int = 0) -> dict:
    key = jax.random.key(seed)
    ks = jax.random.split(key, 24)
    f32 = jnp.float32
    D = D_MODEL

    def nrm(k, shape, scale):
        return jax.random.normal(k, shape, f32) * scale

    return {
        'x': nrm(ks[0], (BATCH, SEQ, D), 1.0),
        'ln_in_g': 1.0 + nrm(ks[1], (D,), 0.02),
        'ln_in_b': nrm(ks[2], (D,), 0.02),
        'w_in': nrm(ks[3], (DEPTH, D, N_IN), D ** -0.5),
        'ret_w_out': nrm(ks[4], (DEPTH, RET_V, D), DN_BETA * RET_V ** -0.5),
        'hgrn_lower_bounds': 1.0 + nrm(ks[5], (DEPTH, HG_K), 0.5),
        'hgrn_norm_g': 1.0 + nrm(ks[6], (DEPTH, HG_DV), 0.02),
        'hgrn_w_out': nrm(ks[7], (DEPTH, HG_V, D), DN_BETA * HG_V ** -0.5),
        'swa_sinks': nrm(ks[8], (DEPTH, SWA_HQ), 0.5),
        'swa_w_out': nrm(ks[9], (DEPTH, SWA_Q, D), DN_BETA * SWA_Q ** -0.5),
        'w_o': nrm(ks[10], (DEPTH, D, D), DN_BETA * D ** -0.5),
        'ln_mix_g': 1.0 + nrm(ks[11], (DEPTH, D), 0.02),
        'ln_mix_b': nrm(ks[12], (DEPTH, D), 0.02),
        'ffn_w_gate': nrm(ks[13], (N_DENSE, D, D_FF_2), D ** -0.5),
        'ffn_w_up': nrm(ks[14], (N_DENSE, D, D_FF_2), D ** -0.5),
        'ffn_w_down': nrm(ks[15], (N_DENSE, D_FF_2, D), DN_BETA * D_FF_2 ** -0.5),
        'moe_router': nrm(ks[16], (N_MOE, D, N_EXPERTS), D ** -0.5),
        'moe_w_gate': nrm(ks[17], (N_MOE, N_EXPERTS, D, D_EXP), D ** -0.5),
        'moe_w_up': nrm(ks[18], (N_MOE, N_EXPERTS, D, D_EXP), D ** -0.5),
        'moe_w_down': nrm(ks[19], (N_MOE, N_EXPERTS, D_EXP, D), DN_BETA * D_EXP ** -0.5),
        'ln_ffn_g': 1.0 + nrm(ks[20], (DEPTH, D), 0.02),
        'ln_ffn_b': nrm(ks[21], (DEPTH, D), 0.02),
    }

def second_block(x, ln_in_g, ln_in_b, w_in, ret_w_out, hgrn_lower_bounds, hgrn_norm_g, hgrn_w_out,
              swa_sinks, swa_w_out, w_o, ln_mix_g, ln_mix_b, ffn_w_gate, ffn_w_up, ffn_w_down,
              moe_router, moe_w_gate, moe_w_up, moe_w_down, ln_ffn_g, ln_ffn_b):
    B, S, D = x.shape
    f32 = jnp.float32
    pos = jnp.arange(S, dtype=f32)
    split_points = np.cumsum(np.array(IN_SPLITS_2))[:-1].tolist()
    lb_all = jnp.cumsum(jax.nn.softmax(hgrn_lower_bounds.astype(f32), axis=0), axis=0)
    lb_all = lb_all - lb_all[0]

    h = layer_norm(x, ln_in_g, ln_in_b)
    for layer in range(DEPTH):
        proj = jnp.einsum('bsd,dc->bsc', h, w_in[layer])
        (rq, rk, rv, rg, hq, hf, hi, hg, sq, sk, sv, ga, gb, gc) = jnp.split(proj, split_points, axis=-1)

        r_q = rotary(rq.astype(f32).reshape(B, S, RET_HEADS, RET_DK), pos)
        r_k = rotary(rk.astype(f32).reshape(B, S, RET_HEADS, RET_DK), pos)
        r_v = rv.astype(f32).reshape(B, S, RET_HEADS, RET_DV)
        r_o = rms_norm(retention(r_q, r_k, r_v)).reshape(B, S, RET_V)
        y_a = (jax.nn.silu(rg.astype(f32)) * r_o) @ ret_w_out[layer]

        lb = lb_all[layer].reshape(HG_HEADS, HG_DK)
        z = hf.astype(f32).reshape(B, S, HG_HEADS, HG_DK)
        log_f = jnp.logaddexp(jnp.log(lb), jnp.log1p(-lb) + jax.nn.log_sigmoid(z))
        h_k = -jnp.expm1(log_f)
        h_q = hq.astype(f32).reshape(B, S, HG_HEADS, HG_DK)
        h_v = hi.astype(f32).reshape(B, S, HG_HEADS, HG_DV)
        h_o = rms_norm(hgrn2_scan(h_q, log_f, h_k, h_v)) * hgrn_norm_g[layer]
        y_b = (jax.nn.silu(hg.astype(f32)) * h_o.reshape(B, S, HG_V)) @ hgrn_w_out[layer]

        s_o = swa_with_sinks(sq.reshape(B, S, SWA_HQ, SWA_HD), sk.reshape(B, S, SWA_HKV, SWA_HD),
                             sv.reshape(B, S, SWA_HKV, SWA_HD), swa_sinks[layer])
        y_c = s_o @ swa_w_out[layer]

        merged = (jax.nn.sigmoid(ga.astype(f32)) * y_a + jax.nn.sigmoid(gb.astype(f32)) * y_b
                  + jax.nn.sigmoid(gc.astype(f32)) * y_c)
        mix = merged @ w_o[layer]
        h = layer_norm((DN_ALPHA * h + mix).astype(h.dtype), ln_mix_g[layer], ln_mix_b[layer])

        j = layer // 2
        if layer % 2 == 0:
            ff = swiglu(h, ffn_w_gate[j], ffn_w_up[j], ffn_w_down[j])
        else:
            ff = moe_swiglu(h.reshape(B * S, D), moe_router[j], moe_w_gate[j], moe_w_up[j],
                            moe_w_down[j]).reshape(B, S, D)
        h = layer_norm((DN_ALPHA * h + ff).astype(h.dtype), ln_ffn_g[layer], ln_ffn_b[layer])
    return h


def setup_inputs(seed=0):
    out = dict(first_inputs(seed))
    for name, value in second_inputs(seed + 1).items():
        if name != "x":
            out[name + "_2"] = value
    return out


def reference(
    x, p, positions, attn_norm, w_in, a_q_norm, a_k_norm, a_lambda, a_subln, c_q_norm, c_k_norm,
    idx_k_norm, w_br_a, w_br_b, w_br_c, w_out, mlp_norm, w_up, w_down, ple_norm, w_ple_gate,
    w_ple_proj, ln_in_g_2, ln_in_b_2, w_in_2, ret_w_out_2, hgrn_lower_bounds_2, hgrn_norm_g_2,
    hgrn_w_out_2, swa_sinks_2, swa_w_out_2, w_o_2, ln_mix_g_2, ln_mix_b_2, ffn_w_gate_2,
    ffn_w_up_2, ffn_w_down_2, moe_router_2, moe_w_gate_2, moe_w_up_2, moe_w_down_2, ln_ffn_g_2,
    ln_ffn_b_2,
):
    x = first_block(
        x, p, positions, attn_norm, w_in, a_q_norm, a_k_norm, a_lambda, a_subln, c_q_norm,
        c_k_norm, idx_k_norm, w_br_a, w_br_b, w_br_c, w_out, mlp_norm, w_up, w_down, ple_norm,
        w_ple_gate, w_ple_proj,
    )
    return second_block(
        x, ln_in_g_2, ln_in_b_2, w_in_2, ret_w_out_2, hgrn_lower_bounds_2, hgrn_norm_g_2,
        hgrn_w_out_2, swa_sinks_2, swa_w_out_2, w_o_2, ln_mix_g_2, ln_mix_b_2, ffn_w_gate_2,
        ffn_w_up_2, ffn_w_down_2, moe_router_2, moe_w_gate_2, moe_w_up_2, moe_w_down_2,
        ln_ffn_g_2, ln_ffn_b_2,
    )


_drawn_inputs = setup_inputs


def setup_inputs(seed=0):
    import zlib

    import numpy as np

    out = dict(_drawn_inputs(seed))
    spreads = {}
    factors = {'c_q_norm': 4.73,
     'c_k_norm': 4.968,
     'ple_norm': 4.416,
     'hgrn_norm_g_2': 24.697,
     'swa_sinks_2': 31.155}
    for name, (base, spread) in spreads.items():
        noise = np.random.default_rng([zlib.crc32(name.encode()), seed]).standard_normal(out[name].shape)
        drawn = base * np.exp(spread * noise) if base else spread * noise
        out[name] = __import__('jax').numpy.asarray(drawn.astype(out[name].dtype))
    for name, factor in factors.items():
        out[name] = (out[name] * factor).astype(out[name].dtype)
    return out
```

```python
import math
from contextlib import ExitStack

import numpy as np

import concourse.bass as bass
from concourse import mybir

F32 = mybir.dt.float32
I32 = mybir.dt.int32
ALU = mybir.AluOpType
ACT = mybir.ActivationFunctionType
AX = mybir.AxisListType.X

P = 128
S = 256
T = S // P
D = 1024
KD = D // P
HD = 64
CH = 64
NB = 512
RING = 6
TILE = 4096
DEPTH = 2
TOPK = 64
IDX_HEADS = 4
HG_BLOCK = 16
HG_HEADS = 8
RET_HEADS = 4
D_FF_2 = 2816
N_EXPERTS = 8
D_EXP = 3584
NEG = -1.0e30
RMS_EPS = 1e-6
LN_EPS = 1e-5
ALPHA = (2.0 * DEPTH) ** 0.25
SCALE = HD ** -0.5
MAGIC = 1.5 * 2.0 ** 23


def shape_constants():
    q, k = np.arange(S), np.arange(S)
    r = np.arange(P)
    parts = {}
    parts["ident"] = np.eye(P)
    chunk_ok = (k[None, :] // CH) <= (q[:, None] // CH)
    window_ok = chunk_ok & ((q[:, None] // CH) - (k[None, :] // CH) <= 2)
    by_tile = lambda m: m.reshape(T, P, -1).transpose(1, 0, 2).reshape(P, -1)
    parts["chunk_mask"] = by_tile(np.where(chunk_ok, 0.0, NEG))
    parts["window_mask"] = np.where(window_ok, 0.0, NEG)[P:]
    dist = np.concatenate([q[None, :] - r[:, None], r[None, :] - r[:, None]], 1)
    parts["strict"] = (dist > 0) * 1.0
    parts["dist"] = np.where(dist >= 0, dist, 1e6)
    parts["later"] = (r[:, None] > r[None, :]) * 1.0
    parts["upto"] = (r[:, None] <= r[None, :]) * 1.0
    parts["ones"] = np.ones((P, P))
    same = (r[:, None] // HG_BLOCK) == (r[None, :] // HG_BLOCK)
    parts["block_upto"] = (same & (r[:, None] <= r[None, :])) * 1.0
    parts["block_later"] = (same & (r[:, None] > r[None, :])) * 1.0
    parts["in_block"] = (r[:, None] // HG_BLOCK == np.arange(P // HG_BLOCK)[None, :]) * 1.0
    parts["even_odd"] = np.stack([(r // HG_BLOCK) % 2 == 0, (r // HG_BLOCK) % 2 == 1], 1) * 1.0
    half = 64
    inv = (1.0 / (np.float32(10000.0) ** np.linspace(0, 1, half, dtype=np.float32))).astype(np.float32)
    ang = (q.astype(np.float32)[:, None] * inv[None, :]).astype(np.float64)
    parts["ret_cos"] = by_tile(np.cos(ang))
    parts["ret_sin"] = by_tile(np.sin(ang))
    inv1 = np.float32(10000.0) ** (-np.arange(0, HD, 2, dtype=np.float32) / HD)
    parts["inv_freq"] = np.broadcast_to(inv1, (P, HD // 2))
    parts["slots"] = np.broadcast_to(r, (P, P))
    e = np.arange(N_EXPERTS)
    parts["tie_first"] = np.broadcast_to((e[None, :] < e[:, None]).reshape(1, -1) * 1.0, (P, 64))
    at, n = {}, 0
    for name, a in parts.items():
        at[name] = (n, a.shape[1])
        n += a.shape[1]
    return np.concatenate([np.asarray(a, np.float32) for a in parts.values()], 1), at


def schedule():
    out = []

    def add(kind, **kw):
        out.append(dict(kind=kind, **kw))

    def product(use, weights, **kw):
        add("product", use=use, weights=weights, **kw)

    def cols(name, layer, c0, n, rows=KD):
        per = min(NB * (KD // rows), 1024)
        return [(name, layer, 0, rows, c0 + c, min(per, n - c)) for c in range(0, n, per)]

    add("setup")
    for l in range(DEPTH):
        add("rms_in", gain=("attn_norm", l))
        add("turn", src="S0", dst="HT", chunks=KD, gain=("attn_norm", l))
        product("copy", cols("w_in", l, 0, 1536), lhs="HT", first=0)
        add("qk_norm", layer=l, gain="a", src="P")
        add("pairs", use="A", layer=l)
        add("a_finish", layer=l)
        product("gate", cols("w_in", l, 4932, D), lhs="HT")
        add("turn", src="S3", dst="S1", chunks=4, gain=None)
        product("merge", cols("w_br_a", l, 0, D, rows=4), lhs="S1", first_branch=True)
        product("copy", cols("w_in", l, 1536, 1536), lhs="HT", first=0)
        add("sticks", layer=l)
        product("gate", cols("w_in", l, 4932 + D, D), lhs="HT")
        add("turn", src="S3", dst="S1", chunks=4, gain=None)
        product("merge", cols("w_br_b", l, 0, D, rows=4), lhs="S1", first_branch=False)
        product("copy", cols("w_in", l, 3072, 1536) + [("w_in", l, 0, KD, 4608, 324)], lhs="HT", first=0)
        add("qk_norm", layer=l, gain="c", src="P")
        add("index_prepare", layer=l)
        add("pairs", use="I", layer=l)
        add("index_select", layer=l)
        add("pairs", use="C", layer=l)
        product("gate", cols("w_in", l, 4932 + 2 * D, D), lhs="HT")
        add("turn", src="S3", dst="S1", chunks=4, gain=None)
        product("merge", cols("w_br_c", l, 0, D, rows=4), lhs="S1", first_branch=False)
        add("turn", src="MERGED", dst="HT", chunks=KD, gain=None)
        product("resid", cols("w_out", l, 0, D), lhs="HT", alpha=1.0)
        add("rms_in", gain=("mlp_norm", l))
        add("turn", src="S0", dst="HT", chunks=KD, gain=("mlp_norm", l))
        add("mlp", layer=l, use="relu2", blocks=[(c, NB) for c in range(0, 4 * D, NB)])
        add("mlp_add", alpha=1.0)
        add("rms_in", gain=("ple_norm", l))
        add("turn", src="S0", dst="HT", chunks=KD, gain=("ple_norm", l))
        product("gate", cols("w_ple_gate", l, 0, D), lhs="HT", ple=l)
        add("turn", src="P", dst="S1", chunks=2, gain=None, width=256)
        product("ple", [("w_ple_proj", l, 0, 2, 0, D)], lhs="S1", **({"load": 0} if l == DEPTH - 1 else {}))
    add("layer_norm", gain=("ln_in_g_2", "ln_in_b_2", None), n=0)
    for l in range(DEPTH):
        add("turn", src="X", dst="HT", chunks=KD, gain=None)
        product("copy", cols("w_in_2", l, 0, 3072), lhs="HT", first=0)
        add("ret_rotary", layer=l)
        add("retention")
        add("ret_finish")
        product("gate", cols("w_in_2", l, 8704, D), lhs="HT")
        add("turn", src="S3", dst="S1", chunks=KD, gain=None)
        product("merge", cols("ret_w_out_2", l, 0, D), lhs="S1", first_branch=True)
        product("copy", cols("w_in_2", l, 3072, 4096), lhs="HT", first=0)
        add("hgrn_forget", layer=l)
        add("hgrn_decay")
        add("hgrn_scale")
        add("hgrn_heads")
        add("hgrn_finish", layer=l)
        product("gate", cols("w_in_2", l, 8704 + D, D), lhs="HT")
        add("turn", src="S3", dst="S1", chunks=KD, gain=None)
        product("merge", cols("hgrn_w_out_2", l, 0, D), lhs="S1", first_branch=False)
        product("copy", cols("w_in_2", l, 7168, 1536), lhs="HT", first=0)
        add("swa_prepare", load=2 * l + 1)
        add("pairs", use="W", layer=l)
        product("gate", cols("w_in_2", l, 8704 + 2 * D, D), lhs="HT")
        add("turn", src="S3", dst="S1", chunks=KD, gain=None)
        product("merge", cols("swa_w_out_2", l, 0, D), lhs="S1", first_branch=False)
        add("turn", src="MERGED", dst="HT", chunks=KD, gain=None)
        product("resid", cols("w_o_2", l, 0, D), lhs="HT", alpha=ALPHA)
        add("layer_norm", gain=("ln_mix_g_2", "ln_mix_b_2", l), n=2 * l + 1)
        add("turn", src="X", dst="HT", chunks=KD, gain=None, load=2 * l + 2)
        if l % 2 == 0:
            add("mlp", layer=l // 2, use="swiglu",
                blocks=[(c, min(NB, D_FF_2 - c)) for c in range(0, D_FF_2, NB)])
            add("mlp_add", alpha=ALPHA)
        else:
            add("route", layer=l // 2)
            add("experts", layer=l // 2)
            add("moe_add")
        add("layer_norm", gain=("ln_ffn_g_2", "ln_ffn_b_2", l), n=2 * l + 2)
    return out


LN_ROWS = [("ln_in_g_2", "ln_in_b_2", None), ("ln_mix_g_2", "ln_mix_b_2", 0), ("ln_ffn_g_2", "ln_ffn_b_2", 0),
           ("ln_mix_g_2", "ln_mix_b_2", 1), ("ln_ffn_g_2", "ln_ffn_b_2", 1)]


def build(nc, a, out, const_at):
    stages = schedule()
    with ExitStack() as ctx:
        def sb(name, shape, dt=F32):
            return ctx.enter_context(nc.sbuf_tensor(name, [P] + shape, dt))

        def sem(name):
            return ctx.enter_context(nc.semaphore(name))

        ring = sb("weight_ring", [RING, TILE])
        X = sb("x_residual", [T, D])
        HT = sb("h_transposed", [KD, S])
        PR = sb("projected", [T, 4096])
        MERGED = sb("merged", [T, D])
        S0 = sb("scratch0", [T, D])
        S1 = sb("scratch1", [T, D])
        S2 = sb("scratch2", [T, D])
        S3 = sb("scratch3", [T, D])
        QKT = sb("qk_transposed", [2, NB])
        PT = sb("weights_transposed", [2, 384])
        n_const = sum(w for _, w in const_at.values())
        CONST = sb("constants", [n_const])
        STAT = sb("mean_squares", [32])
        RSTD = sb("rsqrt", [32])
        MHALF = sb("minus_half", [32])
        COS = sb("rope_cos", [T, 32])
        SIN = sb("rope_sin", [T, 32])
        GAINS = sb("gain_columns", [6, KD])
        HG = sb("head_gains", [DEPTH, 5, HD])
        SUBLN = sb("subln_gain", [DEPTH, P])
        HGN = SUBLN
        LAM = sb("minus_lambda", [DEPTH, 4])
        SINK = sb("sinks", [DEPTH, 16])
        MX = sb("row_max", [2, 4])
        NMX = sb("minus_row_max", [2, 4])
        SINKD = sb("sink_minus_max", [2, 4])
        SUM = sb("row_sum", [2, 4])
        RS = sb("row_scale", [2, 4])
        MV = sb("mean_var", [T, 2])
        BST = sb("bn_stats", [T, 2, 6])
        POSI = sb("positions_int", [T], I32)
        DEC = sb("block_decay", [2, 16])
        LAME = sb("lambda_exp", [DEPTH, 2])
        EDS = sb("sink_exp", [2, 4])
        TOP = sb("top_values", [T, 8])
        NEED = sb("ties_needed", [T, 2])
        ROUTE = sb("route", [T, 4, 16])
        NPASS = sb("passes", [2], I32)
        PS = ctx.enter_context(nc.psum_tensor("banks", [P, 8, NB], F32))
        buf = dict(X=X, HT=HT, P=PR, MERGED=MERGED, S0=S0, S1=S1, S2=S2, S3=S3)

        def C(name):
            n, w = const_at[name]
            return CONST[:, n:n + w]

        SM = S0.rearrange("p t d -> p (t d)").rearrange("p (b i k) -> p b i k", b=2, i=4)
        PRf = PR.rearrange("p t d -> p (t d)")
        S0f, S1f, S2f = (b.rearrange("p t d -> p (t d)") for b in (S0, S1, S2))
        IDXM = PR[:, :, 2304:2560]
        SQ = sb("square_sums", [T])
        ROUTER = PRf[:, 6400:6464].rearrange("p (k e) -> p k e", k=KD)
        RT = PRf[:, 6144:6400].rearrange("p (i t e) -> p i t e", i=2, t=T)
        STATE = PT.rearrange("p a b -> p (a b)")[:, 0:512].rearrange("p (s v) -> p s v", s=4)
        HA = PT.rearrange("p a b -> p (a b)")[:, 512:768].rearrange("p (t q) -> p t q", t=T)
        LAMB = PR[:, 0, 0:DEPTH * 4 * HD].rearrange("p (l i d) -> p l i d", l=DEPTH, i=4)
        HID = PRf[:, 0:2048].rearrange("p (b t c) -> p b t c", b=2, t=T)
        HIDT = PRf[:, 2048:4096].rearrange("p (b k s) -> p b k s", b=2, k=4)
        SG = PRf[:, 4096:6144].rearrange("p (b t c) -> p b t c", b=2, t=T)
        HID2 = PRf[:, 0:1024].rearrange("p (b c) -> p b c", b=2)
        HIDT2 = PRf[:, 1024:2048].rearrange("p (b k s) -> p b k s", b=2, k=4)
        SG2 = PRf[:, 2048:3072].rearrange("p (b c) -> p b c", b=2)
        XG = PRf[:, 3072:4096].rearrange("p (k s) -> p k s", k=KD)
        YE = PRf[:, 4096:5120].rearrange("p (b c) -> p b c", b=2)
        CHOICE = PRf[:, 5120:5376].rearrange("p (t s) -> p t s", t=T)
        CHOICEW = PRf[:, 5376:5632].rearrange("p (t s) -> p t s", t=T)
        CHOICET = PRf[:, 5632:5888].rearrange("p (t s) -> p t s", t=T)

        stage_done = sem("stage_done")
        landed = [sem(f"tile_landed{i}") for i in range(RING)]
        down_used = sem("down_tile_used")
        xd_used = sem("expert_down_tile_used")
        const_in = sem("constants_loaded")
        rows_in = sem("ln_rows_loaded")
        ple_in = sem("ple_loaded")
        router_in = sem("router_loaded")
        hgn_in = sem("hgrn_gains_loaded")
        lb_in = sem("lower_bounds_loaded")
        sums_ready = sem("sums_ready")
        rsqrt_ready = sem("rsqrt_ready")
        squares = sem("squares_summed")
        product_full = sem("product_full")
        act_evac = sem("product_read_by_scalar")
        dve_evac = sem("product_read_by_vector")
        turned = sem("bank_turned")
        turned_act = sem("turned_read_by_scalar")
        turned_dve = sem("turned_read_by_vector")
        qk_turned = sem("qk_turned")
        qk_copied = sem("qk_copied")
        scores_full = sem("scores_full")
        scores_read = sem("scores_read")
        max_ready = sem("max_ready")
        probs_ready = sem("probs_ready")
        probs_turned = sem("probs_turned")
        probs_act = sem("probs_read_by_scalar")
        probs_dve = sem("probs_read_by_vector")
        values_full = sem("values_full")
        values_read = sem("values_read")
        dve_to_act = sem("vector_to_scalar")
        act_to_dve = sem("scalar_to_vector")
        dve_to_pe = sem("vector_to_tensor")
        pe_to_dve = sem("tensor_to_vector")
        stick_scores = sem("stick_scores_full")
        kv_full = sem("kv_full")
        state_ready = sem("state_ready")
        state_used = sem("state_used")
        xg_full = sem("expert_gate_full")
        xu_full = sem("expert_up_full")
        xh_ready = sem("expert_hidden_ready")
        xh_turned = sem("expert_hidden_turned")
        xh_copied = sem("expert_hidden_copied")
        sig_ready = sem("sigmoid_exp_ready")
        xsig_ready = sem("expert_sigmoid_exp_ready")
        hidden_ready = sem("hidden_ready")
        gate_full = sem("gate_full")
        gate_read = sem("gate_read")
        up_full = sem("up_full")
        up_read = sem("up_read")
        hid_turned = sem("hidden_turned")
        hid_act = sem("hidden_read_by_scalar")
        hid_dve = sem("hidden_read_by_vector")
        down_read = sem("down_read")
        gathered = sem("gathered")
        gathered_read = sem("gathered_read")
        choice_ready = sem("choice_ready")
        choice_turned = sem("choice_turned")
        choice_copied = sem("choice_copied")
        spread_full = sem("spread_full")
        spread_read = sem("spread_read")
        passes_ready = sem("passes_ready")
        out_sem = sem("out_written")

        class Count:

            def __init__(self):
                self.n = {}

            def of(self, name):
                return self.n.get(name, 0)

            def add(self, name, k=1):
                self.n[name] = self.n.get(name, 0) + k
                return self.n[name]

        def finish_stage(eng, n):
            eng.drain().then_inc(stage_done, 1)
            eng.wait_ge(stage_done, 3 * (n + 1))

        def heads(ap, g, d):
            return ap.rearrange("p (g d) -> p g d", g=g, d=d)

        def pair_cols(use, n):
            if use == "A":
                return n * P, 512 + n * P, [1024 + n * P] * 2, P
            if use == "C":
                return n * P, 512 + n * P, [1024 + n * P, 1024 + n * P + HD], HD
            if use == "W":
                g = n // 2
                return n * P, 2048 + g * P, [1280 + g * HD] * 2, HD
            return 1536 + n * P, 2048, None, 0

        N_PAIRS = dict(A=4, C=4, W=8, I=2)

        N_LOADS = 25

        def gain_col(gain, k):
            name, l = gain
            return GAINS[:, ("attn_norm", "mlp_norm", "ple_norm").index(name) * DEPTH + l, k:k + 1]

        def block_widths(st):
            for *_, w in st["weights"]:
                for b0 in range(0, w, NB):
                    yield min(NB, w - b0)

        seen = 0
        for st in stages:
            st["qk_before"] = seen
            seen += {"pairs": N_PAIRS.get(st.get("use"), 0), "sticks": 4, "retention": RET_HEADS,
                     "hgrn_heads": HG_HEADS}.get(st["kind"], 0)

        block = ctx.enter_context(nc.Block())

        @block.sync
        def _(sp):
            q = 0

            released = []

            def load(dst, src, q, used_at):
                if q >= RING:
                    sp.wait_ge(*released[q - RING])
                sp.dma_start(dst, src).then_inc(landed[q % RING], 16)
                released.append(used_at)

            blocks_seen, gates_seen, ups_seen, downs_seen = 0, 0, 0, 0

            def dst(q, rows, width):
                return ring[:, q % RING, 0:rows * width].rearrange("p (k c) -> p k c", k=rows)

            for st in stages:
                if st["kind"] == "product":
                    for name, l, r0, rows, c0, w in st["weights"]:
                        src = a[name][l, r0 * P:(r0 + rows) * P, c0:c0 + w].rearrange("(k p) c -> p k c", p=P)
                        blocks_seen += -(-w // NB)
                        load(dst(q, rows, w), src, q, (product_full, blocks_seen))
                        q += 1
                if st["kind"] == "mlp":
                    l = st["layer"]
                    ups = ["w_up"] if st["use"] == "relu2" else ["ffn_w_gate_2", "ffn_w_up_2"]
                    down = a["w_down" if st["use"] == "relu2" else "ffn_w_down_2"]
                    for c0, w in st["blocks"]:
                        for name in ups:
                            if name == "ffn_w_gate_2":
                                gates_seen += 1
                                used_at = (gate_full, gates_seen)
                            else:
                                ups_seen += 1
                                used_at = (up_full, ups_seen)
                            load(dst(q, KD, w), a[name][l, :, c0:c0 + w].rearrange("(k p) c -> p k c", p=P), q, used_at)
                            q += 1
                        downs_seen += 1
                        load(dst(q, w // P, D), down[l, c0:c0 + w, :].rearrange("(k p) c -> p k c", p=P), q,
                             (down_used, downs_seen))
                        q += 1
                if st["kind"] == "experts":
                    J = D_EXP // NB
                    sp.wait_ge(passes_ready, 1)
                    passes = sp.value_load(NPASS[0:1, 0:1], min_val=1, max_val=T)
                    per = 3 * (D_EXP // NB) * 2
                    assert per % RING == 0
                    with sp.Fori(0, passes * (N_EXPERTS // 2)) as i:
                        ee = i % (N_EXPERTS // 2) * 2
                        for k in range(per):
                            e, j, role = ee + k // (per // 2), k % (per // 2) // 3, k % 3
                            if role == 2:
                                src = a["moe_w_down_2"][0, bass.ds(e, 1), j * NB:(j + 1) * NB, :].rearrange(
                                    "e (k p) c -> p (e k) c", p=P)
                                d = dst(q + k, NB // P, D)
                            else:
                                name = ("moe_w_gate_2", "moe_w_up_2")[role]
                                src = a[name][0, bass.ds(e, 1), :, j * NB:(j + 1) * NB].rearrange(
                                    "e (k p) c -> p (e k) c", p=P)
                                d = dst(q + k, KD, NB)
                            block_index = i * (2 * J) + k // 3
                            sp.wait_ge(xd_used if role == 2 else xh_ready, block_index + 1)
                            sp.dma_start(d, src).then_inc(landed[(q + k) % RING], 16)
            sp.wait_ge(stage_done, 3 * len(stages))
            sp.dma_start(out[0].rearrange("(t p) d -> p t d", p=P), X[:]).then_inc(out_sem, 16)
            sp.wait_ge(out_sem, 16)

        @block.tensor
        def _(pe):
            c = Count()
            tiles = [0]
            ident = C("ident")

            def take_tile(extra=0):
                q = tiles[0]
                tiles[0] += 1
                pe.wait_ge(landed[q % RING], 16 * (q // RING + 1 + extra))
                return q % RING

            history = []

            def product(st):
                lhs = buf[st["lhs"]].rearrange("p t d -> p (t d)").rearrange("p (k s) -> p k s", s=S)
                for name, l, r0, rows, c0, w in st["weights"]:
                    slot = take_tile()
                    wt = ring[:, slot, 0:rows * w].rearrange("p (k c) -> p k c", k=rows)
                    for b0 in range(0, w, NB):
                        bw = min(NB, w - b0)
                        g = len(history)
                        if g >= 2:
                            na = sum(h[0] for h in history[:g - 1])
                            nd = sum(h[1] for h in history[:g - 1])
                            if na:
                                pe.wait_ge(act_evac, na)
                            if nd:
                                pe.wait_ge(dve_evac, nd)
                        for k in range(rows):
                            for t in range(T):
                                mm = nc.tensor.matmul(PS[:, 2 * (g % 2) + t, 0:bw], lhs[:, k, t * P:(t + 1) * P],
                                                      wt[:, k, b0:b0 + bw], start=k == 0, stop=k == rows - 1)
                        mm.then_inc(product_full, 1)
                        history.append({"copy": (1, 1), "gate": (1, 0)}.get(st["use"], (0, 1)))

            def turn(st):
                src = buf[st["src"]]
                for b in range((st["chunks"] + 1) // 2):
                    for k in (2 * b, 2 * b + 1):
                        for t in range(T):
                            tr = nc.tensor.transpose(PS[:, 4 + b, (k % 2) * S + t * P:(k % 2) * S + (t + 1) * P],
                                                     src[:, t, k * P:(k + 1) * P], ident)
                    tr.then_inc(turned, 1)

            def turn_qk(q0, k0):
                n = c.of("qk")
                if n:
                    pe.wait_ge(qk_copied, n)
                for i, (col, t) in enumerate([(q0, 0), (q0, 1), (k0, 0), (k0, 1)]):
                    tr = nc.tensor.transpose(PS[:, 0, i * P:(i + 1) * P], PR[:, t, col:col + P], ident)
                tr.then_inc(qk_turned, 1)
                c.add("qk")
                pe.wait_ge(qk_copied, n + 1)
                return QKT[:, n % 2]

            def pairs(st):
                use = st["use"]
                N = N_PAIRS[use]

                def front(n):
                    q0, k0, _, _ = pair_cols(use, n)
                    z = turn_qk(q0, k0)
                    m = c.add("scores")
                    if m > 2:
                        pe.wait_ge(scores_read, m - 2)
                    for t in range(T):
                        for h in range(2):
                            rows = slice(h * HD, (h + 1) * HD)
                            mm = nc.tensor.matmul(PS[:, 1 + 2 * (m % 2) + h, t * S:(t + 1) * S],
                                                  z[rows, t * P:(t + 1) * P], z[rows, S:2 * S], start=True, stop=True)
                    mm.then_inc(scores_full, 1)

                def back(n):
                    m = c.add("probs")
                    _, _, v0, vw = pair_cols(use, n)
                    pe.wait_ge(probs_ready, m)
                    if m > 1:
                        pe.wait_ge(probs_act, m - 1)
                        pe.wait_ge(probs_dve, m - 1)
                    for h in range(2):
                        for kt, t in ((0, 0), (0, 1), (1, 1)):
                            tr = nc.tensor.transpose(PS[:, 5 + h, (kt + t) * P:(kt + t + 1) * P],
                                                     SM[:, m % 2, 2 * t + h, kt * P:(kt + 1) * P], ident)
                    tr.then_inc(probs_turned, 1)
                    pe.wait_ge(probs_act, m)
                    pe.wait_ge(probs_dve, m)
                    if m > 1:
                        pe.wait_ge(values_read, m - 1)
                    for t in range(T):
                        for h in range(2):
                            for kt in range(t + 1):
                                o = (2 * t + h) * vw
                                mm = nc.tensor.matmul(PS[:, 7, o:o + vw], PT[:, h, (kt + t) * P:(kt + t + 1) * P],
                                                      PR[:, kt, v0[h]:v0[h] + vw], start=kt == 0, stop=kt == t)
                    mm.then_inc(values_full, 1)

                for n in range(N + 1):
                    if n < N:
                        front(n)
                    if n >= 1 and use != "I":
                        back(n - 1)

            def sticks(st):
                for n in range(4):
                    z = turn_qk(n * P, 512 + n * P)
                    for h in range(2):
                        rows = slice(h * HD, (h + 1) * HD)
                        nc.tensor.matmul(PS[:, 1 + h, 0:S], z[rows, S:S + P], z[rows, 0:S], start=True, stop=True)
                        mm = nc.tensor.matmul(PS[:, 1 + h, S:S + P], z[rows, S + P:2 * S], z[rows, P:S],
                                              start=True, stop=True)
                    mm.then_inc(stick_scores, 1)
                    pe.wait_ge(dve_to_pe, c.add("dve_to_pe"))
                    for h in range(2):
                        lg = S1.rearrange("p t d -> p (t d)")[:, h * 384:(h + 1) * 384]
                        nc.tensor.matmul(PS[:, 5 + h, 0:P], C("later"), lg[:, 0:P], start=True, stop=True)
                        nc.tensor.matmul(PS[:, 5 + h, P:S], C("later"), lg[:, P:S], start=True, stop=False)
                        nc.tensor.matmul(PS[:, 5 + h, P:S], C("ones"), lg[:, S:S + P], start=False, stop=True)
                        mm = nc.tensor.matmul(PS[:, 5 + h, S:S + P], C("later"), lg[:, S:S + P], start=True, stop=True)
                    mm.then_inc(pe_to_dve, 1)
                    pe.wait_ge(dve_to_pe, c.add("dve_to_pe"))
                    for t in range(T):
                        for h in range(2):
                            for kt in range(t + 1):
                                o = (2 * t + h) * HD
                                v0 = 1024 + n * P + h * HD
                                mm = nc.tensor.matmul(PS[:, 7, o:o + HD],
                                                      S0.rearrange("p t d -> p (t d)")[:, h * 384 + (kt + t) * P:h * 384 + (kt + t + 1) * P],
                                                      PR[:, kt, v0:v0 + HD], start=kt == 0, stop=kt == t)
                    mm.then_inc(pe_to_dve, 1)
                    pe.wait_ge(dve_to_pe, c.add("dve_to_pe"))

            def retention(st):
                for n in range(RET_HEADS):
                    z = turn_qk(n * P, 512 + n * P)
                    nc.tensor.matmul(PS[:, 1, 0:S], z[:, S:S + P], z[:, 0:S], start=True, stop=True)
                    nc.tensor.matmul(PS[:, 1, S:S + P], z[:, S + P:2 * S], z[:, P:S], start=True,
                                     stop=True).then_inc(pe_to_dve, 1)
                    pe.wait_ge(dve_to_pe, c.add("dve_to_pe"))
                    for t in range(T):
                        for kt in range(t + 1):
                            mm = nc.tensor.matmul(PS[:, 7, t * S:(t + 1) * S], PT[:, n % 2, (kt + t) * P:(kt + t + 1) * P],
                                                  PR[:, kt, 1024 + n * S:1024 + (n + 1) * S], start=kt == 0, stop=kt == t)
                    mm.then_inc(pe_to_dve, 1)
                    pe.wait_ge(dve_to_pe, c.add("dve_to_pe"))

            def hgrn_decay(st):
                for t in range(T):
                    for nb in range(2):
                        nc.tensor.matmul(PS[:, 2 * t + nb, :], C("block_upto"), S0[:, t, nb * NB:(nb + 1) * NB],
                                         start=True, stop=True)
                        nc.tensor.matmul(PS[:, 4 + 2 * t + nb, :], C("block_later"), S0[:, t, nb * NB:(nb + 1) * NB],
                                         start=True, stop=True)

            def hgrn_heads(st):
                per_tile = P // HG_BLOCK
                for n in range(HG_HEADS):
                    cols = slice(n * P, (n + 1) * P)
                    if n:
                        pe.wait_ge(dve_to_pe, c.of("dve_to_pe"))
                    z = turn_qk(n * P, 1024 + n * P)
                    for t in range(T):
                        nc.tensor.matmul(PS[:, 1, t * P:(t + 1) * P], z[:, S + t * P:S + (t + 1) * P],
                                         z[:, t * P:(t + 1) * P], start=True, stop=True)
                    for t in range(T):
                        mm = nc.tensor.matmul(PS[:, 1, S + t * per_tile:S + (t + 1) * per_tile], S0[:, t, cols],
                                              C("in_block"), start=True, stop=True)
                    mm.then_inc(pe_to_dve, 1)
                    for b in range(2 * per_tile - 1):
                        t, r = b // per_tile, b % per_tile
                        rows = slice(32 * (r // 2), 32 * (r // 2) + 32)
                        kst = (S1, S2)[r % 2]
                        u = 2 * t + r % 2
                        mm = nc.tensor.matmul(PS[:, 2 + r // 2, u * P:(u + 1) * P], kst[rows, t, cols],
                                              PR[rows, t, 2048 + n * P:2048 + (n + 1) * P], start=True, stop=True,
                                              tile_position=(rows.start, 0))
                    mm.then_inc(kv_full, 1)
                    pe.wait_ge(dve_to_pe, c.add("dve_to_pe"))
                    for b in range(2 * per_tile):
                        t, r = b // per_tile, b % per_tile
                        if r == 0:
                            nc.tensor.matmul(PS[:, 6, t * P:(t + 1) * P], PR[:, t, 2048 + n * P:2048 + (n + 1) * P],
                                             HA[:, t, :], start=True, stop=b == 0, skip_group_check=True)
                        if b >= 1:
                            m = c.add("state")
                            pe.wait_ge(state_ready, m)
                            mm = nc.tensor.matmul(PS[:, 6, b * HG_BLOCK:(b + 1) * HG_BLOCK], STATE[:, m % 4],
                                                  z[:, b * HG_BLOCK:(b + 1) * HG_BLOCK], start=False,
                                                  stop=True, skip_group_check=True)
                            mm.then_inc(state_used, 1)
                    pe.wait_ge(dve_to_pe, c.add("dve_to_pe"))
                    ho = QKT[:, c.of("qk") % 2, 0:S]
                    for t in range(T):
                        tr = nc.tensor.transpose(PS[:, 7, t * P:(t + 1) * P], ho[:, t * P:(t + 1) * P], ident)
                    tr.then_inc(pe_to_dve, 1)
                    c.add("dve_to_pe")

            def index_select(st):
                pe.wait_ge(dve_to_pe, c.add("dve_to_pe"))
                for t in range(T):
                    for kt in range(T):
                        tr = nc.tensor.transpose(PS[:, 4 + t, kt * P:(kt + 1) * P], S1[:, t, kt * P:(kt + 1) * P], ident)
                tr.then_inc(pe_to_dve, 1)
                pe.wait_ge(dve_to_pe, c.add("dve_to_pe"))
                n0, _ = const_at["upto"]
                for t in range(T):
                    e = lambda kt: S1[:, t, 512 + kt * P:512 + (kt + 1) * P]
                    nc.tensor.matmul(PS[:, 6, t * S:(t + 1) * S], e(0), CONST[:, n0:n0 + S], start=True, stop=False)
                    mm = nc.tensor.matmul(PS[:, 6, t * S + P:(t + 1) * S], e(1), C("upto"), start=False, stop=True)
                mm.then_inc(pe_to_dve, 1)

            def mlp(st):
                two = st["use"] == "swiglu"
                blocks = st["blocks"]
                down_slot = {}

                def up(j):
                    w = blocks[j][1]
                    for kind in (("gate", "up") if two else ("up",)):
                        if kind == "up" and two:
                            if j >= 1:
                                pe.wait_ge(hid_act, c.of("hid"))
                                pe.wait_ge(hid_dve, c.of("hid"))
                        bank = 0 if kind == "gate" else (2 if two else 2 * (j % 2))
                        if kind == "gate" and j >= 1:
                            pe.wait_ge(gate_read, c.of("gate"))
                        if not two and j >= 2:
                            pe.wait_ge(hid_act, c.of("hid"))
                            pe.wait_ge(hid_dve, c.of("hid"))
                        slot = take_tile()
                        wt = ring[:, slot, 0:KD * w].rearrange("p (k c) -> p k c", k=KD)
                        for k in range(KD):
                            for t in range(T):
                                mm = nc.tensor.matmul(PS[:, bank + t, 0:w], HT[:, k, t * P:(t + 1) * P], wt[:, k, :],
                                                      start=k == 0, stop=k == KD - 1)
                        mm.then_inc(gate_full if kind == "gate" else up_full, 1)
                        if kind == "gate":
                            c.add("gate")
                            if j >= 1:
                                turn_hidden(j - 1)
                                down(j - 1)
                    if not two and j >= 1:
                        turn_hidden(j - 1)
                        down(j - 1)
                    q = tiles[0]
                    tiles[0] += 1
                    down_slot[j] = q

                def turn_hidden(j):
                    w = blocks[j][1]
                    pe.wait_ge(hidden_ready, c.add("hidden"))
                    bank = 2 if two else 2 * (j % 2)
                    for i in range(w // P):
                        for t in range(T):
                            tr = nc.tensor.transpose(PS[:, bank + i // 2, (i % 2) * S + t * P:(i % 2) * S + (t + 1) * P],
                                                     HID[:, j % 2, t, i * P:(i + 1) * P], ident)
                    tr.then_inc(hid_turned, 1)
                    c.add("hid")

                def down(j):
                    w = blocks[j][1]
                    q = down_slot[j]
                    pe.wait_ge(hid_act, c.of("hid"))
                    pe.wait_ge(hid_dve, c.of("hid"))
                    pe.wait_ge(landed[q % RING], 16 * (q // RING + 1))
                    wt = ring[:, q % RING, 0:w // P * D].rearrange("p (k c) -> p k c", c=D)
                    for i in range(w // P):
                        for t in range(T):
                            for nb in range(2):
                                last = j == len(blocks) - 1 and i == w // P - 1
                                mm = nc.tensor.matmul(PS[:, 4 + 2 * t + nb, :], HIDT[:, j % 2, i, t * P:(t + 1) * P],
                                                      wt[:, i, nb * NB:(nb + 1) * NB], start=j == 0 and i == 0, stop=last)
                    mm.then_inc(down_used, 1)

                for j in range(len(blocks)):
                    up(j)
                turn_hidden(len(blocks) - 1)
                down(len(blocks) - 1)

            def route(st):
                pe.wait_ge(router_in, 16)
                for t in range(T):
                    for k in range(KD):
                        mm = nc.tensor.matmul(PS[:, 0, t * 8:(t + 1) * 8], HT[:, k, t * P:(t + 1) * P],
                                              ROUTER[:, k, :], start=k == 0, stop=k == KD - 1)
                mm.then_inc(pe_to_dve, 1)
                pe.wait_ge(dve_to_pe, c.add("dve_to_pe"))
                nc.tensor.matmul(PS[:, 1, 0:8], C("strict")[:, 0:P], ROUTE[:, 0, 1, 0:8], start=True, stop=True)
                nc.tensor.matmul(PS[:, 1, 8:16], C("ones"), ROUTE[:, 0, 1, 0:8], start=True, stop=False)
                nc.tensor.matmul(PS[:, 1, 8:16], C("strict")[:, 0:P], ROUTE[:, 1, 1, 0:8], start=False, stop=True)
                nc.tensor.matmul(PS[:, 1, 16:24], C("ones"), ROUTE[:, 0, 1, 0:8], start=True, stop=False)
                nc.tensor.matmul(PS[:, 1, 16:24], C("ones"), ROUTE[:, 1, 1, 0:8], start=False,
                                 stop=True).then_inc(pe_to_dve, 1)

            def experts(st):
                q0 = tiles[0]
                J = D_EXP // NB
                pe.wait_ge(passes_ready, 1)
                passes = pe.value_load(NPASS[0:1, 0:1], min_val=1, max_val=T)
                pe.drain().then_inc(xd_used, 2)
                pe.drain().then_inc(choice_turned, 1)
                with pe.Fori(0, passes * (N_EXPERTS // 2)) as i:
                    for half in range(2):
                        m = i * 2 + half
                        j0 = m * J
                        pe.wait_ge(choice_ready, m + 1)
                        for kk in range(2):
                            if kk:
                                pe.wait_ge(gathered_read, m * 2 + 1)
                            for k in range(4):
                                f = kk * 4 + k
                                for t in range(T):
                                    mm = nc.tensor.matmul(PS[:, 4, k * P:(k + 1) * P], X[:, t, f * P:(f + 1) * P],
                                                          CHOICE[:, t, :], start=t == 0, stop=t == T - 1)
                            mm.then_inc(gathered, 1)
                        pe.wait_ge(gathered_read, m * 2 + 2)
                        for t in range(T):
                            tr = nc.tensor.transpose(PS[:, 4, t * P:(t + 1) * P], CHOICEW[:, t, :], ident)
                        tr.then_inc(choice_turned, 1)
                        pe.wait_ge(choice_copied, m + 1)

                        def up(j):
                            for role in range(2):
                                k = 21 * half + 3 * j + role
                                qq = q0 + k
                                slot = qq % RING
                                pe.wait_ge(landed[slot], (qq // RING + 1 + i * (42 // RING)) * 16)
                                pe.wait_ge(xh_ready, j0 + j + 1)
                                bank = 2 * role + (half * J + j) % 2
                                wt = ring[:, slot, :].rearrange("p (k c) -> p k c", k=KD)
                                for kk in range(KD):
                                    mm = nc.tensor.matmul(PS[:, bank, :], XG[:, kk, :], wt[:, kk, :],
                                                          start=kk == 0, stop=kk == KD - 1)
                                mm.then_inc(xg_full if role == 0 else xu_full, 1)

                        def down(j):
                            pe.wait_ge(xh_ready, j0 + j + 3)
                            for x in range(4):
                                tr = nc.tensor.transpose(PS[:, 4, x * P:(x + 1) * P], HID2[:, (half * J + j) % 2, x * P:(x + 1) * P], ident)
                            tr.then_inc(xh_turned, 1)
                            pe.wait_ge(xh_copied, j0 + j + 1)
                            k = 21 * half + 3 * j + 2
                            qq = q0 + k
                            slot = qq % RING
                            pe.wait_ge(landed[slot], (qq // RING + 1 + i * (42 // RING)) * 16)
                            wt = ring[:, slot, :].rearrange("p (k c) -> p k c", c=D)
                            for x in range(4):
                                for nb in range(2):
                                    mm = nc.tensor.matmul(PS[:, 6 + nb, :], HIDT2[:, (half * J + j) % 2, x, :],
                                                          wt[:, x, nb * NB:(nb + 1) * NB],
                                                          start=j == 0 and x == 0, stop=j == J - 1 and x == 3)
                            mm.then_inc(xd_used, 1)

                        up(0)
                        for j in range(1, J):
                            up(j)
                            down(j - 1)
                        down(J - 1)
                        pe.wait_ge(down_read, m + 1)
                        for t in range(T):
                            for nb in range(2):
                                s = 2 * t + nb
                                pe.wait_ge(spread_read, m * 4 + s + 1)
                                nc.tensor.matmul(PS[:, 5, :], CHOICET[:, t, :], YE[:, nb, :], start=True,
                                                 stop=True).then_inc(spread_full, 1)

            run = dict(product=product, turn=turn, pairs=pairs, sticks=sticks, retention=retention,
                       hgrn_decay=hgrn_decay, hgrn_heads=hgrn_heads, index_select=index_select, mlp=mlp,
                       route=route, experts=experts)
            for n, st in enumerate(stages):
                if st["kind"] in run:
                    run[st["kind"]](st)
                finish_stage(pe, n)

        @block.scalar
        def _(act):
            c = Count()

            def load_rows(n):
                g, b, l = LN_ROWS[n]
                for i, name in enumerate((g, b)):
                    row = a[name].rearrange("(o d) -> o d", o=1) if l is None else a[name][l:l + 1, :]
                    act.dma_start(S2[:, i], row[0].partition_broadcast(P)).then_inc(rows_in, 16)

            def setup(st):
                k = 0
                loads = [(CONST[:], a["shape_constants"])]
                for i, (name, l) in enumerate([(m, l) for m in ("attn_norm", "mlp_norm", "ple_norm") for l in range(DEPTH)]):
                    loads.append((GAINS[:, i], a[name][l].rearrange("(k p) -> p k", p=P)))
                for i, name in enumerate(("a_q_norm", "a_k_norm", "c_q_norm", "c_k_norm", "idx_k_norm")):
                    for l in range(DEPTH):
                        loads.append((HG[:, l, i], a[name][l].partition_broadcast(P)))
                for l in range(DEPTH):
                    loads.append((SUBLN[:, l], a["a_subln"][l].partition_broadcast(P)))
                    loads.append((SINK[:, l], a["swa_sinks_2"][l].partition_broadcast(P)))
                    loads.append((LAMB[:, l], a["a_lambda"][l].rearrange("i d -> (i d)").partition_broadcast(P)
                                  .rearrange("p (i d) -> p i d", i=4)))
                loads.append((POSI[:], a["positions"][0].rearrange("(t p) -> p t", p=P)))
                loads.append((X[:], a["x"][0].rearrange("(t p) d -> p t d", p=P)))
                for dst, src in loads:
                    act.dma_start(dst, src, allow_slow_non_contiguous=True).then_inc(const_in, 16)
                assert len(loads) == N_LOADS, len(loads)
                act.wait_ge(dve_to_act, c.add("dve_to_act"))
                nc.scalar.activation(COS.rearrange("p t f -> p (t f)"), COS.rearrange("p t f -> p (t f)"), ACT.Sin)
                nc.scalar.activation(SIN.rearrange("p t f -> p (t f)"), SIN.rearrange("p t f -> p (t f)"), ACT.Sin)
                nc.scalar.activation(LAME.rearrange("p l i -> p (l i)"), LAME.rearrange("p l i -> p (l i)"),
                                     ACT.Exp).then_inc(act_to_dve, 1)

            def layer_norm(st):
                if st["n"] == 2 * DEPTH - 1:
                    act.dma_start(ROUTER, a["moe_router_2"][0].rearrange("(k p) e -> p k e", p=P)).then_inc(router_in, 16)

            def ret_rotary(st):
                if st["layer"] == 0:
                    for l in range(DEPTH):
                        act.dma_start(HGN[:, l], a["hgrn_norm_g_2"][l].partition_broadcast(P)).then_inc(hgn_in, 16)

            def rms_in(st):
                for t in range(T):
                    i = nc.scalar.activation(S1[:, t], X[:, t], ACT.Square, accum_out=SQ[:, t:t + 1])
                act.drain().then_inc(squares, 1)

            def turn(st):
                dst = buf[st["dst"]].rearrange("p t d -> p (t d)").rearrange("p (k s) -> p k s", s=S)
                if "load" in st:
                    load_rows(st["load"])
                for b in range(st["chunks"] // 2):
                    c.add("turned")
                    if b % 2 == 0:
                        act.wait_ge(turned, c.of("turned"))
                        if st["gain"] is None:
                            nc.scalar.activation(dst[:, 2 * b:2 * b + 2].rearrange("p k s -> p (k s)"), PS[:, 4 + b], ACT.Copy)
                        else:
                            for k in (2 * b, 2 * b + 1):
                                nc.scalar.activation(dst[:, k], PS[:, 4 + b, (k % 2) * S:(k % 2 + 1) * S], ACT.Copy,
                                                     scale=gain_col(st["gain"], k))

            def product(st):
                if "load" in st:
                    load_rows(st["load"])
                if "ple" in st:
                    act.dma_start(PR[:, :, 0:256], a["p"][st["ple"], 0].rearrange("(t p) d -> p t d", p=P)).then_inc(ple_in, 16)
                col = st.get("first", 0)
                for w in block_widths(st):
                    g = c.add("block") - 1
                    if st["use"] in ("copy", "gate"):
                        act.wait_ge(product_full, g + 1)
                    if st["use"] == "copy":
                        nc.scalar.activation(PR[:, 0, col:col + w], PS[:, 2 * (g % 2), 0:w], ACT.Copy).then_inc(act_evac, 1)
                    if st["use"] == "gate":
                        nc.scalar.activation(S0[:, :, col:col + w], PS[:, 2 * (g % 2):2 * (g % 2) + 2, 0:w], ACT.Exp,
                                             scale=-1.0).then_inc(act_evac, 1)
                    col += w
                if "ple" in st:
                    act.wait_ge(ple_in, 16 * (st["ple"] + 1))

            def copy_qk():
                n = c.add("qk")
                act.wait_ge(qk_turned, n)
                nc.scalar.activation(QKT[:, (n - 1) % 2], PS[:, 0, :], ACT.Copy).then_inc(qk_copied, 1)

            def pairs(st):
                use = st["use"]
                N = N_PAIRS[use]
                for n in range(N + 1):
                    if n < N:
                        copy_qk()
                    if use == "I":
                        continue
                    if n >= 1:
                        act.wait_ge(probs_turned, c.add("turned_probs"))
                        nc.scalar.activation(PT[:, 0], PS[:, 5, 0:384], ACT.Copy).then_inc(probs_act, 1)
                    if n < N:
                        m = c.add("probs")
                        act.wait_ge(max_ready, m)
                        for i in range(4):
                            nc.scalar.activation(SM[:, m % 2, i], SM[:, m % 2, i], ACT.Exp, bias=NMX[:, m % 2, i:i + 1],
                                                 accum_out=SUM[:, m % 2, i:i + 1])
                        if use == "W":
                            nc.scalar.activation(EDS[:, m % 2], SINKD[:, m % 2], ACT.Exp)
                        act.drain().then_inc(probs_ready, 1)

            def sticks(st):
                for n in range(4):
                    copy_qk()
                    z = PS[:, 1:3, 0:384]
                    w = S2f[:, 0:768].rearrange("p (h k) -> p h k", h=2)
                    act.wait_ge(stick_scores, c.add("stick_scores"))
                    nc.scalar.activation(w, z, ACT.Abs, scale=SCALE).then_inc(act_to_dve, 1)
                    act.drain()
                    nc.scalar.activation(w, w, ACT.Exp, scale=-1.0)
                    act.drain()
                    nc.scalar.activation(w, w, ACT.Ln, bias=1.0).then_inc(act_to_dve, 1)
                    act.wait_ge(dve_to_act, c.add("dve_to_act"))
                    nc.scalar.activation(S0f[:, 768:1536], S0f[:, 768:1536], ACT.Exp).then_inc(act_to_dve, 1)

            def retention(st):
                for n in range(RET_HEADS):
                    lg = math.log(1.0 - 2.0 ** (-5.0 - n))
                    nc.scalar.activation(S1f[:, n * 384:(n + 1) * 384], C("dist"), ACT.Exp, scale=lg).then_inc(act_to_dve, 1)
                for n in range(RET_HEADS):
                    copy_qk()

            def neg_exp_of(first, width=D):
                nc.scalar.activation(S0[:, :, 0:width], PR[:, :, first:first + width], ACT.Exp, scale=-1.0).then_inc(act_to_dve, 1)

            def hgrn_forget(st):
                hf = PR[:, :, 1024:2048]
                nc.scalar.activation(hf, hf, ACT.Exp, scale=-1.0).then_inc(act_to_dve, 1)
                if st["layer"] > 0:
                    for i in range(DEPTH):
                        act.dma_start(S3[:, i], a["hgrn_lower_bounds_2"][i].partition_broadcast(P)).then_inc(lb_in, 16)
                    act.wait_ge(dve_to_act, c.add("dve_to_act"))
                    nc.scalar.activation(S3[:, 0], S3[:, 0], ACT.Exp).then_inc(act_to_dve, 1)
                act.wait_ge(dve_to_act, c.add("dve_to_act"))
                nc.scalar.activation(S0[:], S0[:], ACT.Ln)

            def hgrn_scale(st):
                up, later = PS[:, 0:4].rearrange("p b c -> p (b c)"), PS[:, 4:8].rearrange("p b c -> p (b c)")
                nc.scalar.activation(S1f, up, ACT.Exp).then_inc(act_to_dve, 1)
                nc.scalar.activation(S2f, later, ACT.Exp).then_inc(act_to_dve, 1)
                act.wait_ge(dve_to_act, c.add("dve_to_act"))
                nc.scalar.activation(S1f, up, ACT.Exp, scale=-1.0).then_inc(act_to_dve, 1)

            def hgrn_heads(st):
                for n in range(HG_HEADS):
                    copy_qk()
                    act.wait_ge(dve_to_act, c.add("dve_to_act"))
                    nc.scalar.activation(DEC[:, n % 2], DEC[:, n % 2], ACT.Exp).then_inc(act_to_dve, 1)

            def mlp(st):
                two = st["use"] == "swiglu"
                for j in range(len(st["blocks"]) + 1):
                    if two and j < len(st["blocks"]):
                        w = st["blocks"][j][1]
                        act.wait_ge(gate_full, c.add("gate"))
                        nc.scalar.activation(SG[:, j % 2, :, 0:w], PS[:, 0:2, 0:w], ACT.Exp, scale=-1.0).then_inc(sig_ready, 1)
                    if j >= 1:
                        w = st["blocks"][j - 1][1]
                        n = min(2, w // P)
                        bank = 2 if two else 2 * ((j - 1) % 2)
                        act.wait_ge(hid_turned, c.add("hid"))
                        nc.scalar.activation(HIDT[:, (j - 1) % 2, 0:n].rearrange("p k s -> p (k s)"), PS[:, bank, 0:n * S],
                                             ACT.Copy).then_inc(hid_act, 1)

            def route(st):
                act.wait_ge(dve_to_act, c.add("dve_to_act"))
                nc.scalar.activation(ROUTE[:, :, 2, 0:8], ROUTE[:, :, 2, 0:8], ACT.Exp).then_inc(act_to_dve, 1)

            def experts(st):
                J = D_EXP // NB
                act.wait_ge(passes_ready, 1)
                passes = act.value_load(NPASS[0:1, 0:1], min_val=1, max_val=T)
                with act.Fori(0, passes * (N_EXPERTS // 2)) as i:
                    for half in range(2):
                        m = i * 2 + half
                        for kk in range(2):
                            act.wait_ge(gathered, m * 2 + kk + 1)
                            nc.scalar.activation(XG[:, 4 * kk:4 * kk + 4].rearrange("p k s -> p (k s)"), PS[:, 4, :],
                                                 ACT.Copy).then_inc(gathered_read, 1)
                        act.wait_ge(choice_turned, m + 2)
                        nc.scalar.activation(CHOICET.rearrange("p t s -> p (t s)"), PS[:, 4, 0:S],
                                             ACT.Copy).then_inc(choice_copied, 1)
                        for j in range(J + 1):
                            par = (half * J + j) % 2
                            if j < J:
                                act.wait_ge(xg_full, m * J + j + 1)
                                nc.scalar.activation(SG2[:, par], PS[:, par], ACT.Exp, scale=-1.0).then_inc(xsig_ready, 1)
                            if j >= 1:
                                act.wait_ge(xh_turned, m * J + j)
                                nc.scalar.activation(HIDT2[:, 1 - par].rearrange("p k s -> p (k s)"), PS[:, 4, :],
                                                     ACT.Copy).then_inc(xh_copied, 1)
                        act.wait_ge(xd_used, m * J + J + 2)
                        nc.scalar.activation(YE.rearrange("p b c -> p (b c)"), PS[:, 6:8].rearrange("p b c -> p (b c)"),
                                             ACT.Copy).then_inc(down_read, 1)

            run = dict(setup=setup, rms_in=rms_in, ret_rotary=ret_rotary, layer_norm=layer_norm, turn=turn, product=product, pairs=pairs, sticks=sticks,
                       retention=retention, hgrn_forget=hgrn_forget, hgrn_scale=hgrn_scale, hgrn_heads=hgrn_heads,
                       mlp=mlp, route=route, experts=experts, ret_finish=lambda st: neg_exp_of(2048),
                       hgrn_finish=lambda st: neg_exp_of(3072), swa_prepare=lambda st: load_rows(st["load"]))
            for n, st in enumerate(stages):
                if st["kind"] in run:
                    run[st["kind"]](st)
                finish_stage(act, n)

        rsqrts = [0]

        @block.vector
        def _(dve):
            c = Count()
            v = nc.vector

            def rsqrt(n, width):
                dve.drain()
                v.tensor_scalar(STAT[:, 0:n], STAT[:, 0:n], 1.0 / width, RMS_EPS, ALU.mult, ALU.add).then_inc(sums_ready, 1)
                rsqrts[0] += 1
                dve.wait_ge(rsqrt_ready, rsqrts[0])

            def group_norm(x, t, g, d, work):
                view = lambda b: b.rearrange("p t (g d) -> p t g d", g=g, d=d)
                v.tensor_tensor(work, x, x, ALU.mult)
                dve.drain()
                v.tensor_reduce(STAT[:, 0:t * g].rearrange("p (t g) -> p t g", t=t), view(work), AX, ALU.add)
                rsqrt(t * g, d)
                r = RSTD[:, 0:t * g].rearrange("p (t g) -> p t g", t=t).unsqueeze(3).broadcast_to([P, t, g, d])
                v.tensor_tensor(view(x), view(x), r, ALU.mult)
                dve.drain()

            def rope(x, g, half, cos, sin, w1, w2):
                view = lambda b: b.rearrange("p (g h d) -> p g h d", g=g, h=2, d=half)
                X4, A, B = view(x), view(w1), view(w2)
                cb = cos.unsqueeze(1).unsqueeze(1).broadcast_to([P, g, 2, half])
                sb_ = sin.unsqueeze(1).broadcast_to([P, g, half])
                v.tensor_tensor(A, X4, cb, ALU.mult)
                v.tensor_tensor(B[:, :, 0], X4[:, :, 1], sb_, ALU.mult)
                v.tensor_tensor(B[:, :, 1], X4[:, :, 0], sb_, ALU.mult)
                dve.drain()
                v.tensor_tensor(X4[:, :, 0], A[:, :, 0], B[:, :, 0], ALU.subtract)
                v.tensor_tensor(X4[:, :, 1], A[:, :, 1], B[:, :, 1], ALU.add)

            def setup(st):
                v.memset(STAT[:], 1.0)
                dve.wait_ge(const_in, 16 * N_LOADS)
                pos = SQ
                v.tensor_copy(pos[:], POSI[:])
                dve.drain()
                ang, n1, n2 = S1f[:, 0:64], S1f[:, 64:128], S1f[:, 128:192]
                for t in range(T):
                    v.tensor_scalar(ang[:, t * 32:(t + 1) * 32], C("inv_freq"), pos[:, t:t + 1], None, ALU.mult)
                dve.drain()
                for dst, turn_, shift in ((SIN, 0.0, 0.0), (COS, 0.25, math.pi / 2)):
                    d = dst.rearrange("p t f -> p (t f)")
                    v.tensor_scalar(n1, ang, 1 / (2 * math.pi), turn_, ALU.mult, ALU.add)
                    dve.drain()
                    v.tensor_scalar(n1, n1, MAGIC, None, ALU.add)
                    dve.drain()
                    v.tensor_scalar(n1, n1, MAGIC, None, ALU.subtract)
                    dve.drain()
                    v.scalar_tensor_tensor(out=d, in0=n1, scalar=-6.28125, in1=ang, op0=ALU.mult, op1=ALU.add)
                    dve.drain()
                    v.scalar_tensor_tensor(out=d, in0=n1, scalar=-(2 * math.pi - 6.28125), in1=d, op0=ALU.mult, op1=ALU.add)
                    dve.drain()
                    v.tensor_scalar(d, d, shift, 3.1415925, ALU.add, ALU.min)
                    dve.drain()
                    v.tensor_scalar(d, d, -3.1415925, None, ALU.max)
                pairs_ = LAMB.rearrange("p l (i j) d -> p l i j d", j=2)
                prod = S0f[:, 0:DEPTH * 2 * HD].rearrange("p (l i d) -> p l i d", l=DEPTH, i=2)
                for l in range(DEPTH):
                    v.tensor_tensor(prod[:, l], pairs_[:, l, :, 0], pairs_[:, l, :, 1], ALU.mult)
                dve.drain()
                for l in range(DEPTH):
                    v.tensor_reduce(LAME[:, l], prod[:, l], AX, ALU.add)
                dve.drain().then_inc(dve_to_act, 1)
                dve.wait_ge(act_to_dve, c.add("act_to_dve"))
                for l in range(DEPTH):
                    v.tensor_tensor(LAM[:, l, 0:1], LAME[:, l, 1:2], LAME[:, l, 0:1], ALU.subtract)
                dve.drain()
                for l in range(DEPTH):
                    v.tensor_scalar(LAM[:, l, 1:2], LAM[:, l, 0:1], -(0.8 - 0.6 * math.exp(-0.3 * l)), None, ALU.add)

            def rms_in(st):
                dve.wait_ge(squares, c.add("squares"))
                v.tensor_copy(STAT[:, 0:T], SQ[:])
                rsqrt(T, D)
                for t in range(T):
                    v.tensor_scalar(S0[:, t], X[:, t], RSTD[:, t:t + 1], None, ALU.mult)

            def turn(st):
                dst = buf[st["dst"]].rearrange("p t d -> p (t d)").rearrange("p (k s) -> p k s", s=S)
                for b in range(st["chunks"] // 2):
                    c.add("turned")
                    if b % 2 == 1:
                        dve.wait_ge(turned, c.of("turned"))
                        if st["gain"] is None:
                            v.tensor_copy(dst[:, 2 * b:2 * b + 2].rearrange("p k s -> p (k s)"), PS[:, 4 + b])
                        else:
                            for k in (2 * b, 2 * b + 1):
                                v.tensor_scalar(dst[:, k], PS[:, 4 + b, (k % 2) * S:(k % 2 + 1) * S],
                                                gain_col(st["gain"], k), None, ALU.mult)

            def product(st):
                use = st["use"]
                col = st.get("first", 0)
                for w in block_widths(st):
                    g = c.add("block") - 1
                    cs = slice(col, col + w)
                    ps = PS[:, 2 * (g % 2):2 * (g % 2) + 2, 0:w]
                    if use == "gate":
                        dve.wait_ge(act_evac, c.add("act_evac"))
                        v.tensor_scalar(S0[:, :, cs], S0[:, :, cs], 1.0, None, ALU.add)
                        dve.drain()
                        v.reciprocal(S0[:, :, cs], S0[:, :, cs])
                    else:
                        dve.wait_ge(product_full, g + 1)
                    if use == "copy":
                        c.add("act_evac")
                        v.tensor_copy(PR[:, 1, cs], ps[:, 1]).then_inc(dve_evac, 1)
                    if use == "merge" and st["first_branch"]:
                        v.tensor_tensor(MERGED[:, :, cs], ps, S0[:, :, cs], ALU.mult).then_inc(dve_evac, 1)
                    elif use in ("merge", "ple"):
                        v.tensor_tensor(S0[:, :, cs], ps, S0[:, :, cs], ALU.mult).then_inc(dve_evac, 1)
                        dve.drain()
                        acc = MERGED if use == "merge" else X
                        v.tensor_tensor(acc[:, :, cs], acc[:, :, cs], S0[:, :, cs], ALU.add)
                    if use == "resid":
                        v.scalar_tensor_tensor(out=X[:, :, cs], in0=X[:, :, cs], scalar=st["alpha"], in1=ps,
                                               op0=ALU.mult, op1=ALU.add).then_inc(dve_evac, 1)
                    col += w

            def qk_norm(st):
                l = st["layer"]
                i = 0 if st["gain"] == "a" else 2
                group_norm(PR[:, :, 0:D], T, 16, HD, S1[:])
                for k in range(2):
                    x = PR[:, :, k * 512:(k + 1) * 512].rearrange("p t (g d) -> p t g d", d=HD)
                    for t in range(T):
                        gb = HG[:, l, i + k].unsqueeze(1).broadcast_to([P, 8, HD])
                        v.tensor_tensor(x[:, t], x[:, t], gb, ALU.mult)
                dve.drain()
                for t in range(T):
                    rope(PR[:, t, 0:D], 16, 32, COS[:, t], SIN[:, t], S1[:, t], S2[:, t])

            def index_prepare(st):
                ik = PR[:, :, 1792:1856]
                group_norm(ik, T, 1, HD, S1[:, :, 0:HD])
                for t in range(T):
                    v.tensor_tensor(ik[:, t], ik[:, t], HG[:, st["layer"], 4], ALU.mult)
                dve.drain()
                for t in range(T):
                    rope(PR[:, t, 1536:1856], 5, 32, COS[:, t], SIN[:, t], S1[:, t, 0:320], S2[:, t, 0:320])
                dve.drain()
                for i in range(2):
                    v.tensor_copy(PR[:, :, 2048 + i * HD:2048 + (i + 1) * HD], ik)
                v.tensor_scalar(PR[:, :, 1856:1860], PR[:, :, 1856:1860], IDX_HEADS ** -0.5, None, ALU.mult)

            def index_pairs():
                for n in range(2):
                    m = c.add("scores")
                    dve.wait_ge(scores_full, m)
                    for h in range(2):
                        i = v.tensor_scalar(S2[:, :, (2 * n + h) * S:(2 * n + h + 1) * S],
                                            PS[:, 1 + 2 * (m % 2) + h, :].rearrange("p (t k) -> p t k", t=T), SCALE, 0.0,
                                            ALU.mult, ALU.max)
                    i.then_inc(scores_read, 1)
                for h in range(IDX_HEADS):
                    dve.drain()
                    for t in range(T):
                        w = PR[:, t, 1856 + h:1857 + h]
                        other = C("chunk_mask")[:, t * S:(t + 1) * S] if h == 0 else S3[:, t, 0:S]
                        v.scalar_tensor_tensor(out=S3[:, t, 0:S], in0=S2[:, t, h * S:(h + 1) * S], scalar=w,
                                               in1=other, op0=ALU.mult, op1=ALU.add)

            def index_select(st):
                for t in range(T):
                    v.tensor_copy(S2[:, t, 0:S], S3[:, t, 0:S])
                for r in range(TOPK // 8):
                    dve.drain()
                    for t in range(T):
                        v.max(TOP[:, t], S2[:, t, 0:S])
                    if r < TOPK // 8 - 1:
                        dve.drain()
                        for t in range(T):
                            v.match_replace(S2[:, t, 0:S], TOP[:, t], S2[:, t, 0:S], -3.0e38)
                dve.drain()
                for t in range(T):
                    v.tensor_scalar(S1[:, t, 0:S], S3[:, t, 0:S], TOP[:, t, 7:8], None, ALU.is_equal)
                    v.tensor_scalar(S1[:, t, S:2 * S], S3[:, t, 0:S], TOP[:, t, 7:8], None, ALU.is_gt)
                dve.drain()
                dve.drain().then_inc(dve_to_pe, 1)
                for t in range(T):
                    v.tensor_reduce(NEED[:, t, 0:1], S1[:, t, S:2 * S], AX, ALU.add)
                dve.drain()
                for t in range(T):
                    v.tensor_scalar(NEED[:, t, 1:2], NEED[:, t, 0:1], -1.0, float(TOPK), ALU.mult, ALU.add)
                dve.wait_ge(pe_to_dve, c.add("pe_to_dve"))
                v.tensor_copy(S1[:, :, 512:768], PS[:, 4:6, 0:S]).then_inc(dve_to_pe, 1)
                dve.wait_ge(pe_to_dve, c.add("pe_to_dve"))
                for t in range(T):
                    v.tensor_scalar(S2[:, t, 0:S], PS[:, 6, t * S:(t + 1) * S], NEED[:, t, 1:2], None, ALU.is_le)
                dve.drain()
                v.tensor_tensor(S2[:, :, 0:S], S2[:, :, 0:S], S1[:, :, 0:S], ALU.mult)
                dve.drain()
                v.tensor_tensor(S2[:, :, 0:S], S2[:, :, 0:S], S1[:, :, S:2 * S], ALU.add)
                dve.drain()
                v.tensor_scalar(IDXM, S2[:, :, 0:S], -1.0, -NEG, ALU.add, ALU.mult)

            def pairs(st):
                use = st["use"]
                if use == "I":
                    return index_pairs()
                N = N_PAIRS[use]
                mask = {"A": C("chunk_mask").rearrange("p (t k) -> p t k", t=T), "C": IDXM,
                        "W": C("chunk_mask").rearrange("p (t k) -> p t k", t=T)}[use]
                masks = [mask[:, 0], C("window_mask") if use == "W" else mask[:, 1]]

                def mid(n):
                    m = c.add("scores")
                    s = c.add("sm")
                    b = s % 2
                    dve.wait_ge(scores_full, m)
                    if s > 2:
                        dve.wait_ge(probs_turned, s - 2)
                    for h in range(2):
                        scores = PS[:, 1 + 2 * (m % 2) + h, :].rearrange("p (t k) -> p t k", t=T)
                        if use == "W":
                            for t in range(T):
                                i = v.scalar_tensor_tensor(out=SM[:, b, 2 * t + h], in0=scores[:, t], scalar=SCALE,
                                                           in1=masks[t], op0=ALU.mult, op1=ALU.add)
                        else:
                            i = v.scalar_tensor_tensor(out=SM[:, b].rearrange("p (t h) k -> p t h k", t=T)[:, :, h],
                                                       in0=scores, scalar=SCALE, in1=mask, op0=ALU.mult, op1=ALU.add)
                    i.then_inc(scores_read, 1)
                    dve.drain()
                    v.tensor_reduce(MX[:, b], SM[:, b], AX, ALU.max)
                    dve.drain()
                    if use == "W":
                        sk = SINK[:, st["layer"], 2 * n:2 * n + 2].unsqueeze(1).broadcast_to([P, T, 2])
                        by_t = lambda x: x[:, b].rearrange("p (t h) -> p t h", t=T)
                        v.tensor_tensor(by_t(MX), by_t(MX), sk, ALU.max)
                        dve.drain()
                        v.tensor_tensor(by_t(SINKD), sk, by_t(MX), ALU.subtract)
                    v.tensor_scalar(NMX[:, b], MX[:, b], -1.0, None, ALU.mult)
                    dve.drain().then_inc(max_ready, 1)

                def back(n):
                    m = c.add("probs")
                    b = m % 2
                    dve.wait_ge(probs_turned, m)
                    v.tensor_copy(PT[:, 1], PS[:, 6, 0:384]).then_inc(probs_dve, 1)
                    if use == "W":
                        v.tensor_tensor(SUM[:, b], SUM[:, b], EDS[:, b], ALU.add)
                        dve.drain()
                    v.reciprocal(RS[:, b], SUM[:, b])
                    dve.drain()
                    if use == "A":
                        for t in range(T):
                            v.tensor_scalar(RS[:, b, 2 * t + 1:2 * t + 2], RS[:, b, 2 * t + 1:2 * t + 2],
                                            LAM[:, st["layer"], 1:2], None, ALU.mult)
                        dve.drain()
                    dve.wait_ge(values_full, m)
                    vw = P if use == "A" else HD
                    for t in range(T):
                        for h in range(2):
                            i = 2 * t + h
                            o = PS[:, 7, i * vw:(i + 1) * vw]
                            dst = S1[:, t, h * P:(h + 1) * P] if use == "A" else S3[:, t, n * P + h * HD:n * P + (h + 1) * HD]
                            v.tensor_scalar(dst, o, RS[:, b, i:i + 1], None, ALU.mult)
                    dve.drain().then_inc(values_read, 1)
                    if use == "A":
                        v.tensor_tensor(S3[:, :, n * P:(n + 1) * P], S1[:, :, 0:P], S1[:, :, P:2 * P], ALU.add)

                for n in range(N + 1):
                    if n < N:
                        mid(n)
                    if n >= 1:
                        back(n - 1)

            def a_finish(st):
                l = st["layer"]
                group_norm(S3[:, :, 0:512], T, 4, P, S1[:, :, 0:512])
                keep = 1.0 - (0.8 - 0.6 * math.exp(-0.3 * l))
                for t in range(T):
                    y = S3[:, t, 0:512].rearrange("p (g d) -> p g d", g=4)
                    v.scalar_tensor_tensor(out=y, in0=y, scalar=keep, in1=SUBLN[:, l].unsqueeze(1).broadcast_to([P, 4, P]),
                                           op0=ALU.mult, op1=ALU.mult)

            def sticks(st):
                three = lambda x: x.rearrange("p (h k) -> p h k", h=2)
                keep = C("strict").unsqueeze(1).broadcast_to([P, 2, 384])
                soft, logs, arg, wts = (three(x) for x in (S1f[:, 768:1536], S1f[:, 0:768], S0f[:, 768:1536], S0f[:, 0:768]))
                for n in range(4):
                    z = PS[:, 1:3, 0:384]
                    dve.wait_ge(act_to_dve, c.add("act_to_dve"))
                    v.tensor_scalar(soft, z, SCALE, 0.0, ALU.mult, ALU.max)
                    dve.drain()
                    dve.wait_ge(act_to_dve, c.add("act_to_dve"))
                    v.tensor_tensor(soft, soft, three(S2f[:, 0:768]), ALU.add)
                    dve.drain()
                    v.tensor_tensor(logs, soft, keep, ALU.mult).then_inc(dve_to_pe, 1)
                    v.scalar_tensor_tensor(out=arg, in0=z, scalar=SCALE, in1=soft, op0=ALU.mult, op1=ALU.subtract)
                    dve.drain()
                    dve.wait_ge(pe_to_dve, c.add("pe_to_dve"))
                    v.tensor_tensor(arg, arg, PS[:, 5:7, 0:384], ALU.subtract).then_inc(dve_to_act, 1)
                    dve.wait_ge(act_to_dve, c.add("act_to_dve"))
                    v.tensor_tensor(wts, arg, keep, ALU.mult).then_inc(dve_to_pe, 1)
                    dve.wait_ge(pe_to_dve, c.add("pe_to_dve"))
                    v.tensor_copy(S3[:, :, n * P:(n + 1) * P],
                                  PS[:, 7, 0:S].rearrange("p (t d) -> p t d", t=T)).then_inc(dve_to_pe, 1)

            def ret_rotary(st):
                for t in range(T):
                    rope(PR[:, t, 0:D], 8, 64, C("ret_cos")[:, t * 64:(t + 1) * 64], C("ret_sin")[:, t * 64:(t + 1) * 64],
                         S1[:, t], S2[:, t])

            def retention(st):
                for n in range(RET_HEADS):
                    dve.wait_ge(pe_to_dve, c.add("pe_to_dve"))
                    dve.wait_ge(act_to_dve, c.add("act_to_dve"))
                    v.scalar_tensor_tensor(out=PT[:, n % 2], in0=PS[:, 1, 0:384], scalar=P ** -0.5,
                                           in1=S1f[:, n * 384:(n + 1) * 384], op0=ALU.mult, op1=ALU.mult).then_inc(dve_to_pe, 1)
                    dve.wait_ge(pe_to_dve, c.add("pe_to_dve"))
                    v.tensor_copy(S3[:, :, n * S:(n + 1) * S],
                                  PS[:, 7, :].rearrange("p (t d) -> p t d", t=T)).then_inc(dve_to_pe, 1)

            def silu_gate(first):
                g = PR[:, :, first:first + D]
                dve.wait_ge(act_to_dve, c.add("act_to_dve"))
                v.tensor_scalar(S0[:], S0[:], 1.0, None, ALU.add)
                dve.drain()
                v.reciprocal(S0[:], S0[:])
                dve.drain()
                v.tensor_tensor(S0[:], S0[:], g, ALU.mult)
                dve.drain()
                v.tensor_tensor(S3[:], S3[:], S0[:], ALU.mult)

            def ret_finish(st):
                group_norm(S3[:], T, 4, S, S1[:])
                silu_gate(2048)

            def hgrn_finish(st):
                group_norm(S3[:], T, 8, P, S1[:])
                dve.wait_ge(hgn_in, 16 * DEPTH)
                for t in range(T):
                    y = S3[:, t].rearrange("p (g d) -> p g d", g=8)
                    v.tensor_tensor(y, y, HGN[:, st["layer"]].unsqueeze(1).broadcast_to([P, 8, P]), ALU.mult)
                dve.drain()
                silu_gate(3072)

            def hgrn_forget(st):
                hf = PR[:, :, 1024:2048]
                dve.wait_ge(act_to_dve, c.add("act_to_dve"))
                v.tensor_scalar(hf, hf, 1.0, None, ALU.add)
                dve.drain()
                v.reciprocal(hf, hf)
                dve.drain()
                if st["layer"] == 0:
                    v.tensor_scalar(S0[:], hf, 1e-37, None, ALU.max).then_inc(dve_to_act, 1)
                    dve.drain()
                    v.tensor_scalar(hf, hf, -1.0, 1.0, ALU.mult, ALU.add)
                    return
                dve.wait_ge(lb_in, 16 * DEPTH)
                v.tensor_tensor(S3[:, 0], S3[:, 0], S3[:, 1], ALU.subtract).then_inc(dve_to_act, 1)
                dve.wait_ge(act_to_dve, c.add("act_to_dve"))
                v.tensor_scalar(S3[:, 0], S3[:, 0], 1.0, None, ALU.add)
                dve.drain()
                v.reciprocal(S3[:, 0], S3[:, 0])
                dve.drain()
                v.tensor_scalar(S3[:, 1], S3[:, 0], -1.0, 1.0, ALU.mult, ALU.add)
                dve.drain()
                for t in range(T):
                    v.tensor_tensor(S1[:, t], hf[:, t], S3[:, 1], ALU.mult)
                dve.drain()
                for t in range(T):
                    v.tensor_tensor(S0[:, t], S1[:, t], S3[:, 0], ALU.add)
                    v.tensor_tensor(hf[:, t], S3[:, 1], S1[:, t], ALU.subtract)
                dve.drain()
                v.tensor_scalar(S0[:], S0[:], 1e-37, None, ALU.max).then_inc(dve_to_act, 1)

            def hgrn_scale(st):
                hq, hk = PR[:, :, 0:D], PR[:, :, D:2 * D]
                dve.wait_ge(act_to_dve, c.add("act_to_dve"))
                v.tensor_tensor(hq, hq, S1[:], ALU.mult).then_inc(dve_to_act, 1)
                dve.wait_ge(act_to_dve, c.add("act_to_dve"))
                v.tensor_tensor(S2[:], S2[:], hk, ALU.mult)
                dve.drain()
                dve.wait_ge(act_to_dve, c.add("act_to_dve"))
                v.tensor_tensor(hk, hk, S1[:], ALU.mult)
                dve.drain()
                v.tensor_scalar(S1[:], S2[:], C("even_odd")[:, 0:1], None, ALU.mult)
                dve.drain()
                v.tensor_scalar(S2[:], S2[:], C("even_odd")[:, 1:2], None, ALU.mult)

            def hgrn_heads(st):
                for n in range(HG_HEADS):
                    dve.wait_ge(pe_to_dve, c.add("pe_to_dve"))
                    v.tensor_copy(DEC[:, n % 2], PS[:, 1, S:S + 16]).then_inc(dve_to_act, 1)
                    v.tensor_tensor(HA, PS[:, 1, 0:S].rearrange("p (t q) -> p t q", t=T),
                                    C("block_upto").unsqueeze(1).broadcast_to([P, T, P]), ALU.mult).then_inc(dve_to_pe, 1)
                    dve.wait_ge(kv_full, c.add("kv"))
                    dve.wait_ge(act_to_dve, c.add("act_to_dve"))
                    for b in range(S // HG_BLOCK - 1):
                        m = c.add("state")
                        if m > 4:
                            dve.wait_ge(state_used, m - 4)
                        t, r = b // 8, b % 8
                        kv = PS[:, 2 + r // 2, (2 * t + r % 2) * P:(2 * t + r % 2 + 1) * P]
                        if b == 0:
                            i = v.tensor_copy(STATE[:, m % 4], kv)
                        else:
                            dve.wait_ge(state_ready, m - 1)
                            i = v.scalar_tensor_tensor(out=STATE[:, m % 4], in0=STATE[:, (m - 1) % 4],
                                                       scalar=DEC[:, n % 2, b:b + 1], in1=kv, op0=ALU.mult, op1=ALU.add)
                        i.then_inc(state_ready, 1)
                    dve.wait_ge(state_used, c.of("state"))
                    v.tensor_copy(QKT[:, (st["qk_before"] + n + 1) % 2, 0:S], PS[:, 6, 0:S]).then_inc(dve_to_pe, 1)
                    dve.wait_ge(pe_to_dve, c.add("pe_to_dve"))
                    v.tensor_copy(S3[:, :, n * P:(n + 1) * P],
                                  PS[:, 7, 0:S].rearrange("p (t d) -> p t d", t=T)).then_inc(dve_to_pe, 1)

            def swa_prepare(st):
                for g in range(4):
                    for i in range(2):
                        v.tensor_copy(PR[:, :, 2048 + g * P + i * HD:2048 + g * P + (i + 1) * HD],
                                      PR[:, :, 1024 + g * HD:1024 + (g + 1) * HD])

            def layer_norm(st):
                for t in range(T):
                    for h in range(2):
                        v.bn_stats(BST[:, t, h], X[:, t, h * 512:(h + 1) * 512])
                dve.drain()
                for t in range(T):
                    v.bn_aggr(MV[:, t], BST[:, t])
                dve.drain()
                v.tensor_scalar(STAT[:, 0:T], MV[:, :, 1], LN_EPS - RMS_EPS, None, ALU.add)
                rsqrt(T, 1)
                for t in range(T):
                    v.tensor_scalar(X[:, t], X[:, t], MV[:, t, 0:1], RSTD[:, t:t + 1], ALU.subtract, ALU.mult)
                dve.wait_ge(rows_in, 32 * (st["n"] + 1))
                dve.drain()
                for t in range(T):
                    v.tensor_tensor(X[:, t], X[:, t], S2[:, 0], ALU.mult)
                dve.drain()
                for t in range(T):
                    v.tensor_tensor(X[:, t], X[:, t], S2[:, 1], ALU.add)

            def mlp(st):
                two = st["use"] == "swiglu"
                blocks = st["blocks"]
                def copy_hidden(j):
                    w = blocks[j][1]
                    dve.wait_ge(hid_turned, c.add("hid"))
                    if w > S:
                        v.tensor_copy(HIDT[:, j % 2, 2:4].rearrange("p k s -> p (k s)"),
                                      PS[:, 3 if two else 2 * (j % 2) + 1, :]).then_inc(hid_dve, 1)
                    else:
                        dve.drain().then_inc(hid_dve, 1)

                for j in range(len(blocks)):
                    w = blocks[j][1]
                    if two:
                        sg = SG[:, j % 2, :, 0:w]
                        dve.wait_ge(sig_ready, c.add("sig"))
                        v.tensor_scalar(sg, sg, 1.0, None, ALU.add)
                        dve.drain()
                        v.reciprocal(sg, sg)
                        dve.drain()
                        v.tensor_tensor(sg, sg, PS[:, 0:2, 0:w], ALU.mult).then_inc(gate_read, 1)
                        dve.drain()
                        if j >= 1:
                            copy_hidden(j - 1)
                        dve.wait_ge(up_full, c.add("up"))
                        v.tensor_tensor(HID[:, j % 2, :, 0:w], sg, PS[:, 2:4, 0:w], ALU.mult).then_inc(hidden_ready, 1)
                    else:
                        dve.wait_ge(up_full, c.add("up"))
                        relu = S1[:, :, (j % 2) * NB:(j % 2 + 1) * NB]
                        for t in range(T):
                            v.tensor_scalar(relu[:, t], PS[:, 2 * (j % 2) + t, 0:w], 0.0, None, ALU.max)
                        dve.drain()
                        v.tensor_tensor(HID[:, j % 2], relu, relu, ALU.mult).then_inc(hidden_ready, 1)
                        if j >= 1:
                            copy_hidden(j - 1)
                copy_hidden(len(blocks) - 1)

            def mlp_add(st):
                v.scalar_tensor_tensor(out=X[:].rearrange("p t d -> p (t d)"), in0=X[:].rearrange("p t d -> p (t d)"),
                                       scalar=st["alpha"], in1=PS[:, 4:8].rearrange("p b c -> p (b c)"),
                                       op0=ALU.mult, op1=ALU.add)

            def moe_add(st):
                v.scalar_tensor_tensor(out=X[:], in0=X[:], scalar=ALPHA, in1=MERGED[:], op0=ALU.mult, op1=ALU.add)

            def route(st):
                L = ROUTE[:, :, 0, 0:8]
                v.memset(MERGED[:], 0.0)
                dve.wait_ge(pe_to_dve, c.add("pe_to_dve"))
                v.tensor_copy(L, PS[:, 0, 0:16].rearrange("p (t e) -> p t e", t=T))
                dve.drain()
                v.tensor_reduce(MV[:, :, 0:1], L, AX, ALU.max)
                for t in range(T):
                    sq = lambda x: x.rearrange("p (a b) -> p a b", a=8)
                    other = ROUTE[:, t, 0, 0:8].unsqueeze(1).broadcast_to([P, 8, 8])
                    own = ROUTE[:, t, 0, 0:8].unsqueeze(2).broadcast_to([P, 8, 8])
                    v.tensor_tensor(sq(RT[:, 0, t]), other, own, ALU.is_gt)
                    v.tensor_tensor(sq(RT[:, 1, t]), other, own, ALU.is_equal)
                dve.drain()
                for t in range(T):
                    v.tensor_tensor(RT[:, 1, t], RT[:, 1, t], C("tie_first"), ALU.mult)
                    v.tensor_scalar(ROUTE[:, t, 2, 0:8], ROUTE[:, t, 0, 0:8], MV[:, t, 0:1], None, ALU.subtract)
                dve.drain().then_inc(dve_to_act, 1)
                v.tensor_tensor(RT[:, 0], RT[:, 0], RT[:, 1], ALU.add)
                dve.drain()
                for t in range(T):
                    v.tensor_reduce(RT[:, 1, t, 0:8], RT[:, 0, t].rearrange("p (a b) -> p a b", a=8), AX, ALU.add)
                dve.drain()
                for h in range(2):
                    v.tensor_scalar(ROUTE[:, :, 1, 8 * h:8 * h + 8], RT[:, 1, :, 0:8], 1.5, None, ALU.is_lt)
                dve.drain().then_inc(dve_to_pe, 1)
                dve.wait_ge(act_to_dve, c.add("act_to_dve"))
                v.tensor_tensor(ROUTE[:, :, 2, 0:8], ROUTE[:, :, 2, 0:8], ROUTE[:, :, 1, 0:8], ALU.mult)
                dve.drain()
                v.tensor_reduce(MV[:, :, 0:1], ROUTE[:, :, 2, 0:8], AX, ALU.add)
                dve.drain()
                v.reciprocal(MV[:, :, 1], MV[:, :, 0])
                dve.drain()
                for t in range(T):
                    v.tensor_scalar(ROUTE[:, t, 2, 0:8], ROUTE[:, t, 2, 0:8], MV[:, t, 1:2], None, ALU.mult)
                dve.drain()
                v.tensor_copy(ROUTE[:, :, 2, 8:16], ROUTE[:, :, 2, 0:8])
                dve.wait_ge(pe_to_dve, c.add("pe_to_dve"))
                place = PS[:, 1, 0:16].rearrange("p (t e) -> p t e", t=T)
                v.tensor_copy(ROUTE[:, :, 3, 0:8], place)
                v.tensor_scalar(ROUTE[:, :, 3, 8:16], place, -float(P), None, ALU.add)
                v.tensor_reduce(MV[:, 0, 0:1], PS[:, 1, 16:24], AX, ALU.max)
                dve.drain()
                v.tensor_scalar(NPASS[:, 0:1], MV[:, 0, 0:1], P + 0.5, 1.0, ALU.is_gt, ALU.add)
                dve.drain().then_inc(passes_ready, 1)

            def experts(st):
                J = D_EXP // NB
                passes = dve.value_load(NPASS[0:1, 0:1], min_val=1, max_val=T)
                dve.drain().then_inc(xh_ready, 2)
                dve.drain().then_inc(spread_read, 1)
                with dve.Fori(0, passes * (N_EXPERTS // 2)) as i:
                    for half in range(2):
                        m = i * 2 + half
                        dve.wait_ge(choice_turned, m + 1)
                        for t in range(T):
                            v.tensor_scalar(CHOICE[:, t], C("slots"), ROUTE[:, t, 3, bass.ds(m, 1)],
                                            ROUTE[:, t, 1, bass.ds(m, 1)], ALU.is_equal, ALU.mult)
                        dve.drain()
                        for t in range(T):
                            v.tensor_scalar(CHOICEW[:, t], CHOICE[:, t], ROUTE[:, t, 2, bass.ds(m, 1)], None, ALU.mult)
                        dve.drain().then_inc(choice_ready, 1)
                        for j in range(J):
                            par = (half * J + j) % 2
                            sg = SG2[:, par]
                            dve.wait_ge(xsig_ready, m * J + j + 1)
                            v.tensor_scalar(sg, sg, 1.0, None, ALU.add)
                            dve.drain()
                            v.reciprocal(sg, sg)
                            dve.drain()
                            v.tensor_tensor(sg, sg, PS[:, par], ALU.mult)
                            dve.drain()
                            dve.wait_ge(xu_full, m * J + j + 1)
                            v.tensor_tensor(HID2[:, par], sg, PS[:, 2 + par], ALU.mult).then_inc(xh_ready, 1)
                        for t in range(T):
                            for nb in range(2):
                                s = 2 * t + nb
                                dve.wait_ge(spread_full, m * 4 + s + 1)
                                acc = MERGED[:, t, nb * NB:(nb + 1) * NB]
                                v.tensor_tensor(acc, acc, PS[:, 5], ALU.add).then_inc(spread_read, 1)

            run = dict(setup=setup, rms_in=rms_in, turn=turn, product=product, qk_norm=qk_norm,
                       index_prepare=index_prepare, index_select=index_select, pairs=pairs, a_finish=a_finish,
                       sticks=sticks, ret_rotary=ret_rotary, retention=retention, ret_finish=ret_finish,
                       hgrn_forget=hgrn_forget, hgrn_scale=hgrn_scale, hgrn_heads=hgrn_heads, hgrn_finish=hgrn_finish,
                       swa_prepare=swa_prepare, layer_norm=layer_norm, mlp=mlp, mlp_add=mlp_add, moe_add=moe_add,
                       route=route, experts=experts)
            for n, st in enumerate(stages):
                if st["kind"] in run:
                    run[st["kind"]](st)
                finish_stage(dve, n)

        @block.gpsimd
        def _(pool):
            nc.gpsimd.memset(MHALF[:], -0.5)
            pool.drain()
            with pool.Fori(0, rsqrts[0]) as i:
                pool.wait_ge(sums_ready, i + 1)
                nc.gpsimd.tensor_tensor(RSTD[:], STAT[:], MHALF[:], ALU.pow).then_inc(rsqrt_ready, 1)


_INS = ["x", "p", "positions", "attn_norm", "w_in", "a_q_norm", "a_k_norm", "a_lambda", "a_subln", "c_q_norm",
        "c_k_norm", "idx_k_norm", "w_br_a", "w_br_b", "w_br_c", "w_out", "mlp_norm", "w_up", "w_down", "ple_norm",
        "w_ple_gate", "w_ple_proj", "ln_in_g_2", "ln_in_b_2", "w_in_2", "ret_w_out_2", "hgrn_lower_bounds_2",
        "hgrn_norm_g_2", "hgrn_w_out_2", "swa_sinks_2", "swa_w_out_2", "w_o_2", "ln_mix_g_2", "ln_mix_b_2",
        "ffn_w_gate_2", "ffn_w_up_2", "ffn_w_down_2", "moe_router_2", "moe_w_gate_2", "moe_w_up_2", "moe_w_down_2",
        "ln_ffn_g_2", "ln_ffn_b_2"]


def kernel(**inputs):
    import concourse.bacc as _bacc
    from concourse.bass_utils import run_bass_kernel_spmd as _run

    nc = _bacc.Bacc("TRN2", target_bir_lowering=False, num_devices=1)
    arrays, aps = {}, {}
    constants, const_at = shape_constants()
    for name in _INS + ["shape_constants"]:
        x = np.ascontiguousarray(constants if name == "shape_constants" else inputs[name])
        arrays[f"in_{name}_dram"] = x
        aps[name] = nc.dram_tensor(f"in_{name}_dram", x.shape, mybir.dt.from_np(x.dtype), kind="ExternalInput").ap()
    out = nc.dram_tensor("out_0_dram", (1, S, D), F32, kind="ExternalOutput").ap()
    build(nc, aps, out, const_at)
    r = _run(nc, [arrays], core_ids=[0])
    return r.results[0]["out_0_dram"]
```

```python
import math
from contextlib import ExitStack

import numpy as np

import concourse.bass as bass
from concourse import mybir

F32 = mybir.dt.float32
F32R = mybir.dt.float32r
I32 = mybir.dt.int32
ALU = mybir.AluOpType
ACT = mybir.ActivationFunctionType
AX = mybir.AxisListType.X

P = 128
S = 256
T = S // P
D = 1024
KD = D // P
HD = 64
CH = 64
NB = 512
RAW = 3
SPLIT = 3
KT = 4
TILE = KT * NB
DEPTH = 2
TOPK = 64
IDX_HEADS = 4
HG_BLOCK = 16
HG_HEADS = 8
RET_HEADS = 4
D_FF_2 = 2816
N_EXPERTS = 8
D_EXP = 3584
NEG = -1.0e30
RMS_EPS = 1e-6
LN_EPS = 1e-5
ALPHA = (2.0 * DEPTH) ** 0.25
SCALE = HD ** -0.5
MAGIC = 1.5 * 2.0 ** 23


def shape_constants():
    q, k = np.arange(S), np.arange(S)
    r = np.arange(P)
    parts = {}
    parts["ident"] = np.eye(P)
    chunk_ok = (k[None, :] // CH) <= (q[:, None] // CH)
    window_ok = chunk_ok & ((q[:, None] // CH) - (k[None, :] // CH) <= 2)
    by_tile = lambda m: m.reshape(T, P, -1).transpose(1, 0, 2).reshape(P, -1)
    parts["chunk_mask"] = by_tile(np.where(chunk_ok, 0.0, NEG))
    parts["window_mask"] = np.where(window_ok, 0.0, NEG)[P:]
    dist = np.concatenate([q[None, :] - r[:, None], r[None, :] - r[:, None]], 1)
    parts["strict"] = (dist > 0) * 1.0
    parts["dist"] = np.where(dist >= 0, dist, 1e6)
    parts["later"] = (r[:, None] > r[None, :]) * 1.0
    parts["upto"] = (r[:, None] <= r[None, :]) * 1.0
    parts["ones"] = np.ones((P, P))
    same = (r[:, None] // HG_BLOCK) == (r[None, :] // HG_BLOCK)
    parts["block_upto"] = (same & (r[:, None] <= r[None, :])) * 1.0
    parts["block_later"] = (same & (r[:, None] > r[None, :])) * 1.0
    parts["in_block"] = (r[:, None] // HG_BLOCK == np.arange(P // HG_BLOCK)[None, :]) * 1.0
    parts["even_odd"] = np.stack([(r // HG_BLOCK) % 2 == 0, (r // HG_BLOCK) % 2 == 1], 1) * 1.0
    half = 64
    inv = (1.0 / (np.float32(10000.0) ** np.linspace(0, 1, half, dtype=np.float32))).astype(np.float32)
    ang = (q.astype(np.float32)[:, None] * inv[None, :]).astype(np.float64)
    parts["ret_cos"] = by_tile(np.cos(ang))
    parts["ret_sin"] = by_tile(np.sin(ang))
    inv1 = np.float32(10000.0) ** (-np.arange(0, HD, 2, dtype=np.float32) / HD)
    parts["inv_freq"] = np.broadcast_to(inv1, (P, HD // 2))
    parts["slots"] = np.broadcast_to(r, (P, P))
    e = np.arange(N_EXPERTS)
    parts["tie_first"] = np.broadcast_to((e[None, :] < e[:, None]).reshape(1, -1) * 1.0, (P, 64))
    at, n = {}, 0
    for name, a in parts.items():
        at[name] = (n, a.shape[1])
        n += a.shape[1]
    return np.concatenate([np.asarray(a, np.float32) for a in parts.values()], 1), at


def column_tiles(name, layer, rows, c0, n, role="block", block=None):
    for b, c in enumerate(range(0, n, NB)):
        for r in range(0, rows, KT):
            yield dict(name=name, layer=layer, row=r * P, rows=min(KT, rows - r), col=c0 + c, width=min(NB, n - c),
                       k=r, last=r + KT >= rows, role=role, block=b if block is None else block)


def down_tiles(name, layer, row, rows, j):
    for nb in range(D // NB):
        yield dict(name=name, layer=layer, row=row, rows=rows, col=nb * NB, width=NB, k=0, last=nb == D // NB - 1,
                   first=nb == 0, role="down", block=j, half=nb)


def ffn_tiles(gate, up, down, layer, blocks, late_up):
    for j in range(len(blocks) + 1):
        new = []
        if j < len(blocks):
            c, w = blocks[j]
            if gate:
                yield from column_tiles(gate, layer, KD, c, w, "gate", j)
            new = list(column_tiles(up, layer, KD, c, w, "up", j))
        if not late_up:
            yield from new
        if j >= 1:
            c, w = blocks[j - 1]
            yield from down_tiles(down, layer, c, w // P, j - 1)
        if late_up:
            yield from new


def schedule():
    out = []

    def add(kind, **kw):
        out.append(dict(kind=kind, **kw))

    def product(use, name, layer, c0, n, rows=KD, **kw):
        add("product", use=use, tiles=list(column_tiles(name, layer, rows, c0, n)), **kw)

    add("setup")
    for l in range(DEPTH):
        add("rms_in", gain=("attn_norm", l))
        add("turn", src="S0", dst="HT", chunks=KD, gain=("attn_norm", l))
        product("copy", "w_in", l, 0, 1536, lhs="HT", first=0)
        add("qk_norm", layer=l, gain="a", src="P")
        add("pairs", use="A", layer=l)
        add("a_finish", layer=l)
        product("gate", "w_in", l, 4932, D, lhs="HT")
        add("turn", src="S3", dst="YT", chunks=4, gain=None)
        product("merge", "w_br_a", l, 0, D, rows=4, lhs="YT", first_branch=True)
        product("copy", "w_in", l, 1536, 1536, lhs="HT", first=0)
        add("sticks", layer=l)
        product("gate", "w_in", l, 4932 + D, D, lhs="HT")
        add("turn", src="S3", dst="YT", chunks=4, gain=None)
        product("merge", "w_br_b", l, 0, D, rows=4, lhs="YT", first_branch=False)
        product("copy", "w_in", l, 3072, 1860, lhs="HT", first=0)
        add("qk_norm", layer=l, gain="c", src="P")
        add("index_prepare", layer=l)
        add("pairs", use="I", layer=l)
        add("index_select", layer=l)
        add("pairs", use="C", layer=l)
        product("gate", "w_in", l, 4932 + 2 * D, D, lhs="HT")
        add("turn", src="S3", dst="YT", chunks=4, gain=None)
        product("merge", "w_br_c", l, 0, D, rows=4, lhs="YT", first_branch=False)
        add("turn", src="MERGED", dst="HT", chunks=KD, gain=None)
        product("resid", "w_out", l, 0, D, lhs="HT", alpha=1.0)
        add("rms_in", gain=("mlp_norm", l))
        add("turn", src="S0", dst="HT", chunks=KD, gain=("mlp_norm", l))
        add("mlp", use="relu2", tiles=list(ffn_tiles(None, "w_up", "w_down", l, [(c, NB) for c in range(0, 4 * D, NB)], False)))
        add("mlp_add", alpha=1.0)
        add("rms_in", gain=("ple_norm", l))
        add("turn", src="S0", dst="HT", chunks=KD, gain=("ple_norm", l))
        product("gate", "w_ple_gate", l, 0, D, lhs="HT", ple=l)
        add("turn", src="P", dst="YT", chunks=2, gain=None, width=256)
        product("ple", "w_ple_proj", l, 0, D, rows=2, lhs="YT", **({"load": 0} if l == DEPTH - 1 else {}))
    add("layer_norm", gain=("ln_in_g_2", "ln_in_b_2", None), n=0)
    for l in range(DEPTH):
        add("turn", src="X", dst="HT", chunks=KD, gain=None)
        product("copy", "w_in_2", l, 0, 3072, lhs="HT", first=0)
        add("ret_rotary", layer=l)
        add("retention")
        add("ret_finish")
        product("gate", "w_in_2", l, 8704, D, lhs="HT")
        add("turn", src="S3", dst="YT", chunks=KD, gain=None)
        product("merge", "ret_w_out_2", l, 0, D, lhs="YT", first_branch=True)
        product("copy", "w_in_2", l, 3072, 4096, lhs="HT", first=0)
        add("hgrn_forget", layer=l)
        add("hgrn_decay")
        add("hgrn_scale")
        add("hgrn_heads")
        add("hgrn_finish", layer=l)
        product("gate", "w_in_2", l, 8704 + D, D, lhs="HT")
        add("turn", src="S3", dst="YT", chunks=KD, gain=None)
        product("merge", "hgrn_w_out_2", l, 0, D, lhs="YT", first_branch=False)
        product("copy", "w_in_2", l, 7168, 1536, lhs="HT", first=0)
        add("swa_prepare", load=2 * l + 1)
        add("pairs", use="W", layer=l)
        product("gate", "w_in_2", l, 8704 + 2 * D, D, lhs="HT")
        add("turn", src="S3", dst="YT", chunks=KD, gain=None)
        product("merge", "swa_w_out_2", l, 0, D, lhs="YT", first_branch=False)
        add("turn", src="MERGED", dst="HT", chunks=KD, gain=None)
        product("resid", "w_o_2", l, 0, D, lhs="HT", alpha=ALPHA)
        add("layer_norm", gain=("ln_mix_g_2", "ln_mix_b_2", l), n=2 * l + 1)
        add("turn", src="X", dst="HT", chunks=KD, gain=None, load=2 * l + 2)
        if l % 2 == 0:
            add("mlp", use="swiglu", tiles=list(ffn_tiles(
                "ffn_w_gate_2", "ffn_w_up_2", "ffn_w_down_2", l // 2,
                [(c, min(NB, D_FF_2 - c)) for c in range(0, D_FF_2, NB)], True)))
            add("mlp_add", alpha=ALPHA)
        else:
            add("route", layer=l // 2)
            add("experts", layer=l // 2, tiles=list(ffn_tiles(
                "moe_w_gate_2", "moe_w_up_2", "moe_w_down_2", l // 2, [(c, NB) for c in range(0, D_EXP, NB)], False)))
            add("moe_add")
        add("layer_norm", gain=("ln_ffn_g_2", "ln_ffn_b_2", l), n=2 * l + 2)
    return out


LN_ROWS = [("ln_in_g_2", "ln_in_b_2", None), ("ln_mix_g_2", "ln_mix_b_2", 0), ("ln_ffn_g_2", "ln_ffn_b_2", 0),
           ("ln_mix_g_2", "ln_mix_b_2", 1), ("ln_ffn_g_2", "ln_ffn_b_2", 1)]


def build(nc, a, out, const_at):
    stages = schedule()
    with ExitStack() as ctx:
        def sb(name, shape, dt=F32):
            return ctx.enter_context(nc.sbuf_tensor(name, [P] + shape, dt))

        def sem(name):
            return ctx.enter_context(nc.semaphore(name))

        raw = sb("weights_raw", [RAW, TILE])
        WH = sb("weights_high", [SPLIT, TILE], F32R)
        WL = sb("weights_low", [SPLIT, TILE], F32R)
        X = sb("x_residual", [T, D])
        HT = [sb(f"h_transposed_{part}", [KD, S], F32R) for part in ("high", "low")]
        YT = [sb(f"y_transposed_{part}", [KD, S], F32R) for part in ("high", "low")]
        RTR = [sb(f"router_{part}", [KD, N_EXPERTS], F32R) for part in ("high", "low")]
        PR = sb("projected", [T, 4096])
        MERGED = sb("merged", [T, D])
        S0 = sb("scratch0", [T, D])
        S1 = sb("scratch1", [T, D])
        S2 = sb("scratch2", [T, D])
        S3 = sb("scratch3", [T, D])
        QKT = sb("qk_transposed", [2, NB])
        PT = sb("weights_transposed", [2, 384])
        n_const = sum(w for _, w in const_at.values())
        CONST = sb("constants", [n_const])
        STAT = sb("mean_squares", [32])
        RSTD = sb("rsqrt", [32])
        MHALF = sb("minus_half", [32])
        COS = sb("rope_cos", [T, 32])
        SIN = sb("rope_sin", [T, 32])
        GAINS = sb("gain_columns", [6, KD])
        HG = sb("head_gains", [DEPTH, 5, HD])
        SUBLN = sb("subln_gain", [DEPTH, P])
        HGN = SUBLN
        LAM = sb("minus_lambda", [DEPTH, 4])
        SINK = sb("sinks", [DEPTH, 16])
        MX = sb("row_max", [2, 4])
        NMX = sb("minus_row_max", [2, 4])
        SINKD = sb("sink_minus_max", [2, 4])
        SUM = sb("row_sum", [2, 4])
        RS = sb("row_scale", [2, 4])
        MV = sb("mean_var", [T, 2])
        BST = sb("bn_stats", [T, 2, 6])
        POSI = sb("positions_int", [T], I32)
        DEC = sb("block_decay", [2, 16])
        LAME = sb("lambda_exp", [DEPTH, 2])
        EDS = sb("sink_exp", [2, 4])
        TOP = sb("top_values", [T, 8])
        NEED = sb("ties_needed", [T, 2])
        NPASS = sb("passes", [2], I32)
        PS = ctx.enter_context(nc.psum_tensor("banks", [P, 8, NB], F32))
        buf = dict(X=X, HT=HT, YT=YT, P=PR, MERGED=MERGED, S0=S0, S1=S1, S2=S2, S3=S3)

        def C(name):
            n, w = const_at[name]
            return CONST[:, n:n + w]

        SM = S0.rearrange("p t d -> p (t d)").rearrange("p (b i k) -> p b i k", b=2, i=4)
        PRf = PR.rearrange("p t d -> p (t d)")
        S0f, S1f, S2f = (b.rearrange("p t d -> p (t d)") for b in (S0, S1, S2))
        IDXM = PR[:, :, 2304:2560]
        SQ = sb("square_sums", [T])
        ROUTE = PRf[:, 6464:6592].rearrange("p (t i e) -> p t i e", t=T, i=4)
        ROUTER = PRf[:, 6400:6464].rearrange("p (k e) -> p k e", k=KD)
        RT = PRf[:, 6144:6400].rearrange("p (i t e) -> p i t e", i=2, t=T)
        STATE = PT.rearrange("p a b -> p (a b)")[:, 0:512].rearrange("p (s v) -> p s v", s=4)
        HA = PT.rearrange("p a b -> p (a b)")[:, 512:768].rearrange("p (t q) -> p t q", t=T)
        LAMB = PR[:, 0, 0:DEPTH * 4 * HD].rearrange("p (l i d) -> p l i d", l=DEPTH, i=4)
        HID = PRf[:, 0:2048].rearrange("p (b t c) -> p b t c", b=2, t=T)
        SG = PRf[:, 2048:4096].rearrange("p (b t c) -> p b t c", b=2, t=T)
        HIDT = [y.rearrange("p (b k) s -> p b k s", b=2) for y in YT]
        HID2 = PRf[:, 0:1024].rearrange("p (b c) -> p b c", b=2)
        HIDT2 = [y.rearrange("p k s -> p (k s)")[:, 0:1024].rearrange("p (b k s) -> p b k s", b=2, k=4) for y in YT]
        SG2 = PRf[:, 2048:3072].rearrange("p (b c) -> p b c", b=2)
        XG = [h.rearrange("p k s -> p (k s)")[:, 0:1024].rearrange("p (k s) -> p k s", k=KD) for h in HT]
        YE = PRf[:, 4096:5120].rearrange("p (b c) -> p b c", b=2)
        CHOICE = PRf[:, 5120:5376].rearrange("p (t s) -> p t s", t=T)
        CHOICEW = PRf[:, 5376:5632].rearrange("p (t s) -> p t s", t=T)
        CHOICET = PRf[:, 5632:5888].rearrange("p (t s) -> p t s", t=T)

        stage_done = sem("stage_done")
        landed = [sem(f"tile_landed{i}") for i in range(RAW)]
        high_ready = sem("weights_high_ready")
        low_ready = sem("weights_low_ready")
        tile_used = sem("tile_used")
        x_high = sem("transposed_high_ready")
        const_in = sem("constants_loaded")
        rows_in = sem("ln_rows_loaded")
        ple_in = sem("ple_loaded")
        router_in = sem("router_loaded")
        hgn_in = sem("hgrn_gains_loaded")
        lb_in = sem("lower_bounds_loaded")
        sums_ready = sem("sums_ready")
        rsqrt_ready = sem("rsqrt_ready")
        squares = sem("squares_summed")
        act_evac = sem("product_read_by_scalar")
        dve_evac = sem("product_read_by_vector")
        turned = sem("bank_turned")
        qk_turned = sem("qk_turned")
        qk_copied = sem("qk_copied")
        scores_full = sem("scores_full")
        scores_read = sem("scores_read")
        max_ready = sem("max_ready")
        probs_ready = sem("probs_ready")
        probs_turned = sem("probs_turned")
        probs_act = sem("probs_read_by_scalar")
        probs_dve = sem("probs_read_by_vector")
        values_full = sem("values_full")
        values_read = sem("values_read")
        dve_to_act = sem("vector_to_scalar")
        act_to_dve = sem("scalar_to_vector")
        dve_to_pe = sem("vector_to_tensor")
        pe_to_dve = sem("tensor_to_vector")
        stick_scores = sem("stick_scores_full")
        kv_full = sem("kv_full")
        state_ready = sem("state_ready")
        state_used = sem("state_used")
        xh_ready = sem("expert_hidden_ready")
        xh_turned = sem("expert_hidden_turned")
        xh_copied = sem("expert_hidden_copied")
        silu_ready = sem("silu_ready")
        xsilu_ready = sem("expert_silu_ready")
        hid_high = sem("hidden_high_ready")
        hid_low = sem("hidden_low_ready")
        xh_high = sem("expert_hidden_high_ready")
        hidden_ready = sem("hidden_ready")
        hid_turned = sem("hidden_turned")
        down_read = sem("down_read")
        gathered = sem("gathered")
        gathered_high = sem("gathered_high_ready")
        gathered_read = sem("gathered_low_ready")
        choice_ready = sem("choice_ready")
        choice_turned = sem("choice_turned")
        choice_copied = sem("choice_copied")
        spread_full = sem("spread_full")
        spread_read = sem("spread_read")
        passes_ready = sem("passes_ready")
        out_sem = sem("out_written")

        class Count:

            def __init__(self):
                self.n = {}

            def of(self, name):
                return self.n.get(name, 0)

            def add(self, name, k=1):
                self.n[name] = self.n.get(name, 0) + k
                return self.n[name]

        def finish_stage(eng, n):
            eng.drain().then_inc(stage_done, 1)
            eng.wait_ge(stage_done, 3 * (n + 1))

        def heads(ap, g, d):
            return ap.rearrange("p (g d) -> p g d", g=g, d=d)

        def pair_cols(use, n):
            if use == "A":
                return n * P, 512 + n * P, [1024 + n * P] * 2, P
            if use == "C":
                return n * P, 512 + n * P, [1024 + n * P, 1024 + n * P + HD], HD
            if use == "W":
                g = n // 2
                return n * P, 2048 + g * P, [1280 + g * HD] * 2, HD
            return 1536 + n * P, 2048, None, 0

        N_PAIRS = dict(A=4, C=4, W=8, I=2)

        N_LOADS = 25

        def gain_col(gain, k):
            name, l = gain
            return GAINS[:, ("attn_norm", "mlp_norm", "ple_norm").index(name) * DEPTH + l, k:k + 1]

        J = D_EXP // NB
        h = 0
        for st in stages:
            st["h0"] = h
            if st["kind"] != "experts":
                h += len(st.get("tiles", []))
        STATIC = h
        PAIR = 2 * (3 * J * 2)
        assert PAIR % RAW == 0 and PAIR % SPLIT == 0

        def tile_view(buffer, slot, tile):
            return buffer[:, slot, 0:tile["rows"] * tile["width"]].rearrange("p (k c) -> p k c", k=tile["rows"])

        def silus_before(stage):
            return sum(st["tiles"][-1]["block"] + 1 for st in stages if st["kind"] == "mlp" and st["h0"] < stage["h0"])

        static_tiles = [tile for st in stages if st["kind"] != "experts" for tile in st.get("tiles", [])]

        seen = 0
        for st in stages:
            st["qk_before"] = seen
            seen += {"pairs": N_PAIRS.get(st.get("use"), 0), "sticks": 4, "retention": RET_HEADS,
                     "hgrn_heads": HG_HEADS}.get(st["kind"], 0)

        block = ctx.enter_context(nc.Block())

        @block.sync
        def _(sp):
            for h, tile in enumerate(static_tiles):
                if h >= RAW:
                    sp.wait_ge(low_ready, h - RAW + 1)
                src = a[tile["name"]][tile["layer"], tile["row"]:tile["row"] + tile["rows"] * P,
                                      tile["col"]:tile["col"] + tile["width"]].rearrange("(k p) c -> p k c", p=P)
                sp.dma_start(tile_view(raw, h % RAW, tile), src).then_inc(landed[h % RAW], 16)
            for st in stages:
                if st["kind"] == "experts":
                    sp.wait_ge(passes_ready, 1)
                    passes = sp.value_load(NPASS[0:1, 0:1], min_val=1, max_val=T)
                    with sp.Fori(0, passes * (N_EXPERTS // 2)) as i:
                        for half in range(2):
                            expert = i % (N_EXPERTS // 2) * 2 + half
                            for n, tile in enumerate(st["tiles"]):
                                h = STATIC + half * (PAIR // 2) + n
                                src = a[tile["name"]][tile["layer"], bass.ds(expert, 1),
                                                      tile["row"]:tile["row"] + tile["rows"] * P,
                                                      tile["col"]:tile["col"] + tile["width"]].rearrange(
                                    "e (k p) c -> p (e k) c", p=P)
                                sp.wait_ge(low_ready, i * PAIR + h - RAW + 1)
                                sp.dma_start(tile_view(raw, h % RAW, tile), src).then_inc(landed[h % RAW], 16)
            sp.wait_ge(stage_done, 3 * len(stages))
            sp.dma_start(out[0].rearrange("(t p) d -> p t d", p=P), X[:]).then_inc(out_sem, 16)
            sp.wait_ge(out_sem, 16)

        @block.tensor
        def _(pe):
            c = Count()
            ident = C("ident")
            history = []

            def tile_products(h, tile, out_of, lhs, first, last, done=0):
                pe.wait_ge(low_ready, h + 1 + done)
                high, low = tile_view(WH, h % SPLIT, tile), tile_view(WL, h % SPLIT, tile)
                for k in range(tile["rows"]):
                    begin, end = first and k == 0, last and k == tile["rows"] - 1
                    for t in range(len(out_of)):
                        nc.tensor.matmul(out_of[t], lhs(0, k, t), high[:, k], start=begin, stop=False)
                        nc.tensor.matmul(out_of[t], lhs(0, k, t), low[:, k], start=False, stop=False)
                        mm = nc.tensor.matmul(out_of[t], lhs(1, k, t), high[:, k], start=False, stop=end)
                mm.then_inc(tile_used, 1)

            def product(st):
                x = buf[st["lhs"]]
                for n, tile in enumerate(st["tiles"]):
                    if tile["k"] == 0:
                        g = len(history)
                        if g >= 2:
                            na = sum(h[0] for h in history[:g - 1])
                            nd = sum(h[1] for h in history[:g - 1])
                            if na:
                                pe.wait_ge(act_evac, na)
                            if nd:
                                pe.wait_ge(dve_evac, nd)
                        history.append({"copy": (1, 1), "gate": (1, 0)}.get(st["use"], (0, 1)))
                    tile_products(st["h0"] + n, tile, [PS[:, 2 * (g % 2) + t, 0:tile["width"]] for t in range(T)],
                                  lambda part, k, t: x[part][:, tile["k"] + k, t * P:(t + 1) * P],
                                  tile["k"] == 0, tile["last"])

            def turn(st):
                src = buf[st["src"]]
                for b in range((st["chunks"] + 1) // 2):
                    for k in (2 * b, 2 * b + 1):
                        for t in range(T):
                            tr = nc.tensor.transpose(PS[:, 4 + b, (k % 2) * S + t * P:(k % 2) * S + (t + 1) * P],
                                                     src[:, t, k * P:(k + 1) * P], ident)
                    tr.then_inc(turned, 1)

            def turn_qk(q0, k0):
                n = c.of("qk")
                if n:
                    pe.wait_ge(qk_copied, n)
                for i, (col, t) in enumerate([(q0, 0), (q0, 1), (k0, 0), (k0, 1)]):
                    tr = nc.tensor.transpose(PS[:, 0, i * P:(i + 1) * P], PR[:, t, col:col + P], ident)
                tr.then_inc(qk_turned, 1)
                c.add("qk")
                pe.wait_ge(qk_copied, n + 1)
                return QKT[:, n % 2]

            def pairs(st):
                use = st["use"]
                N = N_PAIRS[use]

                def front(n):
                    q0, k0, _, _ = pair_cols(use, n)
                    z = turn_qk(q0, k0)
                    m = c.add("scores")
                    if m > 2:
                        pe.wait_ge(scores_read, m - 2)
                    for t in range(T):
                        for h in range(2):
                            rows = slice(h * HD, (h + 1) * HD)
                            mm = nc.tensor.matmul(PS[:, 1 + 2 * (m % 2) + h, t * S:(t + 1) * S],
                                                  z[rows, t * P:(t + 1) * P], z[rows, S:2 * S], start=True, stop=True)
                    mm.then_inc(scores_full, 1)

                def back(n):
                    m = c.add("probs")
                    _, _, v0, vw = pair_cols(use, n)
                    pe.wait_ge(probs_ready, m)
                    if m > 1:
                        pe.wait_ge(probs_act, m - 1)
                        pe.wait_ge(probs_dve, m - 1)
                    for h in range(2):
                        for kt, t in ((0, 0), (0, 1), (1, 1)):
                            tr = nc.tensor.transpose(PS[:, 5 + h, (kt + t) * P:(kt + t + 1) * P],
                                                     SM[:, m % 2, 2 * t + h, kt * P:(kt + 1) * P], ident)
                    tr.then_inc(probs_turned, 1)
                    pe.wait_ge(probs_act, m)
                    pe.wait_ge(probs_dve, m)
                    if m > 1:
                        pe.wait_ge(values_read, m - 1)
                    for t in range(T):
                        for h in range(2):
                            for kt in range(t + 1):
                                o = (2 * t + h) * vw
                                mm = nc.tensor.matmul(PS[:, 7, o:o + vw], PT[:, h, (kt + t) * P:(kt + t + 1) * P],
                                                      PR[:, kt, v0[h]:v0[h] + vw], start=kt == 0, stop=kt == t)
                    mm.then_inc(values_full, 1)

                for n in range(N + 1):
                    if n < N:
                        front(n)
                    if n >= 1 and use != "I":
                        back(n - 1)

            def sticks(st):
                for n in range(4):
                    z = turn_qk(n * P, 512 + n * P)
                    for h in range(2):
                        rows = slice(h * HD, (h + 1) * HD)
                        nc.tensor.matmul(PS[:, 1 + h, 0:S], z[rows, S:S + P], z[rows, 0:S], start=True, stop=True)
                        mm = nc.tensor.matmul(PS[:, 1 + h, S:S + P], z[rows, S + P:2 * S], z[rows, P:S],
                                              start=True, stop=True)
                    mm.then_inc(stick_scores, 1)
                    pe.wait_ge(dve_to_pe, c.add("dve_to_pe"))
                    for h in range(2):
                        lg = S1.rearrange("p t d -> p (t d)")[:, h * 384:(h + 1) * 384]
                        nc.tensor.matmul(PS[:, 5 + h, 0:P], C("later"), lg[:, 0:P], start=True, stop=True)
                        nc.tensor.matmul(PS[:, 5 + h, P:S], C("later"), lg[:, P:S], start=True, stop=False)
                        nc.tensor.matmul(PS[:, 5 + h, P:S], C("ones"), lg[:, S:S + P], start=False, stop=True)
                        mm = nc.tensor.matmul(PS[:, 5 + h, S:S + P], C("later"), lg[:, S:S + P], start=True, stop=True)
                    mm.then_inc(pe_to_dve, 1)
                    pe.wait_ge(dve_to_pe, c.add("dve_to_pe"))
                    for t in range(T):
                        for h in range(2):
                            for kt in range(t + 1):
                                o = (2 * t + h) * HD
                                v0 = 1024 + n * P + h * HD
                                mm = nc.tensor.matmul(PS[:, 7, o:o + HD],
                                                      S0.rearrange("p t d -> p (t d)")[:, h * 384 + (kt + t) * P:h * 384 + (kt + t + 1) * P],
                                                      PR[:, kt, v0:v0 + HD], start=kt == 0, stop=kt == t)
                    mm.then_inc(pe_to_dve, 1)
                    pe.wait_ge(dve_to_pe, c.add("dve_to_pe"))

            def retention(st):
                for n in range(RET_HEADS):
                    z = turn_qk(n * P, 512 + n * P)
                    nc.tensor.matmul(PS[:, 1, 0:S], z[:, S:S + P], z[:, 0:S], start=True, stop=True)
                    nc.tensor.matmul(PS[:, 1, S:S + P], z[:, S + P:2 * S], z[:, P:S], start=True,
                                     stop=True).then_inc(pe_to_dve, 1)
                    pe.wait_ge(dve_to_pe, c.add("dve_to_pe"))
                    for t in range(T):
                        for kt in range(t + 1):
                            mm = nc.tensor.matmul(PS[:, 7, t * S:(t + 1) * S], PT[:, n % 2, (kt + t) * P:(kt + t + 1) * P],
                                                  PR[:, kt, 1024 + n * S:1024 + (n + 1) * S], start=kt == 0, stop=kt == t)
                    mm.then_inc(pe_to_dve, 1)
                    pe.wait_ge(dve_to_pe, c.add("dve_to_pe"))

            def hgrn_decay(st):
                for t in range(T):
                    for nb in range(2):
                        nc.tensor.matmul(PS[:, 2 * t + nb, :], C("block_upto"), S0[:, t, nb * NB:(nb + 1) * NB],
                                         start=True, stop=True)
                        nc.tensor.matmul(PS[:, 4 + 2 * t + nb, :], C("block_later"), S0[:, t, nb * NB:(nb + 1) * NB],
                                         start=True, stop=True)

            def hgrn_heads(st):
                per_tile = P // HG_BLOCK
                for n in range(HG_HEADS):
                    cols = slice(n * P, (n + 1) * P)
                    if n:
                        pe.wait_ge(dve_to_pe, c.of("dve_to_pe"))
                    z = turn_qk(n * P, 1024 + n * P)
                    for t in range(T):
                        nc.tensor.matmul(PS[:, 1, t * P:(t + 1) * P], z[:, S + t * P:S + (t + 1) * P],
                                         z[:, t * P:(t + 1) * P], start=True, stop=True)
                    for t in range(T):
                        mm = nc.tensor.matmul(PS[:, 1, S + t * per_tile:S + (t + 1) * per_tile], S0[:, t, cols],
                                              C("in_block"), start=True, stop=True)
                    mm.then_inc(pe_to_dve, 1)
                    for b in range(2 * per_tile - 1):
                        t, r = b // per_tile, b % per_tile
                        rows = slice(32 * (r // 2), 32 * (r // 2) + 32)
                        kst = (S1, S2)[r % 2]
                        u = 2 * t + r % 2
                        mm = nc.tensor.matmul(PS[:, 2 + r // 2, u * P:(u + 1) * P], kst[rows, t, cols],
                                              PR[rows, t, 2048 + n * P:2048 + (n + 1) * P], start=True, stop=True,
                                              tile_position=(rows.start, 0))
                    mm.then_inc(kv_full, 1)
                    pe.wait_ge(dve_to_pe, c.add("dve_to_pe"))
                    for b in range(2 * per_tile):
                        t, r = b // per_tile, b % per_tile
                        if r == 0:
                            nc.tensor.matmul(PS[:, 6, t * P:(t + 1) * P], PR[:, t, 2048 + n * P:2048 + (n + 1) * P],
                                             HA[:, t, :], start=True, stop=b == 0, skip_group_check=True)
                        if b >= 1:
                            m = c.add("state")
                            pe.wait_ge(state_ready, m)
                            mm = nc.tensor.matmul(PS[:, 6, b * HG_BLOCK:(b + 1) * HG_BLOCK], STATE[:, m % 4],
                                                  z[:, b * HG_BLOCK:(b + 1) * HG_BLOCK], start=False,
                                                  stop=True, skip_group_check=True)
                            mm.then_inc(state_used, 1)
                    pe.wait_ge(dve_to_pe, c.add("dve_to_pe"))
                    ho = QKT[:, c.of("qk") % 2, 0:S]
                    for t in range(T):
                        tr = nc.tensor.transpose(PS[:, 7, t * P:(t + 1) * P], ho[:, t * P:(t + 1) * P], ident)
                    tr.then_inc(pe_to_dve, 1)
                    c.add("dve_to_pe")

            def index_select(st):
                pe.wait_ge(dve_to_pe, c.add("dve_to_pe"))
                for t in range(T):
                    for kt in range(T):
                        tr = nc.tensor.transpose(PS[:, 4 + t, kt * P:(kt + 1) * P], S1[:, t, kt * P:(kt + 1) * P], ident)
                tr.then_inc(pe_to_dve, 1)
                pe.wait_ge(dve_to_pe, c.add("dve_to_pe"))
                n0, _ = const_at["upto"]
                for t in range(T):
                    e = lambda kt: S1[:, t, 512 + kt * P:512 + (kt + 1) * P]
                    nc.tensor.matmul(PS[:, 6, t * S:(t + 1) * S], e(0), CONST[:, n0:n0 + S], start=True, stop=False)
                    mm = nc.tensor.matmul(PS[:, 6, t * S + P:(t + 1) * S], e(1), C("upto"), start=False, stop=True)
                mm.then_inc(pe_to_dve, 1)

            def mlp(st):
                two = st["use"] == "swiglu"
                tiles = st["tiles"]
                n_blocks = tiles[-1]["block"] + 1
                for n, tile in enumerate(tiles):
                    j, w = tile["block"], tile["width"]
                    bank = 0 if tile["role"] == "gate" else (2 if two else 2 * (j % 2))
                    if tile["role"] != "down":
                        if tile["k"] == 0:
                            if tile["role"] == "gate":
                                if j >= 1:
                                    pe.wait_ge(silu_ready, silus_before(st) + j)
                            elif j >= (1 if two else 2):
                                pe.wait_ge(hid_low, c.of("hid"))
                        tile_products(st["h0"] + n, tile, [PS[:, bank + t, 0:w] for t in range(T)],
                                      lambda part, k, t: HT[part][:, tile["k"] + k, t * P:(t + 1) * P],
                                      tile["k"] == 0, tile["last"])
                        continue
                    if tile["first"]:
                        pe.wait_ge(hidden_ready, c.add("hidden"))
                        for i in range(tile["rows"]):
                            for t in range(T):
                                at = (i % 2) * S + t * P
                                tr = nc.tensor.transpose(PS[:, bank + i // 2, at:at + P],
                                                         HID[:, j % 2, t, i * P:(i + 1) * P], ident)
                        tr.then_inc(hid_turned, 1)
                        pe.wait_ge(hid_low, c.add("hid"))
                    tile_products(st["h0"] + n, tile, [PS[:, 4 + 2 * t + tile["half"], :] for t in range(T)],
                                  lambda part, k, t: HIDT[part][:, j % 2, k, t * P:(t + 1) * P],
                                  j == 0, j == n_blocks - 1)

            def route(st):
                pe.wait_ge(dve_to_pe, c.add("dve_to_pe"))
                for t in range(T):
                    for k in range(KD):
                        for n, (xp, wp) in enumerate(((0, 0), (0, 1), (1, 0))):
                            mm = nc.tensor.matmul(PS[:, 0, t * 8:(t + 1) * 8], HT[xp][:, k, t * P:(t + 1) * P],
                                                  RTR[wp][:, k, :], start=k == 0 and n == 0, stop=k == KD - 1 and n == 2)
                mm.then_inc(pe_to_dve, 1)
                pe.wait_ge(dve_to_pe, c.add("dve_to_pe"))
                nc.tensor.matmul(PS[:, 1, 0:8], C("strict")[:, 0:P], ROUTE[:, 0, 1, 0:8], start=True, stop=True)
                nc.tensor.matmul(PS[:, 1, 8:16], C("ones"), ROUTE[:, 0, 1, 0:8], start=True, stop=False)
                nc.tensor.matmul(PS[:, 1, 8:16], C("strict")[:, 0:P], ROUTE[:, 1, 1, 0:8], start=False, stop=True)
                nc.tensor.matmul(PS[:, 1, 16:24], C("ones"), ROUTE[:, 0, 1, 0:8], start=True, stop=False)
                nc.tensor.matmul(PS[:, 1, 16:24], C("ones"), ROUTE[:, 1, 1, 0:8], start=False,
                                 stop=True).then_inc(pe_to_dve, 1)

            def experts(st):
                pe.wait_ge(passes_ready, 1)
                passes = pe.value_load(NPASS[0:1, 0:1], min_val=1, max_val=T)
                pe.drain().then_inc(choice_turned, 1)
                with pe.Fori(0, passes * (N_EXPERTS // 2)) as i:
                    for half in range(2):
                        m = i * 2 + half
                        pe.wait_ge(choice_ready, m + 1)
                        for kk in range(2):
                            if kk:
                                pe.wait_ge(gathered_read, m * 2 + 1)
                            for k in range(4):
                                f = kk * 4 + k
                                for t in range(T):
                                    mm = nc.tensor.matmul(PS[:, 4, k * P:(k + 1) * P], X[:, t, f * P:(f + 1) * P],
                                                          CHOICE[:, t, :], start=t == 0, stop=t == T - 1)
                            mm.then_inc(gathered, 1)
                        pe.wait_ge(gathered_read, m * 2 + 2)
                        for t in range(T):
                            tr = nc.tensor.transpose(PS[:, 4, t * P:(t + 1) * P], CHOICEW[:, t, :], ident)
                        tr.then_inc(choice_turned, 1)
                        pe.wait_ge(choice_copied, m + 1)
                        for n, tile in enumerate(st["tiles"]):
                            h = STATIC + half * (PAIR // 2) + n
                            j = tile["block"]
                            par = (half * J + j) % 2
                            if tile["role"] != "down":
                                if tile["k"] == 0:
                                    pe.wait_ge(xh_ready, m * J + j + 1)
                                bank = par if tile["role"] == "gate" else 2 + par
                                tile_products(h, tile, [PS[:, bank, :]], lambda part, k, t: XG[part][:, tile["k"] + k, :],
                                              tile["k"] == 0, tile["last"], i * PAIR)
                                continue
                            if tile["first"]:
                                pe.wait_ge(xh_ready, m * J + j + 3)
                                for x in range(4):
                                    tr = nc.tensor.transpose(PS[:, 4, x * P:(x + 1) * P], HID2[:, par, x * P:(x + 1) * P], ident)
                                tr.then_inc(xh_turned, 1)
                                pe.wait_ge(xh_copied, m * J + j + 1)
                            tile_products(h, tile, [PS[:, 6 + tile["half"], :]],
                                          lambda part, k, t: HIDT2[part][:, par, k, :], j == 0, j == J - 1, i * PAIR)
                        pe.wait_ge(down_read, m + 1)
                        for t in range(T):
                            for nb in range(2):
                                s = 2 * t + nb
                                pe.wait_ge(spread_read, m * 4 + s + 1)
                                nc.tensor.matmul(PS[:, 5, :], CHOICET[:, t, :], YE[:, nb, :], start=True,
                                                 stop=True).then_inc(spread_full, 1)

            run = dict(product=product, turn=turn, pairs=pairs, sticks=sticks, retention=retention,
                       hgrn_decay=hgrn_decay, hgrn_heads=hgrn_heads, index_select=index_select, mlp=mlp,
                       route=route, experts=experts)
            for n, st in enumerate(stages):
                if st["kind"] in run:
                    run[st["kind"]](st)
                finish_stage(pe, n)

        @block.scalar
        def _(act):
            c = Count()
            split = [0]

            def high_part(h, tile, done=0):
                act.wait_ge(landed[h % RAW], (h // RAW + 1 + (done and done[0])) * 16)
                if h >= SPLIT:
                    act.wait_ge(tile_used, h - SPLIT + 1 + (done and done[1]))
                nc.scalar.activation(tile_view(WH, h % SPLIT, tile), tile_view(raw, h % RAW, tile),
                                     ACT.Copy).then_inc(high_ready, 1)

            def split_to(n):
                while split[0] < min(n, STATIC):
                    high_part(split[0], static_tiles[split[0]])
                    split[0] += 1

            def load_rows(n):
                g, b, l = LN_ROWS[n]
                for i, name in enumerate((g, b)):
                    row = a[name].rearrange("(o d) -> o d", o=1) if l is None else a[name][l:l + 1, :]
                    act.dma_start(S2[:, i], row[0].partition_broadcast(P)).then_inc(rows_in, 16)

            def setup(st):
                k = 0
                loads = [(CONST[:], a["shape_constants"])]
                for i, (name, l) in enumerate([(m, l) for m in ("attn_norm", "mlp_norm", "ple_norm") for l in range(DEPTH)]):
                    loads.append((GAINS[:, i], a[name][l].rearrange("(k p) -> p k", p=P)))
                for i, name in enumerate(("a_q_norm", "a_k_norm", "c_q_norm", "c_k_norm", "idx_k_norm")):
                    for l in range(DEPTH):
                        loads.append((HG[:, l, i], a[name][l].partition_broadcast(P)))
                for l in range(DEPTH):
                    loads.append((SUBLN[:, l], a["a_subln"][l].partition_broadcast(P)))
                    loads.append((SINK[:, l], a["swa_sinks_2"][l].partition_broadcast(P)))
                    loads.append((LAMB[:, l], a["a_lambda"][l].rearrange("i d -> (i d)").partition_broadcast(P)
                                  .rearrange("p (i d) -> p i d", i=4)))
                loads.append((POSI[:], a["positions"][0].rearrange("(t p) -> p t", p=P)))
                loads.append((X[:], a["x"][0].rearrange("(t p) d -> p t d", p=P)))
                for dst, src in loads:
                    act.dma_start(dst, src, allow_slow_non_contiguous=True).then_inc(const_in, 16)
                assert len(loads) == N_LOADS, len(loads)
                act.wait_ge(dve_to_act, c.add("dve_to_act"))
                nc.scalar.activation(COS.rearrange("p t f -> p (t f)"), COS.rearrange("p t f -> p (t f)"), ACT.Sin)
                nc.scalar.activation(SIN.rearrange("p t f -> p (t f)"), SIN.rearrange("p t f -> p (t f)"), ACT.Sin)
                nc.scalar.activation(LAME.rearrange("p l i -> p (l i)"), LAME.rearrange("p l i -> p (l i)"),
                                     ACT.Exp).then_inc(act_to_dve, 1)

            def layer_norm(st):
                if st["n"] == 2 * DEPTH - 1:
                    act.dma_start(ROUTER, a["moe_router_2"][0].rearrange("(k p) e -> p k e", p=P)).then_inc(router_in, 16)

            def ret_rotary(st):
                if st["layer"] == 0:
                    for l in range(DEPTH):
                        act.dma_start(HGN[:, l], a["hgrn_norm_g_2"][l].partition_broadcast(P)).then_inc(hgn_in, 16)

            def rms_in(st):
                for t in range(T):
                    i = nc.scalar.activation(S1[:, t], X[:, t], ACT.Square, accum_out=SQ[:, t:t + 1])
                act.drain().then_inc(squares, 1)

            def turn(st):
                dst = buf[st["dst"]][0]
                if "load" in st:
                    load_rows(st["load"])
                for b in range(st["chunks"] // 2):
                    act.wait_ge(turned, c.add("turned"))
                    if st["gain"] is None:
                        i = nc.scalar.activation(dst[:, 2 * b:2 * b + 2].rearrange("p k s -> p (k s)"), PS[:, 4 + b], ACT.Copy)
                    else:
                        for k in (2 * b, 2 * b + 1):
                            i = nc.scalar.activation(dst[:, k], PS[:, 4 + b, (k % 2) * S:(k % 2 + 1) * S], ACT.Copy,
                                                     scale=gain_col(st["gain"], k))
                    i.then_inc(x_high, 1)

            def product(st):
                if "load" in st:
                    load_rows(st["load"])
                if "ple" in st:
                    act.dma_start(PR[:, :, 0:256], a["p"][st["ple"], 0].rearrange("(t p) d -> p t d", p=P)).then_inc(ple_in, 16)
                col = st.get("first", 0)
                for n, tile in enumerate(st["tiles"]):
                    h, w = st["h0"] + n, tile["width"]
                    split_to(h + SPLIT)
                    if not tile["last"]:
                        continue
                    g = c.add("block") - 1
                    if st["use"] in ("copy", "gate"):
                        act.wait_ge(tile_used, h + 1)
                    if st["use"] == "copy":
                        nc.scalar.activation(PR[:, 0, col:col + w], PS[:, 2 * (g % 2), 0:w], ACT.Copy).then_inc(act_evac, 1)
                    if st["use"] == "gate":
                        nc.scalar.activation(S0[:, :, col:col + w], PS[:, 2 * (g % 2):2 * (g % 2) + 2, 0:w],
                                             ACT.Sigmoid).then_inc(act_evac, 1)
                    col += w
                split_to(st["h0"] + len(st["tiles"]) + SPLIT - 1)
                if "ple" in st:
                    act.wait_ge(ple_in, 16 * (st["ple"] + 1))

            def copy_qk():
                n = c.add("qk")
                act.wait_ge(qk_turned, n)
                nc.scalar.activation(QKT[:, (n - 1) % 2], PS[:, 0, :], ACT.Copy).then_inc(qk_copied, 1)

            def pairs(st):
                use = st["use"]
                N = N_PAIRS[use]
                for n in range(N + 1):
                    if n < N:
                        copy_qk()
                    if use == "I":
                        continue
                    if n >= 1:
                        act.wait_ge(probs_turned, c.add("turned_probs"))
                        nc.scalar.activation(PT[:, 0], PS[:, 5, 0:384], ACT.Copy).then_inc(probs_act, 1)
                    if n < N:
                        m = c.add("probs")
                        act.wait_ge(max_ready, m)
                        for i in range(4):
                            nc.scalar.activation(SM[:, m % 2, i], SM[:, m % 2, i], ACT.Exp, bias=NMX[:, m % 2, i:i + 1],
                                                 accum_out=SUM[:, m % 2, i:i + 1])
                        if use == "W":
                            nc.scalar.activation(EDS[:, m % 2], SINKD[:, m % 2], ACT.Exp)
                        act.drain().then_inc(probs_ready, 1)

            def sticks(st):
                for n in range(4):
                    copy_qk()
                    z = PS[:, 1:3, 0:384]
                    w = S2f[:, 0:768].rearrange("p (h k) -> p h k", h=2)
                    act.wait_ge(stick_scores, c.add("stick_scores"))
                    nc.scalar.activation(w, z, ACT.Abs, scale=SCALE).then_inc(act_to_dve, 1)
                    act.drain()
                    nc.scalar.activation(w, w, ACT.Exp, scale=-1.0)
                    act.drain()
                    nc.scalar.activation(w, w, ACT.Ln, bias=1.0).then_inc(act_to_dve, 1)
                    act.wait_ge(dve_to_act, c.add("dve_to_act"))
                    nc.scalar.activation(S0f[:, 768:1536], S0f[:, 768:1536], ACT.Exp).then_inc(act_to_dve, 1)

            def retention(st):
                for n in range(RET_HEADS):
                    lg = math.log(1.0 - 2.0 ** (-5.0 - n))
                    nc.scalar.activation(S1f[:, n * 384:(n + 1) * 384], C("dist"), ACT.Exp, scale=lg).then_inc(act_to_dve, 1)
                for n in range(RET_HEADS):
                    copy_qk()

            def silu_of(first):
                nc.scalar.activation(S0[:], PR[:, :, first:first + D], ACT.Silu).then_inc(act_to_dve, 1)

            def hgrn_forget(st):
                hf = PR[:, :, 1024:2048]
                nc.scalar.activation(hf, hf, ACT.Sigmoid).then_inc(act_to_dve, 1)
                if st["layer"] > 0:
                    for i in range(DEPTH):
                        act.dma_start(S3[:, i], a["hgrn_lower_bounds_2"][i].partition_broadcast(P)).then_inc(lb_in, 16)
                    act.wait_ge(dve_to_act, c.add("dve_to_act"))
                    nc.scalar.activation(S3[:, 0], S3[:, 0], ACT.Exp).then_inc(act_to_dve, 1)
                act.wait_ge(dve_to_act, c.add("dve_to_act"))
                nc.scalar.activation(S0[:], S0[:], ACT.Ln)

            def hgrn_scale(st):
                up, later = PS[:, 0:4].rearrange("p b c -> p (b c)"), PS[:, 4:8].rearrange("p b c -> p (b c)")
                nc.scalar.activation(S1f, up, ACT.Exp).then_inc(act_to_dve, 1)
                nc.scalar.activation(S2f, later, ACT.Exp).then_inc(act_to_dve, 1)
                act.wait_ge(dve_to_act, c.add("dve_to_act"))
                nc.scalar.activation(S1f, up, ACT.Exp, scale=-1.0).then_inc(act_to_dve, 1)

            def hgrn_heads(st):
                for n in range(HG_HEADS):
                    copy_qk()
                    act.wait_ge(dve_to_act, c.add("dve_to_act"))
                    nc.scalar.activation(DEC[:, n % 2], DEC[:, n % 2], ACT.Exp).then_inc(act_to_dve, 1)

            def mlp(st):
                two = st["use"] == "swiglu"
                for n, tile in enumerate(st["tiles"]):
                    h, j, w = st["h0"] + n, tile["block"], tile["width"]
                    if tile["role"] == "down" and tile["first"]:
                        k = tile["rows"]
                        bank = 2 if two else 2 * (j % 2)
                        act.wait_ge(hid_turned, c.add("hid"))
                        nc.scalar.activation(HIDT[0][:, j % 2, 0:k].rearrange("p k s -> p (k s)"),
                                             PS[:, bank:bank + 2].rearrange("p b c -> p (b c)")[:, 0:k * S],
                                             ACT.Copy).then_inc(hid_high, 1)
                    split_to(h + SPLIT)
                    if tile["role"] == "gate" and tile["last"]:
                        act.wait_ge(tile_used, h + 1)
                        nc.scalar.activation(SG[:, j % 2, :, 0:w], PS[:, 0:2, 0:w], ACT.Silu).then_inc(silu_ready, 1)
                    if not two and tile["role"] == "up" and tile["last"]:
                        act.wait_ge(tile_used, h + 1)
                        nc.scalar.activation(SG[:, j % 2], PS[:, 2 * (j % 2):2 * (j % 2) + 2], ACT.Relu).then_inc(silu_ready, 1)
                split_to(st["h0"] + len(st["tiles"]) + SPLIT - 1)

            def route(st):
                act.wait_ge(dve_to_act, c.add("dve_to_act"))
                nc.scalar.activation(ROUTE[:, :, 2, 0:8], ROUTE[:, :, 2, 0:8], ACT.Exp).then_inc(act_to_dve, 1)

            def experts(st):
                act.wait_ge(passes_ready, 1)
                passes = act.value_load(NPASS[0:1, 0:1], min_val=1, max_val=T)
                with act.Fori(0, passes * (N_EXPERTS // 2)) as i:
                    made = 0
                    for half in range(2):
                        m = i * 2 + half
                        for kk in range(2):
                            act.wait_ge(gathered, m * 2 + kk + 1)
                            nc.scalar.activation(XG[0][:, 4 * kk:4 * kk + 4].rearrange("p k s -> p (k s)"), PS[:, 4, :],
                                                 ACT.Copy).then_inc(gathered_high, 1)
                        act.wait_ge(choice_turned, m + 2)
                        nc.scalar.activation(CHOICET.rearrange("p t s -> p (t s)"), PS[:, 4, 0:S],
                                             ACT.Copy).then_inc(choice_copied, 1)
                        for n, tile in enumerate(st["tiles"]):
                            h, j = half * (PAIR // 2) + n, tile["block"]
                            par = (half * J + j) % 2
                            if tile["role"] == "down" and tile["first"]:
                                act.wait_ge(xh_turned, m * J + j + 1)
                                nc.scalar.activation(HIDT2[0][:, par].rearrange("p k s -> p (k s)"), PS[:, 4, :],
                                                     ACT.Copy).then_inc(xh_high, 1)
                            while made < min(h + SPLIT, PAIR):
                                high_part(STATIC + made, st["tiles"][made % (PAIR // 2)], (i * (PAIR // RAW), i * PAIR))
                                made += 1
                            if tile["role"] == "gate" and tile["last"]:
                                act.wait_ge(tile_used, i * PAIR + STATIC + h + 1)
                                nc.scalar.activation(SG2[:, par], PS[:, par], ACT.Silu).then_inc(xsilu_ready, 1)
                        act.wait_ge(tile_used, i * PAIR + STATIC + (half + 1) * (PAIR // 2))
                        nc.scalar.activation(YE.rearrange("p b c -> p (b c)"), PS[:, 6:8].rearrange("p b c -> p (b c)"),
                                             ACT.Copy).then_inc(down_read, 1)

            run = dict(setup=setup, rms_in=rms_in, ret_rotary=ret_rotary, layer_norm=layer_norm, turn=turn, product=product, pairs=pairs, sticks=sticks,
                       retention=retention, hgrn_forget=hgrn_forget, hgrn_scale=hgrn_scale, hgrn_heads=hgrn_heads,
                       mlp=mlp, route=route, experts=experts, ret_finish=lambda st: silu_of(2048),
                       hgrn_finish=lambda st: silu_of(3072), swa_prepare=lambda st: load_rows(st["load"]))
            for n, st in enumerate(stages):
                if st["kind"] in run:
                    run[st["kind"]](st)
                finish_stage(act, n)

        rsqrts = [0]

        @block.vector
        def _(dve):
            c = Count()
            v = nc.vector
            split = [0]

            def low_part(h, tile, done=0):
                dve.wait_ge(high_ready, h + 1 + done)
                v.tensor_tensor(tile_view(WL, h % SPLIT, tile), tile_view(raw, h % RAW, tile),
                                tile_view(WH, h % SPLIT, tile).bitcast(F32), ALU.subtract).then_inc(low_ready, 1)

            def split_to(n):
                while split[0] < min(n, STATIC):
                    low_part(split[0], static_tiles[split[0]])
                    split[0] += 1

            def rsqrt(n, width):
                dve.drain()
                v.tensor_scalar(STAT[:, 0:n], STAT[:, 0:n], 1.0 / width, RMS_EPS, ALU.mult, ALU.add).then_inc(sums_ready, 1)
                rsqrts[0] += 1
                dve.wait_ge(rsqrt_ready, rsqrts[0])

            def group_norm(x, t, g, d, work):
                view = lambda b: b.rearrange("p t (g d) -> p t g d", g=g, d=d)
                v.tensor_tensor(work, x, x, ALU.mult)
                dve.drain()
                v.tensor_reduce(STAT[:, 0:t * g].rearrange("p (t g) -> p t g", t=t), view(work), AX, ALU.add)
                rsqrt(t * g, d)
                r = RSTD[:, 0:t * g].rearrange("p (t g) -> p t g", t=t).unsqueeze(3).broadcast_to([P, t, g, d])
                v.tensor_tensor(view(x), view(x), r, ALU.mult)
                dve.drain()

            def rope(x, g, half, cos, sin, w1, w2):
                view = lambda b: b.rearrange("p (g h d) -> p g h d", g=g, h=2, d=half)
                X4, A, B = view(x), view(w1), view(w2)
                cb = cos.unsqueeze(1).unsqueeze(1).broadcast_to([P, g, 2, half])
                sb_ = sin.unsqueeze(1).broadcast_to([P, g, half])
                v.tensor_tensor(A, X4, cb, ALU.mult)
                v.tensor_tensor(B[:, :, 0], X4[:, :, 1], sb_, ALU.mult)
                v.tensor_tensor(B[:, :, 1], X4[:, :, 0], sb_, ALU.mult)
                dve.drain()
                v.tensor_tensor(X4[:, :, 0], A[:, :, 0], B[:, :, 0], ALU.subtract)
                v.tensor_tensor(X4[:, :, 1], A[:, :, 1], B[:, :, 1], ALU.add)

            def setup(st):
                v.memset(STAT[:], 1.0)
                dve.wait_ge(const_in, 16 * N_LOADS)
                pos = SQ
                v.tensor_copy(pos[:], POSI[:])
                dve.drain()
                ang, n1, n2 = S1f[:, 0:64], S1f[:, 64:128], S1f[:, 128:192]
                for t in range(T):
                    v.tensor_scalar(ang[:, t * 32:(t + 1) * 32], C("inv_freq"), pos[:, t:t + 1], None, ALU.mult)
                dve.drain()
                for dst, turn_, shift in ((SIN, 0.0, 0.0), (COS, 0.25, math.pi / 2)):
                    d = dst.rearrange("p t f -> p (t f)")
                    v.tensor_scalar(n1, ang, 1 / (2 * math.pi), turn_, ALU.mult, ALU.add)
                    dve.drain()
                    v.tensor_scalar(n1, n1, MAGIC, None, ALU.add)
                    dve.drain()
                    v.tensor_scalar(n1, n1, MAGIC, None, ALU.subtract)
                    dve.drain()
                    v.scalar_tensor_tensor(out=d, in0=n1, scalar=-6.28125, in1=ang, op0=ALU.mult, op1=ALU.add)
                    dve.drain()
                    v.scalar_tensor_tensor(out=d, in0=n1, scalar=-(2 * math.pi - 6.28125), in1=d, op0=ALU.mult, op1=ALU.add)
                    dve.drain()
                    v.tensor_scalar(d, d, shift, 3.1415925, ALU.add, ALU.min)
                    dve.drain()
                    v.tensor_scalar(d, d, -3.1415925, None, ALU.max)
                pairs_ = LAMB.rearrange("p l (i j) d -> p l i j d", j=2)
                prod = S0f[:, 0:DEPTH * 2 * HD].rearrange("p (l i d) -> p l i d", l=DEPTH, i=2)
                for l in range(DEPTH):
                    v.tensor_tensor(prod[:, l], pairs_[:, l, :, 0], pairs_[:, l, :, 1], ALU.mult)
                dve.drain()
                for l in range(DEPTH):
                    v.tensor_reduce(LAME[:, l], prod[:, l], AX, ALU.add)
                dve.drain().then_inc(dve_to_act, 1)
                dve.wait_ge(act_to_dve, c.add("act_to_dve"))
                for l in range(DEPTH):
                    v.tensor_tensor(LAM[:, l, 0:1], LAME[:, l, 1:2], LAME[:, l, 0:1], ALU.subtract)
                dve.drain()
                for l in range(DEPTH):
                    v.tensor_scalar(LAM[:, l, 1:2], LAM[:, l, 0:1], -(0.8 - 0.6 * math.exp(-0.3 * l)), None, ALU.add)

            def rms_in(st):
                dve.wait_ge(squares, c.add("squares"))
                v.tensor_copy(STAT[:, 0:T], SQ[:])
                rsqrt(T, D)
                for t in range(T):
                    v.tensor_scalar(S0[:, t], X[:, t], RSTD[:, t:t + 1], None, ALU.mult)

            def turn(st):
                high, low = buf[st["dst"]]
                for b in range(st["chunks"] // 2):
                    dve.wait_ge(x_high, c.add("x_high"))
                    if st["gain"] is None:
                        flat = lambda x: x[:, 2 * b:2 * b + 2].rearrange("p k s -> p (k s)")
                        v.tensor_tensor(flat(low), PS[:, 4 + b], flat(high).bitcast(F32), ALU.subtract)
                    else:
                        for k in (2 * b, 2 * b + 1):
                            v.scalar_tensor_tensor(out=low[:, k], in0=PS[:, 4 + b, (k % 2) * S:(k % 2 + 1) * S],
                                                   scalar=gain_col(st["gain"], k), in1=high[:, k].bitcast(F32),
                                                   op0=ALU.mult, op1=ALU.subtract)

            def product(st):
                use = st["use"]
                col = st.get("first", 0)
                for n, tile in enumerate(st["tiles"]):
                    h, w = st["h0"] + n, tile["width"]
                    split_to(h + SPLIT)
                    if not tile["last"]:
                        continue
                    g = c.add("block") - 1
                    cs = slice(col, col + w)
                    ps = PS[:, 2 * (g % 2):2 * (g % 2) + 2, 0:w]
                    if use != "gate":
                        dve.wait_ge(tile_used, h + 1)
                    if use == "copy":
                        v.tensor_copy(PR[:, 1, cs], ps[:, 1]).then_inc(dve_evac, 1)
                    if use == "merge" and st["first_branch"]:
                        v.tensor_tensor(MERGED[:, :, cs], ps, S0[:, :, cs], ALU.mult).then_inc(dve_evac, 1)
                    elif use in ("merge", "ple"):
                        v.tensor_tensor(S0[:, :, cs], ps, S0[:, :, cs], ALU.mult).then_inc(dve_evac, 1)
                        dve.drain()
                        acc = MERGED if use == "merge" else X
                        v.tensor_tensor(acc[:, :, cs], acc[:, :, cs], S0[:, :, cs], ALU.add)
                    if use == "resid":
                        v.scalar_tensor_tensor(out=X[:, :, cs], in0=X[:, :, cs], scalar=st["alpha"], in1=ps,
                                               op0=ALU.mult, op1=ALU.add).then_inc(dve_evac, 1)
                    col += w
                split_to(st["h0"] + len(st["tiles"]) + SPLIT - 1)

            def qk_norm(st):
                l = st["layer"]
                i = 0 if st["gain"] == "a" else 2
                group_norm(PR[:, :, 0:D], T, 16, HD, S1[:])
                for k in range(2):
                    x = PR[:, :, k * 512:(k + 1) * 512].rearrange("p t (g d) -> p t g d", d=HD)
                    for t in range(T):
                        gb = HG[:, l, i + k].unsqueeze(1).broadcast_to([P, 8, HD])
                        v.tensor_tensor(x[:, t], x[:, t], gb, ALU.mult)
                dve.drain()
                for t in range(T):
                    rope(PR[:, t, 0:D], 16, 32, COS[:, t], SIN[:, t], S1[:, t], S2[:, t])

            def index_prepare(st):
                ik = PR[:, :, 1792:1856]
                group_norm(ik, T, 1, HD, S1[:, :, 0:HD])
                for t in range(T):
                    v.tensor_tensor(ik[:, t], ik[:, t], HG[:, st["layer"], 4], ALU.mult)
                dve.drain()
                for t in range(T):
                    rope(PR[:, t, 1536:1856], 5, 32, COS[:, t], SIN[:, t], S1[:, t, 0:320], S2[:, t, 0:320])
                dve.drain()
                for i in range(2):
                    v.tensor_copy(PR[:, :, 2048 + i * HD:2048 + (i + 1) * HD], ik)
                v.tensor_scalar(PR[:, :, 1856:1860], PR[:, :, 1856:1860], IDX_HEADS ** -0.5, None, ALU.mult)

            def index_pairs():
                for n in range(2):
                    m = c.add("scores")
                    dve.wait_ge(scores_full, m)
                    for h in range(2):
                        i = v.tensor_scalar(S2[:, :, (2 * n + h) * S:(2 * n + h + 1) * S],
                                            PS[:, 1 + 2 * (m % 2) + h, :].rearrange("p (t k) -> p t k", t=T), SCALE, 0.0,
                                            ALU.mult, ALU.max)
                    i.then_inc(scores_read, 1)
                for h in range(IDX_HEADS):
                    dve.drain()
                    for t in range(T):
                        w = PR[:, t, 1856 + h:1857 + h]
                        other = C("chunk_mask")[:, t * S:(t + 1) * S] if h == 0 else S3[:, t, 0:S]
                        v.scalar_tensor_tensor(out=S3[:, t, 0:S], in0=S2[:, t, h * S:(h + 1) * S], scalar=w,
                                               in1=other, op0=ALU.mult, op1=ALU.add)

            def index_select(st):
                for t in range(T):
                    v.tensor_copy(S2[:, t, 0:S], S3[:, t, 0:S])
                for r in range(TOPK // 8):
                    dve.drain()
                    for t in range(T):
                        v.max(TOP[:, t], S2[:, t, 0:S])
                    if r < TOPK // 8 - 1:
                        dve.drain()
                        for t in range(T):
                            v.match_replace(S2[:, t, 0:S], TOP[:, t], S2[:, t, 0:S], -3.0e38)
                dve.drain()
                for t in range(T):
                    v.tensor_scalar(S1[:, t, 0:S], S3[:, t, 0:S], TOP[:, t, 7:8], None, ALU.is_equal)
                    v.tensor_scalar(S1[:, t, S:2 * S], S3[:, t, 0:S], TOP[:, t, 7:8], None, ALU.is_gt)
                dve.drain()
                dve.drain().then_inc(dve_to_pe, 1)
                for t in range(T):
                    v.tensor_reduce(NEED[:, t, 0:1], S1[:, t, S:2 * S], AX, ALU.add)
                dve.drain()
                for t in range(T):
                    v.tensor_scalar(NEED[:, t, 1:2], NEED[:, t, 0:1], -1.0, float(TOPK), ALU.mult, ALU.add)
                dve.wait_ge(pe_to_dve, c.add("pe_to_dve"))
                v.tensor_copy(S1[:, :, 512:768], PS[:, 4:6, 0:S]).then_inc(dve_to_pe, 1)
                dve.wait_ge(pe_to_dve, c.add("pe_to_dve"))
                for t in range(T):
                    v.tensor_scalar(S2[:, t, 0:S], PS[:, 6, t * S:(t + 1) * S], NEED[:, t, 1:2], None, ALU.is_le)
                dve.drain()
                v.tensor_tensor(S2[:, :, 0:S], S2[:, :, 0:S], S1[:, :, 0:S], ALU.mult)
                dve.drain()
                v.tensor_tensor(S2[:, :, 0:S], S2[:, :, 0:S], S1[:, :, S:2 * S], ALU.add)
                dve.drain()
                v.tensor_scalar(IDXM, S2[:, :, 0:S], -1.0, -NEG, ALU.add, ALU.mult)

            def pairs(st):
                use = st["use"]
                if use == "I":
                    return index_pairs()
                N = N_PAIRS[use]
                mask = {"A": C("chunk_mask").rearrange("p (t k) -> p t k", t=T), "C": IDXM,
                        "W": C("chunk_mask").rearrange("p (t k) -> p t k", t=T)}[use]
                masks = [mask[:, 0], C("window_mask") if use == "W" else mask[:, 1]]

                def mid(n):
                    m = c.add("scores")
                    s = c.add("sm")
                    b = s % 2
                    dve.wait_ge(scores_full, m)
                    if s > 2:
                        dve.wait_ge(probs_turned, s - 2)
                    for h in range(2):
                        scores = PS[:, 1 + 2 * (m % 2) + h, :].rearrange("p (t k) -> p t k", t=T)
                        if use == "W":
                            for t in range(T):
                                i = v.scalar_tensor_tensor(out=SM[:, b, 2 * t + h], in0=scores[:, t], scalar=SCALE,
                                                           in1=masks[t], op0=ALU.mult, op1=ALU.add)
                        else:
                            i = v.scalar_tensor_tensor(out=SM[:, b].rearrange("p (t h) k -> p t h k", t=T)[:, :, h],
                                                       in0=scores, scalar=SCALE, in1=mask, op0=ALU.mult, op1=ALU.add)
                    i.then_inc(scores_read, 1)
                    dve.drain()
                    v.tensor_reduce(MX[:, b], SM[:, b], AX, ALU.max)
                    dve.drain()
                    if use == "W":
                        sk = SINK[:, st["layer"], 2 * n:2 * n + 2].unsqueeze(1).broadcast_to([P, T, 2])
                        by_t = lambda x: x[:, b].rearrange("p (t h) -> p t h", t=T)
                        v.tensor_tensor(by_t(MX), by_t(MX), sk, ALU.max)
                        dve.drain()
                        v.tensor_tensor(by_t(SINKD), sk, by_t(MX), ALU.subtract)
                    v.tensor_scalar(NMX[:, b], MX[:, b], -1.0, None, ALU.mult)
                    dve.drain().then_inc(max_ready, 1)

                def back(n):
                    m = c.add("probs")
                    b = m % 2
                    dve.wait_ge(probs_turned, m)
                    v.tensor_copy(PT[:, 1], PS[:, 6, 0:384]).then_inc(probs_dve, 1)
                    if use == "W":
                        v.tensor_tensor(SUM[:, b], SUM[:, b], EDS[:, b], ALU.add)
                        dve.drain()
                    v.reciprocal(RS[:, b], SUM[:, b])
                    dve.drain()
                    if use == "A":
                        for t in range(T):
                            v.tensor_scalar(RS[:, b, 2 * t + 1:2 * t + 2], RS[:, b, 2 * t + 1:2 * t + 2],
                                            LAM[:, st["layer"], 1:2], None, ALU.mult)
                        dve.drain()
                    dve.wait_ge(values_full, m)
                    vw = P if use == "A" else HD
                    for t in range(T):
                        for h in range(2):
                            i = 2 * t + h
                            o = PS[:, 7, i * vw:(i + 1) * vw]
                            dst = S1[:, t, h * P:(h + 1) * P] if use == "A" else S3[:, t, n * P + h * HD:n * P + (h + 1) * HD]
                            v.tensor_scalar(dst, o, RS[:, b, i:i + 1], None, ALU.mult)
                    dve.drain().then_inc(values_read, 1)
                    if use == "A":
                        v.tensor_tensor(S3[:, :, n * P:(n + 1) * P], S1[:, :, 0:P], S1[:, :, P:2 * P], ALU.add)

                for n in range(N + 1):
                    if n < N:
                        mid(n)
                    if n >= 1:
                        back(n - 1)

            def a_finish(st):
                l = st["layer"]
                group_norm(S3[:, :, 0:512], T, 4, P, S1[:, :, 0:512])
                keep = 1.0 - (0.8 - 0.6 * math.exp(-0.3 * l))
                for t in range(T):
                    y = S3[:, t, 0:512].rearrange("p (g d) -> p g d", g=4)
                    v.scalar_tensor_tensor(out=y, in0=y, scalar=keep, in1=SUBLN[:, l].unsqueeze(1).broadcast_to([P, 4, P]),
                                           op0=ALU.mult, op1=ALU.mult)

            def sticks(st):
                three = lambda x: x.rearrange("p (h k) -> p h k", h=2)
                keep = C("strict").unsqueeze(1).broadcast_to([P, 2, 384])
                soft, logs, arg, wts = (three(x) for x in (S1f[:, 768:1536], S1f[:, 0:768], S0f[:, 768:1536], S0f[:, 0:768]))
                for n in range(4):
                    z = PS[:, 1:3, 0:384]
                    dve.wait_ge(act_to_dve, c.add("act_to_dve"))
                    v.tensor_scalar(soft, z, SCALE, 0.0, ALU.mult, ALU.max)
                    dve.drain()
                    dve.wait_ge(act_to_dve, c.add("act_to_dve"))
                    v.tensor_tensor(soft, soft, three(S2f[:, 0:768]), ALU.add)
                    dve.drain()
                    v.tensor_tensor(logs, soft, keep, ALU.mult).then_inc(dve_to_pe, 1)
                    v.scalar_tensor_tensor(out=arg, in0=z, scalar=SCALE, in1=soft, op0=ALU.mult, op1=ALU.subtract)
                    dve.drain()
                    dve.wait_ge(pe_to_dve, c.add("pe_to_dve"))
                    v.tensor_tensor(arg, arg, PS[:, 5:7, 0:384], ALU.subtract).then_inc(dve_to_act, 1)
                    dve.wait_ge(act_to_dve, c.add("act_to_dve"))
                    v.tensor_tensor(wts, arg, keep, ALU.mult).then_inc(dve_to_pe, 1)
                    dve.wait_ge(pe_to_dve, c.add("pe_to_dve"))
                    v.tensor_copy(S3[:, :, n * P:(n + 1) * P],
                                  PS[:, 7, 0:S].rearrange("p (t d) -> p t d", t=T)).then_inc(dve_to_pe, 1)

            def ret_rotary(st):
                for t in range(T):
                    rope(PR[:, t, 0:D], 8, 64, C("ret_cos")[:, t * 64:(t + 1) * 64], C("ret_sin")[:, t * 64:(t + 1) * 64],
                         S1[:, t], S2[:, t])

            def retention(st):
                for n in range(RET_HEADS):
                    dve.wait_ge(pe_to_dve, c.add("pe_to_dve"))
                    dve.wait_ge(act_to_dve, c.add("act_to_dve"))
                    v.scalar_tensor_tensor(out=PT[:, n % 2], in0=PS[:, 1, 0:384], scalar=P ** -0.5,
                                           in1=S1f[:, n * 384:(n + 1) * 384], op0=ALU.mult, op1=ALU.mult).then_inc(dve_to_pe, 1)
                    dve.wait_ge(pe_to_dve, c.add("pe_to_dve"))
                    v.tensor_copy(S3[:, :, n * S:(n + 1) * S],
                                  PS[:, 7, :].rearrange("p (t d) -> p t d", t=T)).then_inc(dve_to_pe, 1)

            def silu_gate():
                dve.wait_ge(act_to_dve, c.add("act_to_dve"))
                v.tensor_tensor(S3[:], S3[:], S0[:], ALU.mult)

            def ret_finish(st):
                group_norm(S3[:], T, 4, S, S1[:])
                silu_gate()

            def hgrn_finish(st):
                group_norm(S3[:], T, 8, P, S1[:])
                dve.wait_ge(hgn_in, 16 * DEPTH)
                for t in range(T):
                    y = S3[:, t].rearrange("p (g d) -> p g d", g=8)
                    v.tensor_tensor(y, y, HGN[:, st["layer"]].unsqueeze(1).broadcast_to([P, 8, P]), ALU.mult)
                dve.drain()
                silu_gate()

            def hgrn_forget(st):
                hf = PR[:, :, 1024:2048]
                dve.wait_ge(act_to_dve, c.add("act_to_dve"))
                if st["layer"] == 0:
                    v.tensor_scalar(S0[:], hf, 1e-37, None, ALU.max).then_inc(dve_to_act, 1)
                    dve.drain()
                    v.tensor_scalar(hf, hf, -1.0, 1.0, ALU.mult, ALU.add)
                    return
                dve.wait_ge(lb_in, 16 * DEPTH)
                v.tensor_tensor(S3[:, 0], S3[:, 0], S3[:, 1], ALU.subtract).then_inc(dve_to_act, 1)
                dve.wait_ge(act_to_dve, c.add("act_to_dve"))
                v.tensor_scalar(S3[:, 0], S3[:, 0], 1.0, None, ALU.add)
                dve.drain()
                v.reciprocal(S3[:, 0], S3[:, 0])
                dve.drain()
                v.tensor_scalar(S3[:, 1], S3[:, 0], -1.0, 1.0, ALU.mult, ALU.add)
                dve.drain()
                for t in range(T):
                    v.tensor_tensor(S1[:, t], hf[:, t], S3[:, 1], ALU.mult)
                dve.drain()
                for t in range(T):
                    v.tensor_tensor(S0[:, t], S1[:, t], S3[:, 0], ALU.add)
                    v.tensor_tensor(hf[:, t], S3[:, 1], S1[:, t], ALU.subtract)
                dve.drain()
                v.tensor_scalar(S0[:], S0[:], 1e-37, None, ALU.max).then_inc(dve_to_act, 1)

            def hgrn_scale(st):
                hq, hk = PR[:, :, 0:D], PR[:, :, D:2 * D]
                dve.wait_ge(act_to_dve, c.add("act_to_dve"))
                v.tensor_tensor(hq, hq, S1[:], ALU.mult).then_inc(dve_to_act, 1)
                dve.wait_ge(act_to_dve, c.add("act_to_dve"))
                v.tensor_tensor(S2[:], S2[:], hk, ALU.mult)
                dve.drain()
                dve.wait_ge(act_to_dve, c.add("act_to_dve"))
                v.tensor_tensor(hk, hk, S1[:], ALU.mult)
                dve.drain()
                v.tensor_scalar(S1[:], S2[:], C("even_odd")[:, 0:1], None, ALU.mult)
                dve.drain()
                v.tensor_scalar(S2[:], S2[:], C("even_odd")[:, 1:2], None, ALU.mult)

            def hgrn_heads(st):
                for n in range(HG_HEADS):
                    dve.wait_ge(pe_to_dve, c.add("pe_to_dve"))
                    v.tensor_copy(DEC[:, n % 2], PS[:, 1, S:S + 16]).then_inc(dve_to_act, 1)
                    v.tensor_tensor(HA, PS[:, 1, 0:S].rearrange("p (t q) -> p t q", t=T),
                                    C("block_upto").unsqueeze(1).broadcast_to([P, T, P]), ALU.mult).then_inc(dve_to_pe, 1)
                    dve.wait_ge(kv_full, c.add("kv"))
                    dve.wait_ge(act_to_dve, c.add("act_to_dve"))
                    for b in range(S // HG_BLOCK - 1):
                        m = c.add("state")
                        if m > 4:
                            dve.wait_ge(state_used, m - 4)
                        t, r = b // 8, b % 8
                        kv = PS[:, 2 + r // 2, (2 * t + r % 2) * P:(2 * t + r % 2 + 1) * P]
                        if b == 0:
                            i = v.tensor_copy(STATE[:, m % 4], kv)
                        else:
                            dve.wait_ge(state_ready, m - 1)
                            i = v.scalar_tensor_tensor(out=STATE[:, m % 4], in0=STATE[:, (m - 1) % 4],
                                                       scalar=DEC[:, n % 2, b:b + 1], in1=kv, op0=ALU.mult, op1=ALU.add)
                        i.then_inc(state_ready, 1)
                    dve.wait_ge(state_used, c.of("state"))
                    v.tensor_copy(QKT[:, (st["qk_before"] + n + 1) % 2, 0:S], PS[:, 6, 0:S]).then_inc(dve_to_pe, 1)
                    dve.wait_ge(pe_to_dve, c.add("pe_to_dve"))
                    v.tensor_copy(S3[:, :, n * P:(n + 1) * P],
                                  PS[:, 7, 0:S].rearrange("p (t d) -> p t d", t=T)).then_inc(dve_to_pe, 1)

            def swa_prepare(st):
                for g in range(4):
                    for i in range(2):
                        v.tensor_copy(PR[:, :, 2048 + g * P + i * HD:2048 + g * P + (i + 1) * HD],
                                      PR[:, :, 1024 + g * HD:1024 + (g + 1) * HD])

            def layer_norm(st):
                for t in range(T):
                    for h in range(2):
                        v.bn_stats(BST[:, t, h], X[:, t, h * 512:(h + 1) * 512])
                dve.drain()
                for t in range(T):
                    v.bn_aggr(MV[:, t], BST[:, t])
                dve.drain()
                v.tensor_scalar(STAT[:, 0:T], MV[:, :, 1], LN_EPS - RMS_EPS, None, ALU.add)
                rsqrt(T, 1)
                for t in range(T):
                    v.tensor_scalar(X[:, t], X[:, t], MV[:, t, 0:1], RSTD[:, t:t + 1], ALU.subtract, ALU.mult)
                dve.wait_ge(rows_in, 32 * (st["n"] + 1))
                dve.drain()
                for t in range(T):
                    v.tensor_tensor(X[:, t], X[:, t], S2[:, 0], ALU.mult)
                dve.drain()
                for t in range(T):
                    v.tensor_tensor(X[:, t], X[:, t], S2[:, 1], ALU.add)

            def mlp(st):
                two = st["use"] == "swiglu"
                for n, tile in enumerate(st["tiles"]):
                    h, j, w = st["h0"] + n, tile["block"], tile["width"]
                    bank = 2 if two else 2 * (j % 2)
                    if tile["role"] == "down" and tile["first"]:
                        flat = lambda x: x[:, j % 2, 0:tile["rows"]].rearrange("p k s -> p (k s)")
                        dve.wait_ge(hid_high, c.add("hid"))
                        v.tensor_tensor(flat(HIDT[1]), PS[:, bank:bank + 2].rearrange("p b c -> p (b c)")[:, 0:tile["rows"] * S],
                                        flat(HIDT[0]).bitcast(F32), ALU.subtract).then_inc(hid_low, 1)
                    split_to(h + SPLIT)
                    if tile["role"] == "up" and tile["last"]:
                        dve.wait_ge(silu_ready, c.add("silu"))
                        other = SG[:, j % 2, :, 0:w]
                        if two:
                            dve.wait_ge(tile_used, h + 1)
                            other = PS[:, bank:bank + 2, 0:w]
                        v.tensor_tensor(HID[:, j % 2, :, 0:w], SG[:, j % 2, :, 0:w], other, ALU.mult).then_inc(hidden_ready, 1)
                split_to(st["h0"] + len(st["tiles"]) + SPLIT - 1)

            def mlp_add(st):
                v.scalar_tensor_tensor(out=X[:].rearrange("p t d -> p (t d)"), in0=X[:].rearrange("p t d -> p (t d)"),
                                       scalar=st["alpha"], in1=PS[:, 4:8].rearrange("p b c -> p (b c)"),
                                       op0=ALU.mult, op1=ALU.add)

            def moe_add(st):
                v.scalar_tensor_tensor(out=X[:], in0=X[:], scalar=ALPHA, in1=MERGED[:], op0=ALU.mult, op1=ALU.add)

            def route(st):
                L = ROUTE[:, :, 0, 0:8]
                dve.wait_ge(router_in, 16)
                v.tensor_copy(RTR[0][:], ROUTER)
                dve.drain()
                v.tensor_tensor(RTR[1][:], ROUTER, RTR[0][:].bitcast(F32), ALU.subtract).then_inc(dve_to_pe, 1)
                v.memset(MERGED[:], 0.0)
                dve.wait_ge(pe_to_dve, c.add("pe_to_dve"))
                v.tensor_copy(L, PS[:, 0, 0:16].rearrange("p (t e) -> p t e", t=T))
                dve.drain()
                v.tensor_reduce(MV[:, :, 0:1], L, AX, ALU.max)
                for t in range(T):
                    sq = lambda x: x.rearrange("p (a b) -> p a b", a=8)
                    other = ROUTE[:, t, 0, 0:8].unsqueeze(1).broadcast_to([P, 8, 8])
                    own = ROUTE[:, t, 0, 0:8].unsqueeze(2).broadcast_to([P, 8, 8])
                    v.tensor_tensor(sq(RT[:, 0, t]), other, own, ALU.is_gt)
                    v.tensor_tensor(sq(RT[:, 1, t]), other, own, ALU.is_equal)
                dve.drain()
                for t in range(T):
                    v.tensor_tensor(RT[:, 1, t], RT[:, 1, t], C("tie_first"), ALU.mult)
                    v.tensor_scalar(ROUTE[:, t, 2, 0:8], ROUTE[:, t, 0, 0:8], MV[:, t, 0:1], None, ALU.subtract)
                dve.drain().then_inc(dve_to_act, 1)
                v.tensor_tensor(RT[:, 0], RT[:, 0], RT[:, 1], ALU.add)
                dve.drain()
                for t in range(T):
                    v.tensor_reduce(RT[:, 1, t, 0:8], RT[:, 0, t].rearrange("p (a b) -> p a b", a=8), AX, ALU.add)
                dve.drain()
                for h in range(2):
                    v.tensor_scalar(ROUTE[:, :, 1, 8 * h:8 * h + 8], RT[:, 1, :, 0:8], 1.5, None, ALU.is_lt)
                dve.drain().then_inc(dve_to_pe, 1)
                dve.wait_ge(act_to_dve, c.add("act_to_dve"))
                v.tensor_tensor(ROUTE[:, :, 2, 0:8], ROUTE[:, :, 2, 0:8], ROUTE[:, :, 1, 0:8], ALU.mult)
                dve.drain()
                v.tensor_reduce(MV[:, :, 0:1], ROUTE[:, :, 2, 0:8], AX, ALU.add)
                dve.drain()
                v.reciprocal(MV[:, :, 1], MV[:, :, 0])
                dve.drain()
                for t in range(T):
                    v.tensor_scalar(ROUTE[:, t, 2, 0:8], ROUTE[:, t, 2, 0:8], MV[:, t, 1:2], None, ALU.mult)
                dve.drain()
                v.tensor_copy(ROUTE[:, :, 2, 8:16], ROUTE[:, :, 2, 0:8])
                dve.wait_ge(pe_to_dve, c.add("pe_to_dve"))
                place = PS[:, 1, 0:16].rearrange("p (t e) -> p t e", t=T)
                v.tensor_copy(ROUTE[:, :, 3, 0:8], place)
                v.tensor_scalar(ROUTE[:, :, 3, 8:16], place, -float(P), None, ALU.add)
                v.tensor_reduce(MV[:, 0, 0:1], PS[:, 1, 16:24], AX, ALU.max)
                dve.drain()
                v.tensor_scalar(NPASS[:, 0:1], MV[:, 0, 0:1], P + 0.5, 1.0, ALU.is_gt, ALU.add)
                dve.drain().then_inc(passes_ready, 1)

            def experts(st):
                passes = dve.value_load(NPASS[0:1, 0:1], min_val=1, max_val=T)
                dve.drain().then_inc(xh_ready, 2)
                dve.drain().then_inc(spread_read, 1)
                with dve.Fori(0, passes * (N_EXPERTS // 2)) as i:
                    made = 0
                    for half in range(2):
                        m = i * 2 + half
                        dve.wait_ge(choice_turned, m + 1)
                        for t in range(T):
                            v.tensor_scalar(CHOICE[:, t], C("slots"), ROUTE[:, t, 3, bass.ds(m, 1)],
                                            ROUTE[:, t, 1, bass.ds(m, 1)], ALU.is_equal, ALU.mult)
                        dve.drain()
                        for t in range(T):
                            v.tensor_scalar(CHOICEW[:, t], CHOICE[:, t], ROUTE[:, t, 2, bass.ds(m, 1)], None, ALU.mult)
                        dve.drain().then_inc(choice_ready, 1)
                        for kk in range(2):
                            flat = lambda x: x[:, 4 * kk:4 * kk + 4].rearrange("p k s -> p (k s)")
                            dve.wait_ge(gathered_high, m * 2 + kk + 1)
                            v.tensor_tensor(flat(XG[1]), PS[:, 4, :], flat(XG[0]).bitcast(F32),
                                            ALU.subtract).then_inc(gathered_read, 1)
                        for n, tile in enumerate(st["tiles"]):
                            h, j = half * (PAIR // 2) + n, tile["block"]
                            par = (half * J + j) % 2
                            if tile["role"] == "down" and tile["first"]:
                                flat = lambda x: x[:, par].rearrange("p k s -> p (k s)")
                                dve.wait_ge(xh_high, m * J + j + 1)
                                v.tensor_tensor(flat(HIDT2[1]), PS[:, 4, :], flat(HIDT2[0]).bitcast(F32),
                                                ALU.subtract).then_inc(xh_copied, 1)
                            while made < min(h + SPLIT, PAIR):
                                low_part(STATIC + made, st["tiles"][made % (PAIR // 2)], i * PAIR)
                                made += 1
                            if tile["role"] == "up" and tile["last"]:
                                dve.wait_ge(xsilu_ready, m * J + j + 1)
                                dve.wait_ge(tile_used, i * PAIR + STATIC + h + 1)
                                v.tensor_tensor(HID2[:, par], SG2[:, par], PS[:, 2 + par], ALU.mult).then_inc(xh_ready, 1)
                        for t in range(T):
                            for nb in range(2):
                                s = 2 * t + nb
                                dve.wait_ge(spread_full, m * 4 + s + 1)
                                acc = MERGED[:, t, nb * NB:(nb + 1) * NB]
                                v.tensor_tensor(acc, acc, PS[:, 5], ALU.add).then_inc(spread_read, 1)

            run = dict(setup=setup, rms_in=rms_in, turn=turn, product=product, qk_norm=qk_norm,
                       index_prepare=index_prepare, index_select=index_select, pairs=pairs, a_finish=a_finish,
                       sticks=sticks, ret_rotary=ret_rotary, retention=retention, ret_finish=ret_finish,
                       hgrn_forget=hgrn_forget, hgrn_scale=hgrn_scale, hgrn_heads=hgrn_heads, hgrn_finish=hgrn_finish,
                       swa_prepare=swa_prepare, layer_norm=layer_norm, mlp=mlp, mlp_add=mlp_add, moe_add=moe_add,
                       route=route, experts=experts)
            for n, st in enumerate(stages):
                if st["kind"] in run:
                    run[st["kind"]](st)
                finish_stage(dve, n)

        @block.gpsimd
        def _(pool):
            nc.gpsimd.memset(MHALF[:], -0.5)
            pool.drain()
            with pool.Fori(0, rsqrts[0]) as i:
                pool.wait_ge(sums_ready, i + 1)
                nc.gpsimd.tensor_tensor(RSTD[:], STAT[:], MHALF[:], ALU.pow).then_inc(rsqrt_ready, 1)


_INS = ["x", "p", "positions", "attn_norm", "w_in", "a_q_norm", "a_k_norm", "a_lambda", "a_subln", "c_q_norm",
        "c_k_norm", "idx_k_norm", "w_br_a", "w_br_b", "w_br_c", "w_out", "mlp_norm", "w_up", "w_down", "ple_norm",
        "w_ple_gate", "w_ple_proj", "ln_in_g_2", "ln_in_b_2", "w_in_2", "ret_w_out_2", "hgrn_lower_bounds_2",
        "hgrn_norm_g_2", "hgrn_w_out_2", "swa_sinks_2", "swa_w_out_2", "w_o_2", "ln_mix_g_2", "ln_mix_b_2",
        "ffn_w_gate_2", "ffn_w_up_2", "ffn_w_down_2", "moe_router_2", "moe_w_gate_2", "moe_w_up_2", "moe_w_down_2",
        "ln_ffn_g_2", "ln_ffn_b_2"]


def kernel(**inputs):
    import concourse.bacc as _bacc
    from concourse.bass_utils import run_bass_kernel_spmd as _run

    nc = _bacc.Bacc("TRN2", target_bir_lowering=False, num_devices=1)
    arrays, aps = {}, {}
    constants, const_at = shape_constants()
    for name in _INS + ["shape_constants"]:
        x = np.ascontiguousarray(constants if name == "shape_constants" else inputs[name])
        arrays[f"in_{name}_dram"] = x
        aps[name] = nc.dram_tensor(f"in_{name}_dram", x.shape, mybir.dt.from_np(x.dtype), kind="ExternalInput").ap()
    out = nc.dram_tensor("out_0_dram", (1, S, D), F32, kind="ExternalOutput").ap()
    build(nc, aps, out, const_at)
    r = _run(nc, [arrays], core_ids=[0])
    return r.results[0]["out_0_dram"]
```

```python
import math
from contextlib import ExitStack

import numpy as np

import concourse.bass as bass
from concourse import mybir

F32 = mybir.dt.float32
F32R = mybir.dt.float32r
I32 = mybir.dt.int32
ALU = mybir.AluOpType
ACT = mybir.ActivationFunctionType
AX = mybir.AxisListType.X

P = 128
S = 256
T = S // P
D = 1024
KD = D // P
HD = 64
CH = 64
NB = 512
RAW = 4
SPLIT = 3
KT = 4
TILE = KT * NB
DEPTH = 2
TOPK = 64
IDX_HEADS = 4
HG_BLOCK = 16
HG_HEADS = 8
RET_HEADS = 4
D_FF_2 = 2816
N_EXPERTS = 8
D_EXP = 3584
NEG = -1.0e30
RMS_EPS = 1e-6
LN_EPS = 1e-5
ALPHA = (2.0 * DEPTH) ** 0.25
SCALE = HD ** -0.5
MAGIC = 1.5 * 2.0 ** 23


def shape_constants():
    q, k = np.arange(S), np.arange(S)
    r = np.arange(P)
    parts = {}
    parts["ident"] = np.eye(P)
    chunk_ok = (k[None, :] // CH) <= (q[:, None] // CH)
    window_ok = chunk_ok & ((q[:, None] // CH) - (k[None, :] // CH) <= 2)
    by_tile = lambda m: m.reshape(T, P, -1).transpose(1, 0, 2).reshape(P, -1)
    parts["chunk_mask"] = by_tile(np.where(chunk_ok, 0.0, NEG))
    parts["window_mask"] = np.where(window_ok, 0.0, NEG)[P:]
    dist = np.concatenate([q[None, :] - r[:, None], r[None, :] - r[:, None]], 1)
    parts["strict"] = (dist > 0) * 1.0
    parts["dist"] = np.where(dist >= 0, dist, 1e6)
    parts["later"] = (r[:, None] > r[None, :]) * 1.0
    parts["upto"] = (r[:, None] <= r[None, :]) * 1.0
    parts["ones"] = np.ones((P, P))
    same = (r[:, None] // HG_BLOCK) == (r[None, :] // HG_BLOCK)
    parts["block_upto"] = (same & (r[:, None] <= r[None, :])) * 1.0
    parts["block_later"] = (same & (r[:, None] > r[None, :])) * 1.0
    parts["in_block"] = (r[:, None] // HG_BLOCK == np.arange(P // HG_BLOCK)[None, :]) * 1.0
    parts["even_odd"] = np.stack([(r // HG_BLOCK) % 2 == 0, (r // HG_BLOCK) % 2 == 1], 1) * 1.0
    half = 64
    inv = (1.0 / (np.float32(10000.0) ** np.linspace(0, 1, half, dtype=np.float32))).astype(np.float32)
    ang = (q.astype(np.float32)[:, None] * inv[None, :]).astype(np.float64)
    parts["ret_cos"] = by_tile(np.cos(ang))
    parts["ret_sin"] = by_tile(np.sin(ang))
    inv1 = np.float32(10000.0) ** (-np.arange(0, HD, 2, dtype=np.float32) / HD)
    parts["inv_freq"] = np.broadcast_to(inv1, (P, HD // 2))
    parts["slots"] = np.broadcast_to(r, (P, P))
    e = np.arange(N_EXPERTS)
    parts["tie_first"] = np.broadcast_to((e[None, :] < e[:, None]).reshape(1, -1) * 1.0, (P, 64))
    at, n = {}, 0
    for name, a in parts.items():
        at[name] = (n, a.shape[1])
        n += a.shape[1]
    return np.concatenate([np.asarray(a, np.float32) for a in parts.values()], 1), at


def column_tiles(name, layer, rows, c0, n, role="block", block=None):
    for b, c in enumerate(range(0, n, NB)):
        for r in range(0, rows, KT):
            yield dict(name=name, layer=layer, row=r * P, rows=min(KT, rows - r), col=c0 + c, width=min(NB, n - c),
                       k=r, last=r + KT >= rows, role=role, block=b if block is None else block)


def down_tiles(name, layer, row, rows, j):
    for nb in range(D // NB):
        yield dict(name=name, layer=layer, row=row, rows=rows, col=nb * NB, width=NB, k=0, last=nb == D // NB - 1,
                   first=nb == 0, role="down", block=j, half=nb)


def ffn_tiles(gate, up, down, layer, blocks, late_up):
    for j in range(len(blocks) + 1):
        new = []
        if j < len(blocks):
            c, w = blocks[j]
            if gate:
                yield from column_tiles(gate, layer, KD, c, w, "gate", j)
            new = list(column_tiles(up, layer, KD, c, w, "up", j))
        if not late_up:
            yield from new
        if j >= 1:
            c, w = blocks[j - 1]
            yield from down_tiles(down, layer, c, w // P, j - 1)
        if late_up:
            yield from new


def block_to_turn(tiles, n):
    late = n >= 1 and tiles[n - 1]["block"] == tiles[n]["block"]
    if tiles[n]["role"] == "down" and tiles[n]["first"] and late:
        return tiles[n]
    if n + 1 < len(tiles) and tiles[n + 1]["role"] == "down" and tiles[n + 1]["first"]:
        if tiles[n + 1]["block"] != tiles[n]["block"]:
            return tiles[n + 1]
    return None


def schedule():
    out = []

    def add(kind, **kw):
        out.append(dict(kind=kind, **kw))

    def product(use, name, of_layer, c0, n, rows=KD, **kw):
        add("product", use=use, tiles=list(column_tiles(name, of_layer, rows, c0, n)), **kw)

    add("setup")
    for l in range(DEPTH):
        add("turn", src="X", dst="HT", chunks=KD, gain=("attn_norm", l))
        product("copy", "w_in", l, 0, 1536, lhs="HT", first=0, layer=l, norm=True, scaled=True,
                beside={4: "qk_squares a", 5: "qk_sums a"})
        product("gate", "w_in", l, 4932, D, lhs="HT", gate="G", layer=l, scaled=True,
                beside={0: "qk_scale a", 1: "qk_gain a", 2: "qk_rope0 a", 3: "qk_rope1 a"})
        add("pairs", use="A", layer=l)
        add("a_finish", layer=l)
        add("turn", src="Y", dst="YT", chunks=4, gain=None)
        product("merge", "w_br_a", l, 0, D, rows=4, lhs="YT", gate="G", first_branch=True)
        product("copy", "w_in", l, 1536, 1536, lhs="HT", first=0, scaled=True)
        add("sticks", layer=l, scaled=True, tiles=list(column_tiles("w_in", l, KD, 4932 + D, D)))
        add("turn", src="Y", dst="YT", chunks=4, gain=None)
        product("merge", "w_br_b", l, 0, D, rows=4, lhs="YT", gate="G", first_branch=False)
        product("copy", "w_in", l, 3072, 1860, lhs="HT", first=0, layer=l, scaled=True,
                beside={4: "qk_squares c", 5: "qk_sums c", 6: "qk_scale c", 7: "qk_gain c"})
        product("gate", "w_in", l, 4932 + 2 * D, D, lhs="HT", gate="G", layer=l, scaled=True,
                beside={0: "qk_rope0 c", 1: "qk_rope1 c", 2: "index_norm", 3: "index_rope"})
        add("pairs", use="I", layer=l)
        add("index_select", layer=l)
        add("pairs", use="C", layer=l)
        add("turn", src="Y", dst="YT", chunks=4, gain=None)
        product("merge", "w_br_c", l, 0, D, rows=4, lhs="YT", gate="G", first_branch=False)
        add("turn", src="MERGED", dst="HT", chunks=KD, gain=None)
        product("resid", "w_out", l, 0, D, lhs="HT", alpha=1.0)
        add("turn", src="X", dst="HT", chunks=KD, gain=("mlp_norm", l))
        add("mlp", use="relu2", norm=True, scaled=True, tiles=list(ffn_tiles(None, "w_up", "w_down", l, [(c, NB) for c in range(0, 4 * D, NB)], False)))
        add("mlp_add", alpha=1.0)
        add("turn", src="X", dst="HT", chunks=KD, gain=("ple_norm", l))
        product("gate", "w_ple_gate", l, 0, D, lhs="HT", ple=l, norm=True, scaled=True)
        add("turn", src="P", dst="YT", chunks=2, gain=None, width=256)
        product("ple", "w_ple_proj", l, 0, D, rows=2, lhs="YT", **({"load": 0} if l == DEPTH - 1 else {}))
    add("layer_norm", gain=("ln_in_g_2", "ln_in_b_2", None), n=0)
    for l in range(DEPTH):
        add("turn", src="X", dst="HT", chunks=KD, gain=None)
        product("copy", "w_in_2", l, 0, 3072, lhs="HT", first=0, layer=l, beside={4: "ret_rotary0", 7: "ret_rotary1"})
        add("retention", layer=l)
        product("gate", "w_in_2", l, 8704, D, lhs="HT", layer=l,
                beside={0: "out_squares ret", 1: "out_sums ret", 2: "out_scale ret", 3: "out_gate ret"})
        add("turn", src="Y", dst="YT", chunks=KD, gain=None)
        product("merge", "ret_w_out_2", l, 0, D, lhs="YT", first_branch=True)
        product("copy", "w_in_2", l, 3072, 4096, lhs="HT", first=0, layer=l,
                beside={n: f"forget{n - 8}" for n in range(8, 16)})
        add("hgrn_decay")
        add("hgrn_scale")
        add("hgrn_heads")
        product("gate", "w_in_2", l, 8704 + D, D, lhs="HT", layer=l,
                beside={0: "out_squares hgrn", 1: "out_sums hgrn", 2: "out_scale hgrn", 3: "out_gate hgrn"})
        add("turn", src="YH", dst="YT", chunks=KD, gain=None)
        product("merge", "hgrn_w_out_2", l, 0, D, lhs="YT", first_branch=False)
        product("copy", "w_in_2", l, 7168, 1536, lhs="HT", first=0)
        add("swa_prepare", load=2 * l + 1)
        add("pairs", use="W", layer=l)
        product("gate", "w_in_2", l, 8704 + 2 * D, D, lhs="HT")
        add("turn", src="Y", dst="YT", chunks=KD, gain=None)
        product("merge", "swa_w_out_2", l, 0, D, lhs="YT", first_branch=False)
        add("turn", src="MERGED", dst="HT", chunks=KD, gain=None)
        product("resid", "w_o_2", l, 0, D, lhs="HT", alpha=ALPHA)
        add("layer_norm", gain=("ln_mix_g_2", "ln_mix_b_2", l), n=2 * l + 1)
        add("turn", src="X", dst="HT", chunks=KD, gain=None, load=2 * l + 2)
        if l % 2 == 0:
            add("mlp", use="swiglu", tiles=list(ffn_tiles(
                "ffn_w_gate_2", "ffn_w_up_2", "ffn_w_down_2", l // 2,
                [(c, min(NB, D_FF_2 - c)) for c in range(0, D_FF_2, NB)], True)))
            add("mlp_add", alpha=ALPHA)
        else:
            add("route", layer=l // 2)
            add("experts", layer=l // 2, tiles=list(ffn_tiles(
                "moe_w_gate_2", "moe_w_up_2", "moe_w_down_2", l // 2, [(c, NB) for c in range(0, D_EXP, NB)], False)))
            add("moe_add")
        add("layer_norm", gain=("ln_ffn_g_2", "ln_ffn_b_2", l), n=2 * l + 2)
    return out


LN_ROWS = [("ln_in_g_2", "ln_in_b_2", None), ("ln_mix_g_2", "ln_mix_b_2", 0), ("ln_ffn_g_2", "ln_ffn_b_2", 0),
           ("ln_mix_g_2", "ln_mix_b_2", 1), ("ln_ffn_g_2", "ln_ffn_b_2", 1)]


def build(nc, a, out, const_at):
    stages = schedule()
    with ExitStack() as ctx:
        def sb(name, shape, dt=F32):
            return ctx.enter_context(nc.sbuf_tensor(name, [P] + shape, dt))

        def sem(name):
            return ctx.enter_context(nc.semaphore(name))

        raw = sb("weights_raw", [RAW, TILE])
        WH = sb("weights_high", [SPLIT, TILE], F32R)
        WL = sb("weights_low", [SPLIT, TILE], F32R)
        X = sb("x_residual", [T, D])
        HT = [sb(f"h_transposed_{part}", [KD, S], F32R) for part in ("high", "low")]
        YT = [sb(f"y_transposed_{part}", [KD, S], F32R) for part in ("high", "low")]
        RTR = [sb(f"router_{part}", [KD, N_EXPERTS], F32R) for part in ("high", "low")]
        PR = sb("projected", [T, 4096])
        MERGED = sb("merged", [T, D])
        S0 = sb("scratch0", [T, D])
        S1 = sb("scratch1", [T, D])
        S2 = sb("scratch2", [T, D])
        QKT = sb("qk_transposed", [2, NB])
        PT = sb("weights_transposed", [2, 384])
        n_const = sum(w for _, w in const_at.values())
        CONST = sb("constants", [n_const])
        STAT = sb("mean_squares", [32])
        RSTD = sb("rsqrt", [32])
        MHALF = sb("minus_half", [32])
        COS = sb("rope_cos", [T, 32])
        SIN = sb("rope_sin", [T, 32])
        GAINS = sb("gain_columns", [6, KD])
        HG = sb("head_gains", [DEPTH, 5, HD])
        SUBLN = sb("subln_gain", [DEPTH, P])
        HGN = SUBLN
        LAM = sb("minus_lambda", [DEPTH, 4])
        SINK = sb("sinks", [DEPTH, 16])
        MX = sb("row_max", [2, 4])
        NMX = sb("minus_row_max", [2, 4])
        SINKD = sb("sink_minus_max", [2, 4])
        SUM = sb("row_sum", [2, 4])
        RS = sb("row_scale", [2, 4])
        MV = sb("mean_var", [T, 2])
        BST = sb("bn_stats", [T, 2, 6])
        POSI = sb("positions_int", [T], I32)
        DEC = sb("block_decay", [2, 16])
        LAME = sb("lambda_exp", [DEPTH, 2])
        EDS = sb("sink_exp", [2, 4])
        TOP = sb("top_values", [T, 8])
        NEED = sb("ties_needed", [T, 2])
        NPASS = sb("passes", [2], I32)
        PS = ctx.enter_context(nc.psum_tensor("banks", [P, 8, NB], F32))
        Y, YH = PR[:, :, 3072:4096], PR[:, :, 0:D]
        G = PR[:, :, 2048:3072]
        buf = dict(X=X, HT=HT, YT=YT, P=PR, Y=Y, YH=YH, G=G, MERGED=MERGED, S0=S0, S1=S1, S2=S2)

        def C(name):
            n, w = const_at[name]
            return CONST[:, n:n + w]

        SM = S0.rearrange("p t d -> p (t d)").rearrange("p (b i k) -> p b i k", b=2, i=4)
        PRf = PR.rearrange("p t d -> p (t d)")
        S0f, S1f, S2f = (b.rearrange("p t d -> p (t d)") for b in (S0, S1, S2))
        IDXM = PR[:, :, 3712:3968]
        SQ = sb("square_sums", [T])
        RX = sb("token_scale", [T])
        ROUTE = PRf[:, 6464:6592].rearrange("p (t i e) -> p t i e", t=T, i=4)
        ROUTER = PRf[:, 6400:6464].rearrange("p (k e) -> p k e", k=KD)
        RT = PRf[:, 6144:6400].rearrange("p (i t e) -> p i t e", i=2, t=T)
        STATE = PT.rearrange("p a b -> p (a b)")[:, 0:512].rearrange("p (s v) -> p s v", s=4)
        HA = PT.rearrange("p a b -> p (a b)")[:, 512:768].rearrange("p (t q) -> p t q", t=T)
        LAMB = PR[:, 0, 0:DEPTH * 4 * HD].rearrange("p (l i d) -> p l i d", l=DEPTH, i=4)
        HID = PRf[:, 0:2048].rearrange("p (b t c) -> p b t c", b=2, t=T)
        SG = PRf[:, 2048:4096].rearrange("p (b t c) -> p b t c", b=2, t=T)
        HIDT = [y.rearrange("p (b k) s -> p b k s", b=2) for y in YT]
        HID2 = PRf[:, 0:1024].rearrange("p (b c) -> p b c", b=2)
        HIDT2 = [y.rearrange("p k s -> p (k s)")[:, 0:1024].rearrange("p (b k s) -> p b k s", b=2, k=4) for y in YT]
        SG2 = PRf[:, 2048:3072].rearrange("p (b c) -> p b c", b=2)
        XG = [h.rearrange("p k s -> p (k s)")[:, 0:1024].rearrange("p (k s) -> p k s", k=KD) for h in HT]
        YE = PRf[:, 4096:5120].rearrange("p (b c) -> p b c", b=2)
        CHOICE = PRf[:, 5120:5376].rearrange("p (t s) -> p t s", t=T)
        CHOICEW = PRf[:, 5376:5632].rearrange("p (t s) -> p t s", t=T)
        CHOICET = PRf[:, 5632:6144].rearrange("p (b t s) -> p b t s", b=2, t=T)

        stage_done = sem("stage_done")
        landed = [sem(f"tile_landed{i}") for i in range(RAW)]
        high_ready = sem("weights_high_ready")
        low_ready = sem("weights_low_ready")
        tile_used = sem("tile_used")
        x_high = sem("transposed_high_ready")
        x_low = sem("transposed_low_ready")
        const_in = sem("constants_loaded")
        rows_in = sem("ln_rows_loaded")
        ple_in = sem("ple_loaded")
        router_in = sem("router_loaded")
        hgn_in = sem("hgrn_gains_loaded")
        lb_in = sem("lower_bounds_loaded")
        sums_ready = sem("sums_ready")
        rsqrt_ready = sem("rsqrt_ready")
        squares = sem("squares_summed")
        scale_ready = sem("token_scale_ready")
        act_evac = sem("product_read_by_scalar")
        dve_evac = sem("product_read_by_vector")
        turned = sem("bank_turned")
        qk_turned = sem("qk_turned")
        qk_copied = sem("qk_copied")
        scores_full = sem("scores_full")
        scores_read = sem("scores_read")
        max_ready = sem("max_ready")
        probs_ready = sem("probs_ready")
        probs_turned = sem("probs_turned")
        probs_act = sem("probs_read_by_scalar")
        probs_dve = sem("probs_read_by_vector")
        values_full = sem("values_full")
        values_read = sem("values_read")
        dve_to_act = sem("vector_to_scalar")
        act_to_dve = sem("scalar_to_vector")
        dve_to_pe = sem("vector_to_tensor")
        pe_to_dve = sem("tensor_to_vector")
        stick_scores = sem("stick_scores_full")
        kv_full = sem("kv_full")
        state_ready = sem("state_ready")
        state_used = sem("state_used")
        xh_ready = sem("expert_hidden_ready")
        xh_turned = sem("expert_hidden_turned")
        xh_copied = sem("expert_hidden_copied")
        silu_ready = sem("silu_ready")
        xsilu_ready = sem("expert_silu_ready")
        hid_high = sem("hidden_high_ready")
        hid_low = sem("hidden_low_ready")
        xh_high = sem("expert_hidden_high_ready")
        hidden_ready = sem("hidden_ready")
        hid_turned = sem("hidden_turned")
        down_read = sem("down_read")
        stick_gate = sem("stick_gate_read")
        gathered = sem("gathered")
        gathered_high = sem("gathered_high_ready")
        gathered_read = sem("gathered_low_ready")
        choice_ready = sem("choice_ready")
        choice_turned = sem("choice_turned")
        choice_copied = sem("choice_copied")
        spread_full = sem("spread_full")
        spread_read = sem("spread_read")
        passes_ready = sem("passes_ready")
        out_sem = sem("out_written")

        class Count:

            def __init__(self):
                self.n = {}

            def of(self, name):
                return self.n.get(name, 0)

            def add(self, name, k=1):
                self.n[name] = self.n.get(name, 0) + k
                return self.n[name]

        for before, st in zip(stages, stages[1:]):
            if before["kind"] == "turn" and st["kind"] in ("product", "mlp"):
                before["open"] = True
                st["turned_banks"] = before["chunks"] // 2
        barriers = lambda n: 3 * sum("open" not in st for st in stages[:n])

        def finish_stage(eng, n):
            if "open" in stages[n]:
                return
            eng.drain().then_inc(stage_done, 1)
            eng.wait_ge(stage_done, barriers(n + 1))

        def heads(ap, g, d):
            return ap.rearrange("p (g d) -> p g d", g=g, d=d)

        def pair_cols(use, n):
            if use == "A":
                return n * P, 512 + n * P, [1024 + n * P] * 2, P
            if use == "C":
                return n * P, 512 + n * P, [1024 + n * P, 1024 + n * P + HD], HD
            if use == "W":
                g = n // 2
                return n * P, 1536 + g * P, [1280 + g * HD] * 2, HD
            return 1536 + n * P, 3584, None, 0

        N_PAIRS = dict(A=4, C=4, W=8, I=2)

        N_LOADS = 25

        def gain_col(gain, k):
            name, l = gain
            return GAINS[:, ("attn_norm", "mlp_norm", "ple_norm").index(name) * DEPTH + l, k:k + 1]

        J = D_EXP // NB
        h = 0
        for st in stages:
            st["h0"] = h
            if st["kind"] != "experts":
                h += len(st.get("tiles", []))
        STATIC = h
        PAIR = 2 * (3 * J * 2)
        SPREAD_AT = 3
        GATHER_AT = PAIR // 2 - 4
        assert PAIR % RAW == 0 and PAIR % SPLIT == 0

        def tile_view(buffer, slot, tile):
            return buffer[:, slot, 0:tile["rows"] * tile["width"]].rearrange("p (k c) -> p k c", k=tile["rows"])

        def silus_before(stage):
            return sum(st["tiles"][-1]["block"] + 1 for st in stages if st["kind"] == "mlp" and st["h0"] < stage["h0"])

        static_tiles = [tile for st in stages if st["kind"] != "experts" for tile in st.get("tiles", [])]

        seen = 0
        for st in stages:
            st["qk_before"] = seen
            seen += {"pairs": N_PAIRS.get(st.get("use"), 0), "sticks": 4, "retention": RET_HEADS,
                     "hgrn_heads": HG_HEADS}.get(st["kind"], 0)

        block = ctx.enter_context(nc.Block())

        @block.sync
        def _(sp):
            for h, tile in enumerate(static_tiles):
                if h >= RAW:
                    sp.wait_ge(low_ready, h - RAW + 1)
                src = a[tile["name"]][tile["layer"], tile["row"]:tile["row"] + tile["rows"] * P,
                                      tile["col"]:tile["col"] + tile["width"]].rearrange("(k p) c -> p k c", p=P)
                sp.dma_start(tile_view(raw, h % RAW, tile), src).then_inc(landed[h % RAW], 16)
            for st in stages:
                if st["kind"] == "experts":
                    def load(h, expert, done=0):
                        tile = st["tiles"][h % (PAIR // 2)]
                        src = a[tile["name"]][tile["layer"], bass.ds(expert, 1), tile["row"]:tile["row"] + tile["rows"] * P,
                                              tile["col"]:tile["col"] + tile["width"]].rearrange("e (k p) c -> p (e k) c", p=P)
                        sp.wait_ge(low_ready, STATIC + h - RAW + 1 + done)
                        sp.dma_start(tile_view(raw, (STATIC + h) % RAW, tile), src).then_inc(landed[(STATIC + h) % RAW], 16)

                    for h in range(SPLIT - 1):
                        load(h, 0)
                    sp.wait_ge(passes_ready, 1)
                    passes = sp.value_load(NPASS[0:1, 0:1], min_val=1, max_val=T)
                    with sp.Fori(0, passes * (N_EXPERTS // 2)) as i:
                        for h in range(SPLIT - 1, PAIR + SPLIT - 1):
                            load(h, (i * 2 + h // (PAIR // 2)) % N_EXPERTS, i * PAIR)
            sp.wait_ge(stage_done, barriers(len(stages)))
            sp.dma_start(out[0].rearrange("(t p) d -> p t d", p=P), X[:]).then_inc(out_sem, 16)
            sp.wait_ge(out_sem, 16)

        @block.tensor
        def _(pe):
            c = Count()
            ident = C("ident")
            history = []

            def tile_products(h, tile, out_of, lhs, first, last, done=0):
                pe.wait_ge(low_ready, h + 1 + done)
                high, low = tile_view(WH, h % SPLIT, tile), tile_view(WL, h % SPLIT, tile)
                for k in range(tile["rows"]):
                    begin, end = first and k == 0, last and k == tile["rows"] - 1
                    for t in range(len(out_of)):
                        nc.tensor.matmul(out_of[t], lhs(0, k, t), high[:, k], start=begin, stop=False)
                        nc.tensor.matmul(out_of[t], lhs(0, k, t), low[:, k], start=False, stop=False)
                        mm = nc.tensor.matmul(out_of[t], lhs(1, k, t), high[:, k], start=False, stop=end)
                mm.then_inc(tile_used, 1)

            def wait_turned(st, n):
                if "turned_banks" in st and n < 2:
                    pe.wait_ge(x_low, c.of("x_low") - st["turned_banks"] + min(2 * (n + 1), st["turned_banks"]))

            def product(st):
                x = buf[st["lhs"]]
                for n, tile in enumerate(st["tiles"]):
                    wait_turned(st, n)
                    if tile["k"] == 0:
                        g = len(history)
                        if g >= 2:
                            na = sum(h[0] for h in history[:g - 1])
                            nd = sum(h[1] for h in history[:g - 1])
                            if na:
                                pe.wait_ge(act_evac, na)
                            if nd:
                                pe.wait_ge(dve_evac, nd)
                        history.append({"copy": (1, 1), "gate": (1, 0)}.get(st["use"], (0, 1)))
                    tile_products(st["h0"] + n, tile, [PS[:, 2 * (g % 2) + t, 0:tile["width"]] for t in range(T)],
                                  lambda part, k, t: x[part][:, tile["k"] + k, t * P:(t + 1) * P],
                                  tile["k"] == 0, tile["last"])

            def turn(st):
                src = buf[st["src"]]
                for b in range((st["chunks"] + 1) // 2):
                    for k in (2 * b, 2 * b + 1):
                        for t in range(T):
                            tr = nc.tensor.transpose(PS[:, 4 + b, (k % 2) * S + t * P:(k % 2) * S + (t + 1) * P],
                                                     src[:, t, k * P:(k + 1) * P], ident)
                    tr.then_inc(turned, 1)
                c.add("x_low", st["chunks"] // 2)

            def start_turn_qk(q0, k0):
                n = c.of("qk")
                if n:
                    pe.wait_ge(qk_copied, n)
                for i, (col, t) in enumerate([(q0, 0), (q0, 1), (k0, 0), (k0, 1)]):
                    tr = nc.tensor.transpose(PS[:, 0, i * P:(i + 1) * P], PR[:, t, col:col + P], ident)
                tr.then_inc(qk_turned, 1)
                c.add("qk")

            def turn_qk(q0, k0):
                start_turn_qk(q0, k0)
                pe.wait_ge(qk_copied, c.of("qk"))
                return QKT[:, (c.of("qk") - 1) % 2]

            def pairs(st):
                use = st["use"]
                N = N_PAIRS[use]

                def front(n):
                    q0, k0, _, _ = pair_cols(use, n)
                    z = turn_qk(q0, k0)
                    m = c.add("scores")
                    if m > 2:
                        pe.wait_ge(scores_read, m - 2)
                    for t in range(T):
                        for h in range(2):
                            rows = slice(h * HD, (h + 1) * HD)
                            mm = nc.tensor.matmul(PS[:, 1 + 2 * (m % 2) + h, t * S:(t + 1) * S],
                                                  z[rows, t * P:(t + 1) * P], z[rows, S:2 * S], start=True, stop=True)
                    mm.then_inc(scores_full, 1)

                def turn_probs():
                    m = c.add("probs")
                    pe.wait_ge(probs_ready, m)
                    if m > 1:
                        pe.wait_ge(probs_act, m - 1)
                        pe.wait_ge(probs_dve, m - 1)
                    for h in range(2):
                        for kt, t in ((0, 0), (0, 1), (1, 1)):
                            tr = nc.tensor.transpose(PS[:, 5 + h, (kt + t) * P:(kt + t + 1) * P],
                                                     SM[:, m % 2, 2 * t + h, kt * P:(kt + 1) * P], ident)
                    tr.then_inc(probs_turned, 1)

                def values(n):
                    m = c.of("probs")
                    _, _, v0, vw = pair_cols(use, n)
                    pe.wait_ge(probs_act, m)
                    pe.wait_ge(probs_dve, m)
                    if m > 1:
                        pe.wait_ge(values_read, m - 1)
                    for t in range(T):
                        for h in range(2):
                            for kt in range(t + 1):
                                o = (2 * t + h) * vw
                                mm = nc.tensor.matmul(PS[:, 7, o:o + vw], PT[:, h, (kt + t) * P:(kt + t + 1) * P],
                                                      PR[:, kt, v0[h]:v0[h] + vw], start=kt == 0, stop=kt == t)
                    mm.then_inc(values_full, 1)

                front(0)
                for n in range(N + 1):
                    if n >= 1 and use != "I":
                        turn_probs()
                    if n + 1 < N:
                        front(n + 1)
                    if n >= 1 and use != "I":
                        values(n - 1)

            def sticks(st):
                def scores():
                    pe.wait_ge(qk_copied, c.of("qk"))
                    z = QKT[:, (c.of("qk") - 1) % 2]
                    for h in range(2):
                        rows = slice(h * HD, (h + 1) * HD)
                        nc.tensor.matmul(PS[:, 1 + h, 0:S], z[rows, S:S + P], z[rows, 0:S], start=True, stop=True)
                        mm = nc.tensor.matmul(PS[:, 1 + h, S:S + P], z[rows, S + P:2 * S], z[rows, P:S],
                                              start=True, stop=True)
                    mm.then_inc(stick_scores, 1)

                start_turn_qk(0, 512)
                scores()
                for n in range(4):
                    tile = st["tiles"][n]
                    if tile["k"] == 0 and c.add("stick_gate") > 1:
                        pe.wait_ge(stick_gate, c.of("stick_gate") - 1)
                    tile_products(st["h0"] + n, tile, [PS[:, 3 + t, :] for t in range(T)],
                                  lambda part, k, t: HT[part][:, tile["k"] + k, t * P:(t + 1) * P],
                                  tile["k"] == 0, tile["last"])
                    if n < 3:
                        start_turn_qk((n + 1) * P, 512 + (n + 1) * P)
                    pe.wait_ge(dve_to_pe, c.add("dve_to_pe"))
                    for h in range(2):
                        lg = S1.rearrange("p t d -> p (t d)")[:, h * 384:(h + 1) * 384]
                        nc.tensor.matmul(PS[:, 5 + h, 0:P], C("later"), lg[:, 0:P], start=True, stop=True)
                        nc.tensor.matmul(PS[:, 5 + h, P:S], C("later"), lg[:, P:S], start=True, stop=False)
                        nc.tensor.matmul(PS[:, 5 + h, P:S], C("ones"), lg[:, S:S + P], start=False, stop=True)
                        mm = nc.tensor.matmul(PS[:, 5 + h, S:S + P], C("later"), lg[:, S:S + P], start=True, stop=True)
                    mm.then_inc(pe_to_dve, 1)
                    pe.wait_ge(dve_to_pe, c.add("dve_to_pe"))
                    if n < 3:
                        scores()
                    for t in range(T):
                        for h in range(2):
                            for kt in range(t + 1):
                                o = (2 * t + h) * HD
                                v0 = 1024 + n * P + h * HD
                                mm = nc.tensor.matmul(PS[:, 7, o:o + HD],
                                                      S0.rearrange("p t d -> p (t d)")[:, h * 384 + (kt + t) * P:h * 384 + (kt + t + 1) * P],
                                                      PR[:, kt, v0:v0 + HD], start=kt == 0, stop=kt == t)
                    mm.then_inc(pe_to_dve, 1)
                    pe.wait_ge(dve_to_pe, c.add("dve_to_pe"))

            def retention(st):
                def scores(n):
                    z = turn_qk(n * P, 512 + n * P)
                    nc.tensor.matmul(PS[:, 1 + n % 2, 0:S], z[:, S:S + P], z[:, 0:S], start=True, stop=True)
                    nc.tensor.matmul(PS[:, 1 + n % 2, S:S + P], z[:, S + P:2 * S], z[:, P:S], start=True,
                                     stop=True).then_inc(pe_to_dve, 1)

                scores(0)
                for n in range(RET_HEADS):
                    if n + 1 < RET_HEADS:
                        scores(n + 1)
                    pe.wait_ge(dve_to_pe, c.add("dve_to_pe", 1 if n < 2 else 2))
                    for t in range(T):
                        for kt in range(t + 1):
                            mm = nc.tensor.matmul(PS[:, 6 + n % 2, t * S:(t + 1) * S],
                                                  PT[:, n % 2, (kt + t) * P:(kt + t + 1) * P],
                                                  PR[:, kt, 1024 + n * S:1024 + (n + 1) * S], start=kt == 0, stop=kt == t)
                    mm.then_inc(pe_to_dve, 1)
                c.add("dve_to_pe", 2)

            def hgrn_decay(st):
                for t in range(T):
                    for nb in range(2):
                        nc.tensor.matmul(PS[:, 2 * t + nb, :], C("block_upto"), S0[:, t, nb * NB:(nb + 1) * NB],
                                         start=True, stop=True)
                        nc.tensor.matmul(PS[:, 4 + 2 * t + nb, :], C("block_later"), S0[:, t, nb * NB:(nb + 1) * NB],
                                         start=True, stop=True)

            def hgrn_heads(st):
                per_tile = P // HG_BLOCK

                def scores(n):
                    pe.wait_ge(qk_copied, c.of("qk"))
                    z = QKT[:, (c.of("qk") - 1) % 2]
                    for t in range(T):
                        nc.tensor.matmul(PS[:, 1, t * P:(t + 1) * P], z[:, S + t * P:S + (t + 1) * P],
                                         z[:, t * P:(t + 1) * P], start=True, stop=True)
                    for t in range(T):
                        mm = nc.tensor.matmul(PS[:, 1, S + t * per_tile:S + (t + 1) * per_tile],
                                              S0[:, t, n * P:(n + 1) * P], C("in_block"), start=True, stop=True)
                    mm.then_inc(pe_to_dve, 1)
                    return z

                def turn_out(n):
                    for t in range(T):
                        tr = nc.tensor.transpose(PS[:, 7, t * P:(t + 1) * P], PR[:, t, 1024 + n * P:1024 + (n + 1) * P], ident)
                    tr.then_inc(pe_to_dve, 1)

                start_turn_qk(0, 1024)
                next_z = scores(0)
                for n in range(HG_HEADS):
                    cols = slice(n * P, (n + 1) * P)
                    z = next_z
                    for b in range(2 * per_tile - 1):
                        t, r = b // per_tile, b % per_tile
                        rows = slice(32 * (r // 2), 32 * (r // 2) + 32)
                        kst = (S1, S2)[r % 2]
                        u = 2 * t + r % 2
                        mm = nc.tensor.matmul(PS[:, 2 + r // 2, u * P:(u + 1) * P], kst[rows, t, cols],
                                              PR[rows, t, 2048 + n * P:2048 + (n + 1) * P], start=True, stop=True,
                                              tile_position=(rows.start, 0))
                    mm.then_inc(kv_full, 1)
                    pe.wait_ge(dve_to_pe, c.add("dve_to_pe", min(n + 1, 3)))
                    for b in range(2 * per_tile):
                        t, r = b // per_tile, b % per_tile
                        if r == 0:
                            nc.tensor.matmul(PS[:, 6, t * P:(t + 1) * P], PR[:, t, 2048 + n * P:2048 + (n + 1) * P],
                                             HA[:, t, :], start=True, stop=b == 0, skip_group_check=True)
                        if b == 0:
                            if n:
                                turn_out(n - 1)
                            continue
                        m = c.add("state")
                        pe.wait_ge(state_ready, m)
                        mm = nc.tensor.matmul(PS[:, 6, b * HG_BLOCK:(b + 1) * HG_BLOCK], STATE[:, m % 4],
                                              z[:, b * HG_BLOCK:(b + 1) * HG_BLOCK], start=False,
                                              stop=True, skip_group_check=True)
                        mm.then_inc(state_used, 1)
                        if n < HG_HEADS - 1 and b == 2:
                            start_turn_qk((n + 1) * P, 1024 + (n + 1) * P)
                        if n < HG_HEADS - 1 and b == 6:
                            next_z = scores(n + 1)
                pe.wait_ge(dve_to_pe, c.add("dve_to_pe", 2))
                turn_out(HG_HEADS - 1)
                c.add("dve_to_pe")

            def index_select(st):
                pe.wait_ge(dve_to_pe, c.add("dve_to_pe"))
                for t in range(T):
                    for kt in range(T):
                        tr = nc.tensor.transpose(PS[:, 4 + t, kt * P:(kt + 1) * P], S1[:, t, kt * P:(kt + 1) * P], ident)
                tr.then_inc(pe_to_dve, 1)
                pe.wait_ge(dve_to_pe, c.add("dve_to_pe"))
                n0, _ = const_at["upto"]
                for t in range(T):
                    e = lambda kt: S1[:, t, 512 + kt * P:512 + (kt + 1) * P]
                    nc.tensor.matmul(PS[:, 6, t * S:(t + 1) * S], e(0), CONST[:, n0:n0 + S], start=True, stop=False)
                    mm = nc.tensor.matmul(PS[:, 6, t * S + P:(t + 1) * S], e(1), C("upto"), start=False, stop=True)
                mm.then_inc(pe_to_dve, 1)

            def mlp(st):
                two = st["use"] == "swiglu"
                tiles = st["tiles"]
                n_blocks = tiles[-1]["block"] + 1
                for n, tile in enumerate(tiles):
                    wait_turned(st, n)
                    j, w = tile["block"], tile["width"]
                    bank = 0 if tile["role"] == "gate" else (2 if two else 2 * (j % 2))
                    turned_block = block_to_turn(tiles, n)
                    if turned_block:
                        tb = turned_block["block"]
                        pe.wait_ge(hidden_ready, c.add("hidden"))
                        for i in range(turned_block["rows"]):
                            for t in range(T):
                                at = (i % 2) * S + t * P
                                tr = nc.tensor.transpose(PS[:, (2 if two else 2 * (tb % 2)) + i // 2, at:at + P],
                                                         HID[:, tb % 2, t, i * P:(i + 1) * P], ident)
                        tr.then_inc(hid_turned, 1)
                    if tile["role"] != "down":
                        if tile["k"] == 0:
                            if tile["role"] == "gate":
                                if j >= 1:
                                    pe.wait_ge(silu_ready, silus_before(st) + j)
                            elif j >= (1 if two else 2):
                                pe.wait_ge(hid_low, c.of("hid"))
                        tile_products(st["h0"] + n, tile, [PS[:, bank + t, 0:w] for t in range(T)],
                                      lambda part, k, t: HT[part][:, tile["k"] + k, t * P:(t + 1) * P],
                                      tile["k"] == 0, tile["last"])
                        continue
                    if tile["first"]:
                        pe.wait_ge(hid_low, c.add("hid"))
                    tile_products(st["h0"] + n, tile, [PS[:, 4 + 2 * t + tile["half"], :] for t in range(T)],
                                  lambda part, k, t: HIDT[part][:, j % 2, k, t * P:(t + 1) * P],
                                  j == 0, j == n_blocks - 1)

            def route(st):
                pe.wait_ge(dve_to_pe, c.add("dve_to_pe"))
                for t in range(T):
                    for k in range(KD):
                        for n, (xp, wp) in enumerate(((0, 0), (0, 1), (1, 0))):
                            mm = nc.tensor.matmul(PS[:, 0, t * 8:(t + 1) * 8], HT[xp][:, k, t * P:(t + 1) * P],
                                                  RTR[wp][:, k, :], start=k == 0 and n == 0, stop=k == KD - 1 and n == 2)
                mm.then_inc(pe_to_dve, 1)
                pe.wait_ge(dve_to_pe, c.add("dve_to_pe"))
                nc.tensor.matmul(PS[:, 1, 0:8], C("strict")[:, 0:P], ROUTE[:, 0, 1, 0:8], start=True, stop=True)
                nc.tensor.matmul(PS[:, 1, 8:16], C("ones"), ROUTE[:, 0, 1, 0:8], start=True, stop=False)
                nc.tensor.matmul(PS[:, 1, 8:16], C("strict")[:, 0:P], ROUTE[:, 1, 1, 0:8], start=False, stop=True)
                nc.tensor.matmul(PS[:, 1, 16:24], C("ones"), ROUTE[:, 0, 1, 0:8], start=True, stop=False)
                nc.tensor.matmul(PS[:, 1, 16:24], C("ones"), ROUTE[:, 1, 1, 0:8], start=False,
                                 stop=True).then_inc(pe_to_dve, 1)

            def experts(st):
                pe.wait_ge(passes_ready, 1)
                passes = pe.value_load(NPASS[0:1, 0:1], min_val=1, max_val=T)
                pe.drain().then_inc(choice_turned, 1)

                def gather(m, kk):
                    if kk:
                        pe.wait_ge(gathered_read, m * 2 + 1)
                    else:
                        pe.wait_ge(choice_ready, m + 1)
                    for k in range(4):
                        f = kk * 4 + k
                        for t in range(T):
                            mm = nc.tensor.matmul(PS[:, 5, k * P:(k + 1) * P], X[:, t, f * P:(f + 1) * P],
                                                  CHOICE[:, t, :], start=t == 0, stop=t == T - 1)
                    mm.then_inc(gathered, 1)

                def turn_choice(m):
                    pe.wait_ge(gathered_read, m * 2 + 2)
                    for t in range(T):
                        tr = nc.tensor.transpose(PS[:, 5, t * P:(t + 1) * P], CHOICEW[:, t, :], ident)
                    tr.then_inc(choice_turned, 1)

                def spread(m, half, s):
                    pe.wait_ge(spread_read, m * 4 + s + 1)
                    nc.tensor.matmul(PS[:, 5, :], CHOICET[:, half, s // 2, :], YE[:, s % 2, :], start=True,
                                     stop=True).then_inc(spread_full, 1)

                gather(0, 0)
                gather(0, 1)
                turn_choice(0)
                with pe.Fori(0, passes * (N_EXPERTS // 2)) as i:
                    for half in range(2):
                        m = i * 2 + half
                        pe.wait_ge(choice_copied, m + 1)
                        for n, tile in enumerate(st["tiles"]):
                            h = STATIC + half * (PAIR // 2) + n
                            j = tile["block"]
                            par = (half * J + j) % 2
                            if n == SPREAD_AT:
                                pe.wait_ge(down_read, m + 1)
                            if SPREAD_AT <= n < SPREAD_AT + 4:
                                spread(m, 1 - half, n - SPREAD_AT)
                            if n == GATHER_AT:
                                pe.wait_ge(spread_read, m * 4 + 5)
                            if n in (GATHER_AT, GATHER_AT + 1):
                                gather(m + 1, n - GATHER_AT)
                            if n == GATHER_AT + 2:
                                turn_choice(m + 1)
                            turned_block = block_to_turn(st["tiles"], n)
                            if turned_block:
                                tb = turned_block["block"]
                                pe.wait_ge(xh_ready, m * J + tb + 3)
                                for x in range(4):
                                    tr = nc.tensor.transpose(PS[:, 4, x * P:(x + 1) * P],
                                                             HID2[:, (half * J + tb) % 2, x * P:(x + 1) * P], ident)
                                tr.then_inc(xh_turned, 1)
                            if tile["role"] != "down":
                                if tile["k"] == 0:
                                    pe.wait_ge(xh_ready, m * J + j + 1)
                                bank = par if tile["role"] == "gate" else 2 + par
                                tile_products(h, tile, [PS[:, bank, :]], lambda part, k, t: XG[part][:, tile["k"] + k, :],
                                              tile["k"] == 0, tile["last"], i * PAIR)
                            else:
                                if tile["first"]:
                                    pe.wait_ge(xh_copied, m * J + j + 1)
                                tile_products(h, tile, [PS[:, 6 + tile["half"], :]],
                                              lambda part, k, t: HIDT2[part][:, par, k, :], j == 0, j == J - 1, i * PAIR)
                n_experts = passes * N_EXPERTS
                pe.wait_ge(down_read, n_experts + 1)
                for s in range(4):
                    spread(n_experts, 1, s)

            run = dict(product=product, turn=turn, pairs=pairs, sticks=sticks, retention=retention,
                       hgrn_decay=hgrn_decay, hgrn_heads=hgrn_heads, index_select=index_select, mlp=mlp,
                       route=route, experts=experts)
            for n, st in enumerate(stages):
                if st["kind"] in run:
                    run[st["kind"]](st)
                finish_stage(pe, n)

        @block.scalar
        def _(act):
            c = Count()
            split = [0]

            def high_part(h, tile, done=0):
                act.wait_ge(landed[h % RAW], (h // RAW + 1 + (done and done[0])) * 16)
                if h >= SPLIT:
                    act.wait_ge(tile_used, h - SPLIT + 1 + (done and done[1]))
                nc.scalar.activation(tile_view(WH, h % SPLIT, tile), tile_view(raw, h % RAW, tile),
                                     ACT.Copy).then_inc(high_ready, 1)

            def split_to(n):
                while split[0] < min(n, STATIC):
                    high_part(split[0], static_tiles[split[0]])
                    split[0] += 1

            def load_rows(n):
                g, b, l = LN_ROWS[n]
                for i, name in enumerate((g, b)):
                    row = a[name].rearrange("(o d) -> o d", o=1) if l is None else a[name][l:l + 1, :]
                    act.dma_start(S2[:, i], row[0].partition_broadcast(P)).then_inc(rows_in, 16)

            def setup(st):
                k = 0
                loads = [(CONST[:], a["shape_constants"])]
                for i, (name, l) in enumerate([(m, l) for m in ("attn_norm", "mlp_norm", "ple_norm") for l in range(DEPTH)]):
                    loads.append((GAINS[:, i], a[name][l].rearrange("(k p) -> p k", p=P)))
                for i, name in enumerate(("a_q_norm", "a_k_norm", "c_q_norm", "c_k_norm", "idx_k_norm")):
                    for l in range(DEPTH):
                        loads.append((HG[:, l, i], a[name][l].partition_broadcast(P)))
                for l in range(DEPTH):
                    loads.append((SUBLN[:, l], a["a_subln"][l].partition_broadcast(P)))
                    loads.append((SINK[:, l], a["swa_sinks_2"][l].partition_broadcast(P)))
                    loads.append((LAMB[:, l], a["a_lambda"][l].rearrange("i d -> (i d)").partition_broadcast(P)
                                  .rearrange("p (i d) -> p i d", i=4)))
                loads.append((POSI[:], a["positions"][0].rearrange("(t p) -> p t", p=P)))
                loads.append((X[:], a["x"][0].rearrange("(t p) d -> p t d", p=P)))
                for dst, src in loads:
                    act.dma_start(dst, src, allow_slow_non_contiguous=True).then_inc(const_in, 16)
                assert len(loads) == N_LOADS, len(loads)
                act.wait_ge(dve_to_act, c.add("dve_to_act"))
                nc.scalar.activation(COS.rearrange("p t f -> p (t f)"), COS.rearrange("p t f -> p (t f)"), ACT.Sin)
                nc.scalar.activation(SIN.rearrange("p t f -> p (t f)"), SIN.rearrange("p t f -> p (t f)"), ACT.Sin)
                nc.scalar.activation(LAME.rearrange("p l i -> p (l i)"), LAME.rearrange("p l i -> p (l i)"),
                                     ACT.Exp).then_inc(act_to_dve, 1)

            def layer_norm(st):
                if st["n"] == 2 * DEPTH - 1:
                    act.dma_start(ROUTER, a["moe_router_2"][0].rearrange("(k p) e -> p k e", p=P)).then_inc(router_in, 16)

            def norm_squares(st, n):
                if st.get("norm") and n == 0:
                    for t in range(T):
                        nc.scalar.activation(S1[:, t], X[:, t], ACT.Square, accum_out=SQ[:, t:t + 1])
                    act.drain().then_inc(squares, 1)

            def norm_wait(st, n):
                if st.get("norm") and n == 1:
                    act.wait_ge(scale_ready, c.add("scale"))

            def token_scaled(st, out_, in_, func):
                if not st.get("scaled"):
                    return nc.scalar.activation(out_, in_, func)
                for t in range(T):
                    i = nc.scalar.activation(out_[:, t], in_[:, t], func, scale=RX[:, t:t + 1])
                return i

            def turn(st):
                dst = buf[st["dst"]][0]
                if "load" in st:
                    load_rows(st["load"])
                for b in range(st["chunks"] // 2):
                    act.wait_ge(turned, c.add("turned"))
                    if st["gain"] is None:
                        i = nc.scalar.activation(dst[:, 2 * b:2 * b + 2].rearrange("p k s -> p (k s)"), PS[:, 4 + b], ACT.Copy)
                    else:
                        for k in (2 * b, 2 * b + 1):
                            i = nc.scalar.activation(dst[:, k], PS[:, 4 + b, (k % 2) * S:(k % 2 + 1) * S], ACT.Copy,
                                                     scale=gain_col(st["gain"], k))
                    i.then_inc(x_high, 1)

            def beside(st, step):
                if step.split()[0] in ("qk_squares", "ret_rotary0", "index_norm"):
                    act.drain().then_inc(act_to_dve, 1)
                if step.startswith("out_squares"):
                    first = 2048 if step.endswith("ret") else 3072
                    cols = PR[:, :, first:first + D]
                    nc.scalar.activation(cols, cols, ACT.Silu).then_inc(act_to_dve, 1)
                if not step.startswith("forget"):
                    return
                k, hf = int(step[6:]), PR[:, :, 1024:2048]
                if k == 0:
                    act.wait_ge(dve_to_act, c.add("dve_to_act"))
                    act.drain()
                    nc.scalar.activation(hf, hf, ACT.Sigmoid).then_inc(act_to_dve, 1)
                    if st["layer"] > 0:
                        for i in range(DEPTH):
                            act.dma_start(S2[:, i], a["hgrn_lower_bounds_2"][i].partition_broadcast(P)).then_inc(lb_in, 16)
                if k == 2 and st["layer"] > 0:
                    act.wait_ge(dve_to_act, c.add("dve_to_act"))
                    nc.scalar.activation(S2[:, 0], S2[:, 0], ACT.Exp).then_inc(act_to_dve, 1)
                if k == (3 if st["layer"] == 0 else 7):
                    act.wait_ge(dve_to_act, c.add("dve_to_act"))
                    nc.scalar.activation(S0[:], S0[:], ACT.Ln)

            def product(st):
                if "load" in st:
                    load_rows(st["load"])
                if "ple" in st:
                    act.dma_start(PR[:, :, 0:256], a["p"][st["ple"], 0].rearrange("(t p) d -> p t d", p=P)).then_inc(ple_in, 16)
                col = st.get("first", 0)
                for n, tile in enumerate(st["tiles"]):
                    h, w = st["h0"] + n, tile["width"]
                    split_to(h + SPLIT)
                    norm_squares(st, n)
                    norm_wait(st, n)
                    if n in st.get("beside", {}):
                        beside(st, st["beside"][n])
                    if not tile["last"]:
                        continue
                    g = c.add("block") - 1
                    if st["use"] in ("copy", "gate"):
                        act.wait_ge(tile_used, h + 1)
                    if st["use"] == "copy":
                        nc.scalar.activation(PR[:, 0, col:col + w], PS[:, 2 * (g % 2), 0:w], ACT.Copy,
                                             scale=RX[:, 0:1] if st.get("scaled") else 1.0).then_inc(act_evac, 1)
                    if st["use"] == "gate":
                        token_scaled(st, buf[st.get("gate", "S0")][:, :, col:col + w],
                                     PS[:, 2 * (g % 2):2 * (g % 2) + 2, 0:w], ACT.Sigmoid).then_inc(act_evac, 1)
                    col += w
                split_to(st["h0"] + len(st["tiles"]) + SPLIT - 1)
                if "ple" in st:
                    act.wait_ge(ple_in, 16 * (st["ple"] + 1))

            def copy_qk():
                n = c.add("qk")
                act.wait_ge(qk_turned, n)
                nc.scalar.activation(QKT[:, (n - 1) % 2], PS[:, 0, :], ACT.Copy).then_inc(qk_copied, 1)

            def pairs(st):
                use = st["use"]
                N = N_PAIRS[use]
                copy_qk()
                for n in range(N + 1):
                    if n >= 1 and use != "I":
                        act.wait_ge(probs_turned, c.add("turned_probs"))
                        nc.scalar.activation(PT[:, 0], PS[:, 5, 0:384], ACT.Copy).then_inc(probs_act, 1)
                    if n + 1 < N:
                        copy_qk()
                    if use == "I":
                        continue
                    if n < N:
                        m = c.add("probs")
                        act.wait_ge(max_ready, m)
                        for i in range(4):
                            nc.scalar.activation(SM[:, m % 2, i], SM[:, m % 2, i], ACT.Exp, bias=NMX[:, m % 2, i:i + 1],
                                                 accum_out=SUM[:, m % 2, i:i + 1])
                        if use == "W":
                            nc.scalar.activation(EDS[:, m % 2], SINKD[:, m % 2], ACT.Exp)
                        act.drain().then_inc(probs_ready, 1)

            def sticks(st):
                copy_qk()
                for n in range(4):
                    z = PS[:, 1:3, 0:384]
                    w = S2f[:, 0:768].rearrange("p (h k) -> p h k", h=2)
                    act.wait_ge(stick_scores, c.add("stick_scores"))
                    nc.scalar.activation(w, z, ACT.Abs, scale=SCALE).then_inc(act_to_dve, 1)
                    act.drain()
                    nc.scalar.activation(w, w, ACT.Exp, scale=-1.0)
                    act.drain()
                    nc.scalar.activation(w, w, ACT.Ln, bias=1.0).then_inc(act_to_dve, 1)
                    split_to(st["h0"] + n + SPLIT)
                    if n < 3:
                        copy_qk()
                    act.wait_ge(dve_to_act, c.add("dve_to_act"))
                    nc.scalar.activation(S0f[:, 768:1536], S0f[:, 768:1536], ACT.Exp).then_inc(act_to_dve, 1)
                    tile = st["tiles"][n]
                    if tile["last"]:
                        act.wait_ge(tile_used, st["h0"] + n + 1)
                        token_scaled(st, G[:, :, tile["block"] * NB:(tile["block"] + 1) * NB], PS[:, 3:5, :],
                                     ACT.Sigmoid).then_inc(stick_gate, 1)
                split_to(st["h0"] + len(st["tiles"]) + SPLIT - 1)

            def retention(st):
                if st["layer"] == 0:
                    for l in range(DEPTH):
                        act.dma_start(HGN[:, l], a["hgrn_norm_g_2"][l].partition_broadcast(P)).then_inc(hgn_in, 16)
                for n in range(RET_HEADS):
                    lg = math.log(1.0 - 2.0 ** (-5.0 - n))
                    nc.scalar.activation(S1f[:, n * 384:(n + 1) * 384], C("dist"), ACT.Exp, scale=lg).then_inc(act_to_dve, 1)
                for n in range(RET_HEADS):
                    copy_qk()

            def hgrn_scale(st):
                up, later = PS[:, 0:4].rearrange("p b c -> p (b c)"), PS[:, 4:8].rearrange("p b c -> p (b c)")
                nc.scalar.activation(S1f, up, ACT.Exp).then_inc(act_to_dve, 1)
                nc.scalar.activation(S2f, later, ACT.Exp).then_inc(act_to_dve, 1)
                act.wait_ge(dve_to_act, c.add("dve_to_act"))
                nc.scalar.activation(S1f, up, ACT.Exp, scale=-1.0).then_inc(act_to_dve, 1)

            def hgrn_heads(st):
                for n in range(HG_HEADS):
                    copy_qk()
                    act.wait_ge(dve_to_act, c.add("dve_to_act"))
                    nc.scalar.activation(DEC[:, n % 2], DEC[:, n % 2], ACT.Exp).then_inc(act_to_dve, 1)

            def mlp(st):
                two = st["use"] == "swiglu"
                for n, tile in enumerate(st["tiles"]):
                    h, j, w = st["h0"] + n, tile["block"], tile["width"]
                    turned_block = block_to_turn(st["tiles"], n)
                    if turned_block:
                        k, tb = turned_block["rows"], turned_block["block"]
                        bank = 2 if two else 2 * (tb % 2)
                        act.wait_ge(hid_turned, c.add("hid"))
                        nc.scalar.activation(HIDT[0][:, tb % 2, 0:k].rearrange("p k s -> p (k s)"),
                                             PS[:, bank:bank + 2].rearrange("p b c -> p (b c)")[:, 0:k * S],
                                             ACT.Copy).then_inc(hid_high, 1)
                    split_to(h + SPLIT)
                    norm_squares(st, n)
                    norm_wait(st, n)
                    if tile["role"] == "gate" and tile["last"]:
                        act.wait_ge(tile_used, h + 1)
                        nc.scalar.activation(SG[:, j % 2, :, 0:w], PS[:, 0:2, 0:w], ACT.Silu).then_inc(silu_ready, 1)
                    if not two and tile["role"] == "up" and tile["last"]:
                        act.wait_ge(tile_used, h + 1)
                        token_scaled(st, SG[:, j % 2], PS[:, 2 * (j % 2):2 * (j % 2) + 2],
                                     ACT.Relu).then_inc(silu_ready, 1)
                split_to(st["h0"] + len(st["tiles"]) + SPLIT - 1)

            def route(st):
                act.wait_ge(dve_to_act, c.add("dve_to_act"))
                nc.scalar.activation(ROUTE[:, :, 2, 0:8], ROUTE[:, :, 2, 0:8], ACT.Exp).then_inc(act_to_dve, 1)

            def experts(st):
                act.wait_ge(passes_ready, 1)
                passes = act.value_load(NPASS[0:1, 0:1], min_val=1, max_val=T)
                act.drain().then_inc(down_read, 1)

                def gather(m, kk):
                    act.wait_ge(gathered, m * 2 + kk + 1)
                    nc.scalar.activation(XG[0][:, 4 * kk:4 * kk + 4].rearrange("p k s -> p (k s)"), PS[:, 5, :],
                                         ACT.Copy).then_inc(gathered_high, 1)

                def copy_choice(m, half):
                    act.wait_ge(choice_turned, m + 2)
                    nc.scalar.activation(CHOICET[:, half].rearrange("p t s -> p (t s)"), PS[:, 5, 0:S],
                                         ACT.Copy).then_inc(choice_copied, 1)

                for h in range(SPLIT - 1):
                    high_part(STATIC + h, st["tiles"][h])
                gather(0, 0)
                gather(0, 1)
                copy_choice(0, 0)
                with act.Fori(0, passes * (N_EXPERTS // 2)) as i:
                    for half in range(2):
                        m = i * 2 + half
                        for n, tile in enumerate(st["tiles"]):
                            h, j = half * (PAIR // 2) + n, tile["block"]
                            par = (half * J + j) % 2
                            if n in (GATHER_AT, GATHER_AT + 1):
                                gather(m + 1, n - GATHER_AT)
                            if n == GATHER_AT + 2:
                                copy_choice(m + 1, 1 - half)
                            turned_block = block_to_turn(st["tiles"], n)
                            if turned_block:
                                tb = turned_block["block"]
                                act.wait_ge(xh_turned, m * J + tb + 1)
                                nc.scalar.activation(HIDT2[0][:, (half * J + tb) % 2].rearrange("p k s -> p (k s)"),
                                                     PS[:, 4, :], ACT.Copy).then_inc(xh_high, 1)
                            ahead = h + SPLIT - 1
                            high_part(STATIC + ahead, st["tiles"][ahead % (PAIR // 2)], (i * (PAIR // RAW), i * PAIR))
                            if tile["role"] == "gate" and tile["last"]:
                                act.wait_ge(tile_used, i * PAIR + STATIC + h + 1)
                                nc.scalar.activation(SG2[:, par], PS[:, par], ACT.Silu).then_inc(xsilu_ready, 1)
                        act.wait_ge(tile_used, i * PAIR + STATIC + (half + 1) * (PAIR // 2))
                        nc.scalar.activation(YE.rearrange("p b c -> p (b c)"), PS[:, 6:8].rearrange("p b c -> p (b c)"),
                                             ACT.Copy).then_inc(down_read, 1)

            run = dict(setup=setup, layer_norm=layer_norm, turn=turn, product=product, pairs=pairs, sticks=sticks,
                       retention=retention, hgrn_scale=hgrn_scale, hgrn_heads=hgrn_heads,
                       mlp=mlp, route=route, experts=experts,
                       swa_prepare=lambda st: load_rows(st["load"]))
            for n, st in enumerate(stages):
                if st["kind"] in run:
                    run[st["kind"]](st)
                finish_stage(act, n)

        rsqrts = [0]

        @block.vector
        def _(dve):
            c = Count()
            v = nc.vector
            split = [0]

            def low_part(h, tile, done=0):
                dve.wait_ge(high_ready, h + 1 + done)
                v.tensor_tensor(tile_view(WL, h % SPLIT, tile), tile_view(raw, h % RAW, tile),
                                tile_view(WH, h % SPLIT, tile).bitcast(F32), ALU.subtract).then_inc(low_ready, 1)

            def split_to(n):
                while split[0] < min(n, STATIC):
                    low_part(split[0], static_tiles[split[0]])
                    split[0] += 1

            def rsqrt(n, width):
                dve.drain()
                v.tensor_scalar(STAT[:, 0:n], STAT[:, 0:n], 1.0 / width, RMS_EPS, ALU.mult, ALU.add).then_inc(sums_ready, 1)
                rsqrts[0] += 1
                dve.wait_ge(rsqrt_ready, rsqrts[0])

            def group_norm(x, t, g, d, work):
                view = lambda b: b.rearrange("p t (g d) -> p t g d", g=g, d=d)
                v.tensor_tensor(work, x, x, ALU.mult)
                dve.drain()
                v.tensor_reduce(STAT[:, 0:t * g].rearrange("p (t g) -> p t g", t=t), view(work), AX, ALU.add)
                rsqrt(t * g, d)
                r = RSTD[:, 0:t * g].rearrange("p (t g) -> p t g", t=t).unsqueeze(3).broadcast_to([P, t, g, d])
                v.tensor_tensor(view(x), view(x), r, ALU.mult)
                dve.drain()

            def rope(x, g, half, cos, sin, w1, w2):
                view = lambda b: b.rearrange("p (g h d) -> p g h d", g=g, h=2, d=half)
                X4, A, B = view(x), view(w1), view(w2)
                cb = cos.unsqueeze(1).unsqueeze(1).broadcast_to([P, g, 2, half])
                sb_ = sin.unsqueeze(1).broadcast_to([P, g, half])
                v.tensor_tensor(A, X4, cb, ALU.mult)
                v.tensor_tensor(B[:, :, 0], X4[:, :, 1], sb_, ALU.mult)
                v.tensor_tensor(B[:, :, 1], X4[:, :, 0], sb_, ALU.mult)
                dve.drain()
                v.tensor_tensor(X4[:, :, 0], A[:, :, 0], B[:, :, 0], ALU.subtract)
                v.tensor_tensor(X4[:, :, 1], A[:, :, 1], B[:, :, 1], ALU.add)

            def setup(st):
                v.memset(STAT[:], 1.0)
                dve.wait_ge(const_in, 16 * N_LOADS)
                pos = SQ
                v.tensor_copy(pos[:], POSI[:])
                dve.drain()
                ang, n1, n2 = S1f[:, 0:64], S1f[:, 64:128], S1f[:, 128:192]
                for t in range(T):
                    v.tensor_scalar(ang[:, t * 32:(t + 1) * 32], C("inv_freq"), pos[:, t:t + 1], None, ALU.mult)
                dve.drain()
                for dst, turn_, shift in ((SIN, 0.0, 0.0), (COS, 0.25, math.pi / 2)):
                    d = dst.rearrange("p t f -> p (t f)")
                    v.tensor_scalar(n1, ang, 1 / (2 * math.pi), turn_, ALU.mult, ALU.add)
                    dve.drain()
                    v.tensor_scalar(n1, n1, MAGIC, None, ALU.add)
                    dve.drain()
                    v.tensor_scalar(n1, n1, MAGIC, None, ALU.subtract)
                    dve.drain()
                    v.scalar_tensor_tensor(out=d, in0=n1, scalar=-6.28125, in1=ang, op0=ALU.mult, op1=ALU.add)
                    dve.drain()
                    v.scalar_tensor_tensor(out=d, in0=n1, scalar=-(2 * math.pi - 6.28125), in1=d, op0=ALU.mult, op1=ALU.add)
                    dve.drain()
                    v.tensor_scalar(d, d, shift, 3.1415925, ALU.add, ALU.min)
                    dve.drain()
                    v.tensor_scalar(d, d, -3.1415925, None, ALU.max)
                pairs_ = LAMB.rearrange("p l (i j) d -> p l i j d", j=2)
                prod = S0f[:, 0:DEPTH * 2 * HD].rearrange("p (l i d) -> p l i d", l=DEPTH, i=2)
                for l in range(DEPTH):
                    v.tensor_tensor(prod[:, l], pairs_[:, l, :, 0], pairs_[:, l, :, 1], ALU.mult)
                dve.drain()
                for l in range(DEPTH):
                    v.tensor_reduce(LAME[:, l], prod[:, l], AX, ALU.add)
                dve.drain().then_inc(dve_to_act, 1)
                dve.wait_ge(act_to_dve, c.add("act_to_dve"))
                for l in range(DEPTH):
                    v.tensor_tensor(LAM[:, l, 0:1], LAME[:, l, 1:2], LAME[:, l, 0:1], ALU.subtract)
                dve.drain()
                for l in range(DEPTH):
                    v.tensor_scalar(LAM[:, l, 1:2], LAM[:, l, 0:1], -(0.8 - 0.6 * math.exp(-0.3 * l)), None, ALU.add)

            def norm_scale(st, n):
                if st.get("norm") and n == 0:
                    dve.wait_ge(squares, c.add("squares"))
                    v.tensor_copy(STAT[:, 0:T], SQ[:])
                    rsqrt(T, D)
                    v.tensor_copy(RX[:], RSTD[:, 0:T])
                    dve.drain().then_inc(scale_ready, 1)

            def turn(st):
                high, low = buf[st["dst"]]
                for b in range(st["chunks"] // 2):
                    dve.wait_ge(x_high, c.add("x_high"))
                    if st["gain"] is None:
                        flat = lambda x: x[:, 2 * b:2 * b + 2].rearrange("p k s -> p (k s)")
                        v.tensor_tensor(flat(low), PS[:, 4 + b], flat(high).bitcast(F32),
                                        ALU.subtract).then_inc(x_low, 1)
                    else:
                        for k in (2 * b, 2 * b + 1):
                            i = v.scalar_tensor_tensor(out=low[:, k], in0=PS[:, 4 + b, (k % 2) * S:(k % 2 + 1) * S],
                                                       scalar=gain_col(st["gain"], k), in1=high[:, k].bitcast(F32),
                                                       op0=ALU.mult, op1=ALU.subtract)
                        i.then_inc(x_low, 1)

            def product(st):
                use = st["use"]
                col = st.get("first", 0)
                gates = buf[st.get("gate", "S0")]
                for n, tile in enumerate(st["tiles"]):
                    h, w = st["h0"] + n, tile["width"]
                    split_to(h + SPLIT)
                    norm_scale(st, n)
                    if n in st.get("beside", {}):
                        beside(st, st["beside"][n])
                    if not tile["last"]:
                        continue
                    g = c.add("block") - 1
                    cs = slice(col, col + w)
                    ps = PS[:, 2 * (g % 2):2 * (g % 2) + 2, 0:w]
                    if use != "gate":
                        dve.wait_ge(tile_used, h + 1)
                    if use == "copy" and st.get("scaled"):
                        v.tensor_scalar(PR[:, 1, cs], ps[:, 1], RX[:, 1:2], None, ALU.mult).then_inc(dve_evac, 1)
                    elif use == "copy":
                        v.tensor_copy(PR[:, 1, cs], ps[:, 1]).then_inc(dve_evac, 1)
                    if use == "merge" and st["first_branch"]:
                        v.tensor_tensor(MERGED[:, :, cs], ps, gates[:, :, cs], ALU.mult).then_inc(dve_evac, 1)
                    elif use in ("merge", "ple"):
                        v.tensor_tensor(gates[:, :, cs], ps, gates[:, :, cs], ALU.mult).then_inc(dve_evac, 1)
                        dve.drain()
                        acc = MERGED if use == "merge" else X
                        v.tensor_tensor(acc[:, :, cs], acc[:, :, cs], gates[:, :, cs], ALU.add)
                    if use == "resid":
                        v.scalar_tensor_tensor(out=X[:, :, cs], in0=X[:, :, cs], scalar=st["alpha"], in1=ps,
                                               op0=ALU.mult, op1=ALU.add).then_inc(dve_evac, 1)
                    col += w
                split_to(st["h0"] + len(st["tiles"]) + SPLIT - 1)

            def beside(st, step):
                what, which = (step + " ").split(" ")[:2]
                if what.startswith("forget"):
                    return forget(st, int(what[6:]))
                l = st["layer"]
                hg = 0 if which == "a" else 2
                QK, ik = PR[:, :, 0:D], PR[:, :, 1792:1856]
                groups = lambda x: x.rearrange("p t (g d) -> p t g d", d=HD)
                if what == "qk_squares":
                    dve.wait_ge(act_to_dve, c.add("act_to_dve"))
                    dve.drain()
                    v.tensor_tensor(S1[:], QK, QK, ALU.mult)
                if what == "qk_sums":
                    dve.drain()
                    v.tensor_reduce(STAT[:].rearrange("p (t g) -> p t g", t=T), groups(S1[:]), AX, ALU.add)
                    rsqrt(T * 16, HD)
                if what == "qk_scale":
                    r = RSTD[:].rearrange("p (t g) -> p t g", t=T).unsqueeze(3).broadcast_to([P, T, 16, HD])
                    v.tensor_tensor(groups(QK), groups(QK), r, ALU.mult)
                if what == "qk_gain":
                    dve.drain()
                    for k in range(2):
                        for t in range(T):
                            x = groups(PR[:, :, k * 512:(k + 1) * 512])[:, t]
                            v.tensor_tensor(x, x, HG[:, l, hg + k].unsqueeze(1).broadcast_to([P, 8, HD]), ALU.mult)
                if what.startswith("out_"):
                    y, gate_cols, g = (Y, PR[:, :, 2048:3072], 4) if which == "ret" else (YH, PR[:, :, 3072:4096], 8)
                    by_group = lambda x: x.rearrange("p t (g d) -> p t g d", g=g)
                    dve.drain()
                    if what == "out_squares":
                        v.tensor_tensor(S1[:], y, y, ALU.mult)
                    if what == "out_sums":
                        v.tensor_reduce(STAT[:, 0:T * g].rearrange("p (t g) -> p t g", t=T), by_group(S1[:]), AX, ALU.add)
                        rsqrt(T * g, D // g)
                    if what == "out_scale":
                        r = RSTD[:, 0:T * g].rearrange("p (t g) -> p t g", t=T).unsqueeze(3).broadcast_to([P, T, g, D // g])
                        v.tensor_tensor(by_group(y), by_group(y), r, ALU.mult)
                        dve.wait_ge(act_to_dve, c.add("act_to_dve"))
                        if which == "ret":
                            return
                        dve.wait_ge(hgn_in, 16 * DEPTH)
                        dve.drain()
                        for t in range(T):
                            yt = by_group(y)[:, t]
                            v.tensor_tensor(yt, yt, HGN[:, l].unsqueeze(1).broadcast_to([P, g, P]), ALU.mult)
                    if what == "out_gate":
                        v.tensor_tensor(y, y, gate_cols, ALU.mult)
                if what in ("qk_rope0", "qk_rope1"):
                    t = int(what[-1])
                    dve.drain()
                    rope(PR[:, t, 0:D], 16, 32, COS[:, t], SIN[:, t], S1[:, t], S2[:, t])
                if what in ("ret_rotary0", "ret_rotary1"):
                    t = int(what[-1])
                    if t == 0:
                        dve.wait_ge(act_to_dve, c.add("act_to_dve"))
                    dve.drain()
                    rope(PR[:, t, 0:D], 8, 64, C("ret_cos")[:, t * 64:(t + 1) * 64],
                         C("ret_sin")[:, t * 64:(t + 1) * 64], S1[:, t], S2[:, t])
                if what == "index_norm":
                    dve.wait_ge(act_to_dve, c.add("act_to_dve"))
                    dve.drain()
                    group_norm(ik, T, 1, HD, S1[:, :, 0:HD])
                    for t in range(T):
                        v.tensor_tensor(ik[:, t], ik[:, t], HG[:, l, 4], ALU.mult)
                if what == "index_rope":
                    dve.drain()
                    for t in range(T):
                        rope(PR[:, t, 1536:1856], 5, 32, COS[:, t], SIN[:, t], S1[:, t, 0:320], S2[:, t, 0:320])
                    dve.drain()
                    for i in range(2):
                        v.tensor_copy(PR[:, :, 3584 + i * HD:3584 + (i + 1) * HD], ik)
                    v.tensor_scalar(PR[:, :, 1856:1860], PR[:, :, 1856:1860], IDX_HEADS ** -0.5, None, ALU.mult)

            def forget(st, k):
                hf = PR[:, :, 1024:2048]
                if k == 0:
                    dve.drain().then_inc(dve_to_act, 1)
                if st["layer"] == 0:
                    if k == 1:
                        dve.wait_ge(act_to_dve, c.add("act_to_dve"))
                        v.tensor_scalar(S0[:], hf, 1e-37, None, ALU.max).then_inc(dve_to_act, 1)
                    if k == 2:
                        dve.drain()
                        v.tensor_scalar(hf, hf, -1.0, 1.0, ALU.mult, ALU.add)
                    return
                if k == 1:
                    dve.wait_ge(lb_in, 16 * DEPTH)
                    v.tensor_tensor(S2[:, 0], S2[:, 0], S2[:, 1], ALU.subtract).then_inc(dve_to_act, 1)
                if k == 3:
                    dve.wait_ge(act_to_dve, c.add("act_to_dve", 2))
                    v.tensor_scalar(S2[:, 0], S2[:, 0], 1.0, None, ALU.add)
                    dve.drain()
                    v.reciprocal(S2[:, 0], S2[:, 0])
                if k == 4:
                    dve.drain()
                    v.tensor_scalar(S2[:, 1], S2[:, 0], -1.0, 1.0, ALU.mult, ALU.add)
                    dve.drain()
                    for t in range(T):
                        v.tensor_tensor(S1[:, t], hf[:, t], S2[:, 1], ALU.mult)
                if k == 5:
                    dve.drain()
                    for t in range(T):
                        v.tensor_tensor(S0[:, t], S1[:, t], S2[:, 0], ALU.add)
                if k == 6:
                    dve.drain()
                    for t in range(T):
                        v.tensor_tensor(hf[:, t], S2[:, 1], S1[:, t], ALU.subtract)
                    v.tensor_scalar(S0[:], S0[:], 1e-37, None, ALU.max).then_inc(dve_to_act, 1)

            def index_pairs():
                for n in range(2):
                    m = c.add("scores")
                    dve.wait_ge(scores_full, m)
                    for h in range(2):
                        i = v.tensor_scalar(S2[:, :, (2 * n + h) * S:(2 * n + h + 1) * S],
                                            PS[:, 1 + 2 * (m % 2) + h, :].rearrange("p (t k) -> p t k", t=T), SCALE, 0.0,
                                            ALU.mult, ALU.max)
                    i.then_inc(scores_read, 1)
                for h in range(IDX_HEADS):
                    dve.drain()
                    for t in range(T):
                        w = PR[:, t, 1856 + h:1857 + h]
                        other = C("chunk_mask")[:, t * S:(t + 1) * S] if h == 0 else Y[:, t, 0:S]
                        v.scalar_tensor_tensor(out=Y[:, t, 0:S], in0=S2[:, t, h * S:(h + 1) * S], scalar=w,
                                               in1=other, op0=ALU.mult, op1=ALU.add)

            def index_select(st):
                for t in range(T):
                    v.tensor_copy(S2[:, t, 0:S], Y[:, t, 0:S])
                for r in range(TOPK // 8):
                    dve.drain()
                    for t in range(T):
                        v.max(TOP[:, t], S2[:, t, 0:S])
                    if r < TOPK // 8 - 1:
                        dve.drain()
                        for t in range(T):
                            v.match_replace(S2[:, t, 0:S], TOP[:, t], S2[:, t, 0:S], -3.0e38)
                dve.drain()
                for t in range(T):
                    v.tensor_scalar(S1[:, t, 0:S], Y[:, t, 0:S], TOP[:, t, 7:8], None, ALU.is_equal)
                    v.tensor_scalar(S1[:, t, S:2 * S], Y[:, t, 0:S], TOP[:, t, 7:8], None, ALU.is_gt)
                dve.drain()
                dve.drain().then_inc(dve_to_pe, 1)
                for t in range(T):
                    v.tensor_reduce(NEED[:, t, 0:1], S1[:, t, S:2 * S], AX, ALU.add)
                dve.drain()
                for t in range(T):
                    v.tensor_scalar(NEED[:, t, 1:2], NEED[:, t, 0:1], -1.0, float(TOPK), ALU.mult, ALU.add)
                dve.wait_ge(pe_to_dve, c.add("pe_to_dve"))
                v.tensor_copy(S1[:, :, 512:768], PS[:, 4:6, 0:S]).then_inc(dve_to_pe, 1)
                dve.wait_ge(pe_to_dve, c.add("pe_to_dve"))
                for t in range(T):
                    v.tensor_scalar(S2[:, t, 0:S], PS[:, 6, t * S:(t + 1) * S], NEED[:, t, 1:2], None, ALU.is_le)
                dve.drain()
                v.tensor_tensor(S2[:, :, 0:S], S2[:, :, 0:S], S1[:, :, 0:S], ALU.mult)
                dve.drain()
                v.tensor_tensor(S2[:, :, 0:S], S2[:, :, 0:S], S1[:, :, S:2 * S], ALU.add)
                dve.drain()
                v.tensor_scalar(IDXM, S2[:, :, 0:S], -1.0, -NEG, ALU.add, ALU.mult)

            def pairs(st):
                use = st["use"]
                if use == "I":
                    return index_pairs()
                N = N_PAIRS[use]
                mask = {"A": C("chunk_mask").rearrange("p (t k) -> p t k", t=T), "C": IDXM,
                        "W": C("chunk_mask").rearrange("p (t k) -> p t k", t=T)}[use]
                masks = [mask[:, 0], C("window_mask") if use == "W" else mask[:, 1]]

                def mid(n):
                    m = c.add("scores")
                    s = c.add("sm")
                    b = s % 2
                    dve.wait_ge(scores_full, m)
                    if s > 2:
                        dve.wait_ge(probs_turned, s - 2)
                    for h in range(2):
                        scores = PS[:, 1 + 2 * (m % 2) + h, :].rearrange("p (t k) -> p t k", t=T)
                        if use == "W":
                            for t in range(T):
                                i = v.scalar_tensor_tensor(out=SM[:, b, 2 * t + h], in0=scores[:, t], scalar=SCALE,
                                                           in1=masks[t], op0=ALU.mult, op1=ALU.add)
                        else:
                            i = v.scalar_tensor_tensor(out=SM[:, b].rearrange("p (t h) k -> p t h k", t=T)[:, :, h],
                                                       in0=scores, scalar=SCALE, in1=mask, op0=ALU.mult, op1=ALU.add)
                    i.then_inc(scores_read, 1)
                    dve.drain()
                    v.tensor_reduce(MX[:, b], SM[:, b], AX, ALU.max)
                    dve.drain()
                    if use == "W":
                        sk = SINK[:, st["layer"], 2 * n:2 * n + 2].unsqueeze(1).broadcast_to([P, T, 2])
                        by_t = lambda x: x[:, b].rearrange("p (t h) -> p t h", t=T)
                        v.tensor_tensor(by_t(MX), by_t(MX), sk, ALU.max)
                        dve.drain()
                        v.tensor_tensor(by_t(SINKD), sk, by_t(MX), ALU.subtract)
                    v.tensor_scalar(NMX[:, b], MX[:, b], -1.0, None, ALU.mult)
                    dve.drain().then_inc(max_ready, 1)

                def take_probs():
                    m = c.add("probs")
                    b = m % 2
                    dve.wait_ge(probs_turned, m)
                    v.tensor_copy(PT[:, 1], PS[:, 6, 0:384]).then_inc(probs_dve, 1)
                    if use == "W":
                        v.tensor_tensor(SUM[:, b], SUM[:, b], EDS[:, b], ALU.add)
                        dve.drain()
                    v.reciprocal(RS[:, b], SUM[:, b])
                    dve.drain()
                    if use == "A":
                        for t in range(T):
                            v.tensor_scalar(RS[:, b, 2 * t + 1:2 * t + 2], RS[:, b, 2 * t + 1:2 * t + 2],
                                            LAM[:, st["layer"], 1:2], None, ALU.mult)
                        dve.drain()

                def finish(n):
                    m = c.add("values")
                    b = m % 2
                    dve.wait_ge(values_full, m)
                    vw = P if use == "A" else HD
                    for t in range(T):
                        for h in range(2):
                            i = 2 * t + h
                            o = PS[:, 7, i * vw:(i + 1) * vw]
                            dst = S1[:, t, (2 * b + h) * P:(2 * b + h + 1) * P] if use == "A" else Y[:, t, n * P + h * HD:n * P + (h + 1) * HD]
                            v.tensor_scalar(dst, o, RS[:, b, i:i + 1], None, ALU.mult)
                    dve.drain().then_inc(values_read, 1)
                    if use == "A":
                        v.tensor_tensor(Y[:, :, n * P:(n + 1) * P], S1[:, :, 2 * b * P:(2 * b + 1) * P],
                                        S1[:, :, (2 * b + 1) * P:(2 * b + 2) * P], ALU.add)

                for n in range(N + 2):
                    if n < N:
                        mid(n)
                    if 1 <= n <= N:
                        take_probs()
                    if n >= 2:
                        finish(n - 2)

            def a_finish(st):
                l = st["layer"]
                group_norm(Y[:, :, 0:512], T, 4, P, S1[:, :, 0:512])
                keep = 1.0 - (0.8 - 0.6 * math.exp(-0.3 * l))
                for t in range(T):
                    y = Y[:, t, 0:512].rearrange("p (g d) -> p g d", g=4)
                    v.scalar_tensor_tensor(out=y, in0=y, scalar=keep, in1=SUBLN[:, l].unsqueeze(1).broadcast_to([P, 4, P]),
                                           op0=ALU.mult, op1=ALU.mult)

            def sticks(st):
                three = lambda x: x.rearrange("p (h k) -> p h k", h=2)
                keep = C("strict").unsqueeze(1).broadcast_to([P, 2, 384])
                soft, logs, arg, wts = (three(x) for x in (S1f[:, 768:1536], S1f[:, 0:768], S0f[:, 768:1536], S0f[:, 0:768]))
                for n in range(4):
                    z = PS[:, 1:3, 0:384]
                    dve.wait_ge(act_to_dve, c.add("act_to_dve"))
                    v.tensor_scalar(soft, z, SCALE, 0.0, ALU.mult, ALU.max)
                    dve.drain()
                    dve.wait_ge(act_to_dve, c.add("act_to_dve"))
                    v.tensor_tensor(soft, soft, three(S2f[:, 0:768]), ALU.add)
                    dve.drain()
                    v.tensor_tensor(logs, soft, keep, ALU.mult).then_inc(dve_to_pe, 1)
                    v.scalar_tensor_tensor(out=arg, in0=z, scalar=SCALE, in1=soft, op0=ALU.mult, op1=ALU.subtract)
                    split_to(st["h0"] + n + SPLIT)
                    dve.drain()
                    dve.wait_ge(pe_to_dve, c.add("pe_to_dve"))
                    v.tensor_tensor(arg, arg, PS[:, 5:7, 0:384], ALU.subtract).then_inc(dve_to_act, 1)
                    dve.wait_ge(act_to_dve, c.add("act_to_dve"))
                    v.tensor_tensor(wts, arg, keep, ALU.mult).then_inc(dve_to_pe, 1)
                    dve.wait_ge(pe_to_dve, c.add("pe_to_dve"))
                    v.tensor_copy(Y[:, :, n * P:(n + 1) * P],
                                  PS[:, 7, 0:S].rearrange("p (t d) -> p t d", t=T)).then_inc(dve_to_pe, 1)
                split_to(st["h0"] + len(st["tiles"]) + SPLIT - 1)

            def retention(st):
                def decay(n):
                    dve.wait_ge(pe_to_dve, c.add("pe_to_dve"))
                    dve.wait_ge(act_to_dve, c.add("act_to_dve"))
                    v.scalar_tensor_tensor(out=PT[:, n % 2], in0=PS[:, 1 + n % 2, 0:384], scalar=P ** -0.5,
                                           in1=S1f[:, n * 384:(n + 1) * 384], op0=ALU.mult, op1=ALU.mult).then_inc(dve_to_pe, 1)

                decay(0)
                for n in range(RET_HEADS):
                    if n + 1 < RET_HEADS:
                        decay(n + 1)
                    dve.wait_ge(pe_to_dve, c.add("pe_to_dve"))
                    v.tensor_copy(Y[:, :, n * S:(n + 1) * S],
                                  PS[:, 6 + n % 2, :].rearrange("p (t d) -> p t d", t=T)).then_inc(dve_to_pe, 1)

            def hgrn_scale(st):
                hq, hk = PR[:, :, 0:D], PR[:, :, D:2 * D]
                dve.wait_ge(act_to_dve, c.add("act_to_dve"))
                v.tensor_tensor(hq, hq, S1[:], ALU.mult).then_inc(dve_to_act, 1)
                dve.wait_ge(act_to_dve, c.add("act_to_dve"))
                v.tensor_tensor(S2[:], S2[:], hk, ALU.mult)
                dve.drain()
                dve.wait_ge(act_to_dve, c.add("act_to_dve"))
                v.tensor_tensor(hk, hk, S1[:], ALU.mult)
                dve.drain()
                v.tensor_scalar(S1[:], S2[:], C("even_odd")[:, 0:1], None, ALU.mult)
                dve.drain()
                v.tensor_scalar(S2[:], S2[:], C("even_odd")[:, 1:2], None, ALU.mult)

            def hgrn_heads(st):
                def take_scores(n):
                    dve.wait_ge(pe_to_dve, c.add("pe_to_dve"))
                    v.tensor_copy(DEC[:, n % 2], PS[:, 1, S:S + 16]).then_inc(dve_to_act, 1)
                    v.tensor_tensor(HA, PS[:, 1, 0:S].rearrange("p (t q) -> p t q", t=T),
                                    C("block_upto").unsqueeze(1).broadcast_to([P, T, P]), ALU.mult).then_inc(dve_to_pe, 1)

                def take_output(n):
                    dve.wait_ge(pe_to_dve, c.add("pe_to_dve"))
                    v.tensor_copy(YH[:, :, n * P:(n + 1) * P],
                                  PS[:, 7, 0:S].rearrange("p (t d) -> p t d", t=T)).then_inc(dve_to_pe, 1)

                take_scores(0)
                for n in range(HG_HEADS):
                    dve.wait_ge(kv_full, c.add("kv"))
                    dve.wait_ge(act_to_dve, c.add("act_to_dve"))
                    for b in range(S // HG_BLOCK - 1):
                        m = c.add("state")
                        if m > 4:
                            dve.wait_ge(state_used, m - 4)
                        t, r = b // 8, b % 8
                        kv = PS[:, 2 + r // 2, (2 * t + r % 2) * P:(2 * t + r % 2 + 1) * P]
                        if b == 0:
                            i = v.tensor_copy(STATE[:, m % 4], kv)
                        else:
                            dve.wait_ge(state_ready, m - 1)
                            i = v.scalar_tensor_tensor(out=STATE[:, m % 4], in0=STATE[:, (m - 1) % 4],
                                                       scalar=DEC[:, n % 2, b:b + 1], in1=kv, op0=ALU.mult, op1=ALU.add)
                        i.then_inc(state_ready, 1)
                        if n and b == 4:
                            take_output(n - 1)
                        if n < HG_HEADS - 1 and b == 12:
                            take_scores(n + 1)
                    dve.wait_ge(state_used, c.of("state"))
                    v.tensor_copy(PR[:, :, 1024 + n * P:1024 + (n + 1) * P],
                                  PS[:, 6, 0:S].rearrange("p (t q) -> p t q", t=T)).then_inc(dve_to_pe, 1)
                take_output(HG_HEADS - 1)

            def swa_prepare(st):
                for g in range(4):
                    for i in range(2):
                        v.tensor_copy(PR[:, :, 1536 + g * P + i * HD:1536 + g * P + (i + 1) * HD],
                                      PR[:, :, 1024 + g * HD:1024 + (g + 1) * HD])

            def layer_norm(st):
                for t in range(T):
                    for h in range(2):
                        v.bn_stats(BST[:, t, h], X[:, t, h * 512:(h + 1) * 512])
                dve.drain()
                for t in range(T):
                    v.bn_aggr(MV[:, t], BST[:, t])
                dve.drain()
                v.tensor_scalar(STAT[:, 0:T], MV[:, :, 1], LN_EPS - RMS_EPS, None, ALU.add)
                rsqrt(T, 1)
                for t in range(T):
                    v.tensor_scalar(X[:, t], X[:, t], MV[:, t, 0:1], RSTD[:, t:t + 1], ALU.subtract, ALU.mult)
                dve.wait_ge(rows_in, 32 * (st["n"] + 1))
                dve.drain()
                for t in range(T):
                    v.tensor_tensor(X[:, t], X[:, t], S2[:, 0], ALU.mult)
                dve.drain()
                for t in range(T):
                    v.tensor_tensor(X[:, t], X[:, t], S2[:, 1], ALU.add)

            def mlp(st):
                two = st["use"] == "swiglu"
                for n, tile in enumerate(st["tiles"]):
                    h, j, w = st["h0"] + n, tile["block"], tile["width"]
                    bank = 2 if two else 2 * (j % 2)
                    turned_block = block_to_turn(st["tiles"], n)
                    if turned_block:
                        k, tb = turned_block["rows"], turned_block["block"]
                        from_bank = 2 if two else 2 * (tb % 2)
                        flat = lambda x: x[:, tb % 2, 0:k].rearrange("p k s -> p (k s)")
                        dve.wait_ge(hid_high, c.add("hid"))
                        v.tensor_tensor(flat(HIDT[1]), PS[:, from_bank:from_bank + 2].rearrange("p b c -> p (b c)")[:, 0:k * S],
                                        flat(HIDT[0]).bitcast(F32), ALU.subtract).then_inc(hid_low, 1)
                    split_to(h + SPLIT)
                    norm_scale(st, n)
                    if tile["role"] == "up" and tile["last"]:
                        dve.wait_ge(silu_ready, c.add("silu"))
                        other = SG[:, j % 2, :, 0:w]
                        if two:
                            dve.wait_ge(tile_used, h + 1)
                            other = PS[:, bank:bank + 2, 0:w]
                        v.tensor_tensor(HID[:, j % 2, :, 0:w], SG[:, j % 2, :, 0:w], other, ALU.mult).then_inc(hidden_ready, 1)
                split_to(st["h0"] + len(st["tiles"]) + SPLIT - 1)

            def mlp_add(st):
                v.scalar_tensor_tensor(out=X[:].rearrange("p t d -> p (t d)"), in0=X[:].rearrange("p t d -> p (t d)"),
                                       scalar=st["alpha"], in1=PS[:, 4:8].rearrange("p b c -> p (b c)"),
                                       op0=ALU.mult, op1=ALU.add)

            def moe_add(st):
                v.scalar_tensor_tensor(out=X[:], in0=X[:], scalar=ALPHA, in1=MERGED[:], op0=ALU.mult, op1=ALU.add)

            def route(st):
                L = ROUTE[:, :, 0, 0:8]
                dve.wait_ge(router_in, 16)
                v.tensor_copy(RTR[0][:], ROUTER)
                dve.drain()
                v.tensor_tensor(RTR[1][:], ROUTER, RTR[0][:].bitcast(F32), ALU.subtract).then_inc(dve_to_pe, 1)
                v.memset(MERGED[:], 0.0)
                dve.wait_ge(pe_to_dve, c.add("pe_to_dve"))
                v.tensor_copy(L, PS[:, 0, 0:16].rearrange("p (t e) -> p t e", t=T))
                dve.drain()
                v.tensor_reduce(MV[:, :, 0:1], L, AX, ALU.max)
                for t in range(T):
                    sq = lambda x: x.rearrange("p (a b) -> p a b", a=8)
                    other = ROUTE[:, t, 0, 0:8].unsqueeze(1).broadcast_to([P, 8, 8])
                    own = ROUTE[:, t, 0, 0:8].unsqueeze(2).broadcast_to([P, 8, 8])
                    v.tensor_tensor(sq(RT[:, 0, t]), other, own, ALU.is_gt)
                    v.tensor_tensor(sq(RT[:, 1, t]), other, own, ALU.is_equal)
                dve.drain()
                for t in range(T):
                    v.tensor_tensor(RT[:, 1, t], RT[:, 1, t], C("tie_first"), ALU.mult)
                    v.tensor_scalar(ROUTE[:, t, 2, 0:8], ROUTE[:, t, 0, 0:8], MV[:, t, 0:1], None, ALU.subtract)
                dve.drain().then_inc(dve_to_act, 1)
                v.tensor_tensor(RT[:, 0], RT[:, 0], RT[:, 1], ALU.add)
                dve.drain()
                for t in range(T):
                    v.tensor_reduce(RT[:, 1, t, 0:8], RT[:, 0, t].rearrange("p (a b) -> p a b", a=8), AX, ALU.add)
                dve.drain()
                for h in range(2):
                    v.tensor_scalar(ROUTE[:, :, 1, 8 * h:8 * h + 8], RT[:, 1, :, 0:8], 1.5, None, ALU.is_lt)
                dve.drain().then_inc(dve_to_pe, 1)
                dve.wait_ge(act_to_dve, c.add("act_to_dve"))
                v.tensor_tensor(ROUTE[:, :, 2, 0:8], ROUTE[:, :, 2, 0:8], ROUTE[:, :, 1, 0:8], ALU.mult)
                dve.drain()
                v.tensor_reduce(MV[:, :, 0:1], ROUTE[:, :, 2, 0:8], AX, ALU.add)
                dve.drain()
                v.reciprocal(MV[:, :, 1], MV[:, :, 0])
                dve.drain()
                for t in range(T):
                    v.tensor_scalar(ROUTE[:, t, 2, 0:8], ROUTE[:, t, 2, 0:8], MV[:, t, 1:2], None, ALU.mult)
                dve.drain()
                v.tensor_copy(ROUTE[:, :, 2, 8:16], ROUTE[:, :, 2, 0:8])
                dve.wait_ge(pe_to_dve, c.add("pe_to_dve"))
                place = PS[:, 1, 0:16].rearrange("p (t e) -> p t e", t=T)
                v.tensor_copy(ROUTE[:, :, 3, 0:8], place)
                v.tensor_scalar(ROUTE[:, :, 3, 8:16], place, -float(P), None, ALU.add)
                v.tensor_reduce(MV[:, 0, 0:1], PS[:, 1, 16:24], AX, ALU.max)
                dve.drain()
                v.tensor_scalar(NPASS[:, 0:1], MV[:, 0, 0:1], P + 0.5, 1.0, ALU.is_gt, ALU.add)
                dve.drain().then_inc(passes_ready, 1)

            def experts(st):
                passes = dve.value_load(NPASS[0:1, 0:1], min_val=1, max_val=T)
                dve.drain().then_inc(xh_ready, 2)
                dve.drain().then_inc(spread_read, 1)
                v.memset(YE, 0.0)
                v.memset(CHOICET[:, 1], 0.0)

                def choose(m):
                    at = m % (T * N_EXPERTS)
                    dve.wait_ge(choice_turned, m + 1)
                    for t in range(T):
                        v.tensor_scalar(CHOICE[:, t], C("slots"), ROUTE[:, t, 3, bass.ds(at, 1)],
                                        ROUTE[:, t, 1, bass.ds(at, 1)], ALU.is_equal, ALU.mult)
                    dve.drain()
                    for t in range(T):
                        v.tensor_scalar(CHOICEW[:, t], CHOICE[:, t], ROUTE[:, t, 2, bass.ds(at, 1)], None, ALU.mult)
                    dve.drain().then_inc(choice_ready, 1)

                def gather(m, kk):
                    flat = lambda x: x[:, 4 * kk:4 * kk + 4].rearrange("p k s -> p (k s)")
                    dve.wait_ge(gathered_high, m * 2 + kk + 1)
                    v.tensor_tensor(flat(XG[1]), PS[:, 5, :], flat(XG[0]).bitcast(F32),
                                    ALU.subtract).then_inc(gathered_read, 1)

                def spread(m, s):
                    dve.wait_ge(spread_full, m * 4 + s + 1)
                    acc = MERGED[:, s // 2, s % 2 * NB:(s % 2 + 1) * NB]
                    v.tensor_tensor(acc, acc, PS[:, 5], ALU.add).then_inc(spread_read, 1)

                choose(0)
                for h in range(SPLIT - 1):
                    low_part(STATIC + h, st["tiles"][h])
                gather(0, 0)
                gather(0, 1)
                with dve.Fori(0, passes * (N_EXPERTS // 2)) as i:
                    for half in range(2):
                        m = i * 2 + half
                        for n, tile in enumerate(st["tiles"]):
                            h, j = half * (PAIR // 2) + n, tile["block"]
                            par = (half * J + j) % 2
                            if SPREAD_AT <= n < SPREAD_AT + 4:
                                spread(m, n - SPREAD_AT)
                            if n in (GATHER_AT, GATHER_AT + 1):
                                gather(m + 1, n - GATHER_AT)
                            turned_block = block_to_turn(st["tiles"], n)
                            if turned_block:
                                tb = turned_block["block"]
                                flat = lambda x: x[:, (half * J + tb) % 2].rearrange("p k s -> p (k s)")
                                dve.wait_ge(xh_high, m * J + tb + 1)
                                v.tensor_tensor(flat(HIDT2[1]), PS[:, 4, :], flat(HIDT2[0]).bitcast(F32),
                                                ALU.subtract).then_inc(xh_copied, 1)
                            ahead = h + SPLIT - 1
                            low_part(STATIC + ahead, st["tiles"][ahead % (PAIR // 2)], i * PAIR)
                            if tile["role"] == "up" and tile["last"]:
                                dve.wait_ge(xsilu_ready, m * J + j + 1)
                                dve.wait_ge(tile_used, i * PAIR + STATIC + h + 1)
                                v.tensor_tensor(HID2[:, par], SG2[:, par], PS[:, 2 + par], ALU.mult).then_inc(xh_ready, 1)
                                if j == 1:
                                    choose(m + 1)
                n_experts = passes * N_EXPERTS
                for s in range(4):
                    spread(n_experts, s)

            run = dict(setup=setup, turn=turn, product=product,
                       index_select=index_select, pairs=pairs, a_finish=a_finish,
                       sticks=sticks, retention=retention, 
                       hgrn_scale=hgrn_scale, hgrn_heads=hgrn_heads, 
                       swa_prepare=swa_prepare, layer_norm=layer_norm, mlp=mlp, mlp_add=mlp_add, moe_add=moe_add,
                       route=route, experts=experts)
            for n, st in enumerate(stages):
                if st["kind"] in run:
                    run[st["kind"]](st)
                finish_stage(dve, n)

        @block.gpsimd
        def _(pool):
            nc.gpsimd.memset(MHALF[:], -0.5)
            pool.drain()
            with pool.Fori(0, rsqrts[0]) as i:
                pool.wait_ge(sums_ready, i + 1)
                nc.gpsimd.tensor_tensor(RSTD[:], STAT[:], MHALF[:], ALU.pow).then_inc(rsqrt_ready, 1)


_INS = ["x", "p", "positions", "attn_norm", "w_in", "a_q_norm", "a_k_norm", "a_lambda", "a_subln", "c_q_norm",
        "c_k_norm", "idx_k_norm", "w_br_a", "w_br_b", "w_br_c", "w_out", "mlp_norm", "w_up", "w_down", "ple_norm",
        "w_ple_gate", "w_ple_proj", "ln_in_g_2", "ln_in_b_2", "w_in_2", "ret_w_out_2", "hgrn_lower_bounds_2",
        "hgrn_norm_g_2", "hgrn_w_out_2", "swa_sinks_2", "swa_w_out_2", "w_o_2", "ln_mix_g_2", "ln_mix_b_2",
        "ffn_w_gate_2", "ffn_w_up_2", "ffn_w_down_2", "moe_router_2", "moe_w_gate_2", "moe_w_up_2", "moe_w_down_2",
        "ln_ffn_g_2", "ln_ffn_b_2"]


def kernel(**inputs):
    import concourse.bacc as _bacc
    from concourse.bass_utils import run_bass_kernel_spmd as _run

    nc = _bacc.Bacc("TRN2", target_bir_lowering=False, num_devices=1)
    arrays, aps = {}, {}
    constants, const_at = shape_constants()
    for name in _INS + ["shape_constants"]:
        x = np.ascontiguousarray(constants if name == "shape_constants" else inputs[name])
        arrays[f"in_{name}_dram"] = x
        aps[name] = nc.dram_tensor(f"in_{name}_dram", x.shape, mybir.dt.from_np(x.dtype), kind="ExternalInput").ap()
    out = nc.dram_tensor("out_0_dram", (1, S, D), F32, kind="ExternalOutput").ap()
    build(nc, aps, out, const_at)
    r = _run(nc, [arrays], core_ids=[0])
    return r.results[0]["out_0_dram"]
```
